# Optimizing a Trainium2 kernel written in Bass

```python
import jax, jax.numpy as jnp
from jax import lax
import numpy as np

D_MODEL = 1024
BATCH = 1
SEQ = 256
DEPTH = 2

CTX_LEN = 256
GRID_W = 64
D_MIX = D_MODEL
RET_DIM = D_MIX // 2
DIFF_DIM = D_MIX - RET_DIM
RET_HEADS = 4
RET_HEAD_DIM = RET_DIM // RET_HEADS
DIFF_HEADS = 4
DIFF_V_HEAD = DIFF_DIM // DIFF_HEADS
DIFF_QK_HEAD = DIFF_V_HEAD // 2
D_PROJ = 4 * RET_DIM + 3 * DIFF_DIM
PROJ_SPLITS = [RET_DIM, 2 * RET_DIM, 3 * RET_DIM, 4 * RET_DIM, 4 * RET_DIM + DIFF_DIM, 4 * RET_DIM + 2 * DIFF_DIM]
CHUNK = 128
Q_BLOCK = 128
D_FF = 2816
N_EXPERTS = 8
TOP_K = 2
N_DENSE = (DEPTH + 1) // 2
N_MOE = DEPTH // 2
ROPE_BASE = 10000.0
EPS = 1e-6

kernel_name = "hymba_retnet_diffattn_moe_prefix_block"

def rms_norm(x, g):
    xf = x.astype(jnp.float32)
    y = xf * lax.rsqrt(jnp.mean(xf * xf, axis=-1, keepdims=True) + EPS)
    return (y * g.astype(jnp.float32)).astype(x.dtype)

def modulate(h, shift, scale):
    return h * (1.0 + scale) + shift

def axial_rope(row_pos, col_pos, dim):
    n_freq = dim // 4
    inv_freq = ROPE_BASE ** (-jnp.arange(n_freq, dtype=jnp.float32) / n_freq)
    ang = jnp.concatenate([row_pos[:, None] * inv_freq, col_pos[:, None] * inv_freq], axis=-1)
    ang = jnp.concatenate([ang, ang], axis=-1)
    return jnp.cos(ang), jnp.sin(ang)

def apply_rope(x, cos, sin):
    half = x.shape[-1] // 2
    xf = x.astype(jnp.float32)
    rot = jnp.concatenate([-xf[..., half:], xf[..., :half]], axis=-1)
    return (xf * cos + rot * sin).astype(x.dtype)

def to_heads(a, n_heads):
    b, t, _ = a.shape
    return a.reshape(b, t, n_heads, -1).transpose(0, 2, 1, 3)

def retention_chunkwise(q, k, v, log_gamma, s0):
    b, h, t, dk = q.shape
    dv = v.shape[-1]
    n = t // CHUNK
    qc = q.astype(jnp.float32).reshape(b, h, n, CHUNK, dk)
    kc = k.astype(jnp.float32).reshape(b, h, n, CHUNK, dk)
    vc = v.astype(jnp.float32).reshape(b, h, n, CHUNK, dv)
    pos = jnp.arange(CHUNK, dtype=jnp.float32)
    rel = pos[:, None] - pos[None, :]
    dmat = jnp.where(rel >= 0, jnp.exp(log_gamma[:, None, None] * jnp.maximum(rel, 0.0)), 0.0)
    scores = jnp.einsum('bhncd,bhnmd->bhncm', qc, kc) * dmat[None, :, None]
    o_inner = jnp.einsum('bhncm,bhnme->bhnce', scores, vc)
    lg = log_gamma[:, None]
    zeta = jnp.exp(lg * (CHUNK - 1.0 - pos))
    xi = jnp.exp(lg * (pos + 1.0))
    kv = jnp.einsum('bhnmd,bhnme->nbhde', kc * zeta[None, :, None, :, None], vc)
    chunk_decay = jnp.exp(log_gamma * CHUNK)[None, :, None, None]

    def step(s, kv_n):
        return chunk_decay * s + kv_n, s

    s_final, s_prev = lax.scan(step, s0.astype(jnp.float32), kv)
    o_cross = jnp.einsum('bhncd,nbhde->bhnce', qc * xi[None, :, None, :, None], s_prev)
    return (o_inner + o_cross).reshape(b, h, t, dv), s_final

def retention_final_state(k, v, log_gamma):
    t = k.shape[2]
    w = jnp.exp(log_gamma[:, None] * (t - 1.0 - jnp.arange(t, dtype=jnp.float32)))
    return jnp.einsum('bhtd,bhte->bhde', k.astype(jnp.float32) * w[None, :, :, None], v.astype(jnp.float32))

def retention_out(y, gproj, gn_g):
    b, h, t, dv = y.shape
    mu = jnp.mean(y, axis=-1, keepdims=True)
    yc = y - mu
    yn = yc * lax.rsqrt(jnp.mean(yc * yc, axis=-1, keepdims=True) + EPS)
    yn = yn.transpose(0, 2, 1, 3).reshape(b, t, h * dv) * gn_g.astype(jnp.float32)
    return (jax.nn.silu(gproj.astype(jnp.float32)) * yn).astype(gproj.dtype)

def diff_qk(p, g):
    b, t, _ = p.shape
    a = p.reshape(b, t, DIFF_HEADS, 2, DIFF_QK_HEAD).transpose(0, 2, 3, 1, 4)
    return rms_norm(a, g)

def diff_attend(q, k, v, lam):
    b, h, _, tq, d = q.shape
    dv = v.shape[-1]
    nb = tq // Q_BLOCK
    qb = jnp.moveaxis(q.reshape(b, h, 2, nb, Q_BLOCK, d), 3, 0)

    def block(qi):
        s = jnp.einsum('bhcqd,bhckd->bhcqk', qi, k).astype(jnp.float32)
        p = jax.nn.softmax(s, axis=-1)
        a = p[:, :, 0] - lam * p[:, :, 1]
        return jnp.einsum('bhqk,bhkv->bhqv', a.astype(v.dtype), v)

    o = lax.map(block, qb)
    return jnp.moveaxis(o, 0, 2).reshape(b, h, tq, dv)

def diff_post(o, g, lam_init):
    b, h, t, dv = o.shape
    y = rms_norm(o, g) * (1.0 - lam_init)
    return y.transpose(0, 2, 1, 3).reshape(b, t, h * dv)

def hybrid_mixer(h, hc, w_in, dec_f, dec_b, gn_g, qn_g, kn_g, lq1, lk1, lq2, lk2, subln_g, w_out,
                 lam_init, cos, sin, ctx_out):
    rq, rk, rv, rg, dq, dk, dv = jnp.split(h @ w_in, PROJ_SPLITS, axis=-1)
    if ctx_out:
        rqc, rkc, rvc, rgc, dqc, dkc, dvc = jnp.split(hc @ w_in, PROJ_SPLITS, axis=-1)
    else:
        rkc, rvc = jnp.split(hc @ w_in[:, RET_DIM:3 * RET_DIM], 2, axis=-1)
        dkc, dvc = jnp.split(hc @ w_in[:, 4 * RET_DIM + DIFF_DIM:], 2, axis=-1)

    lg_f = jax.nn.log_sigmoid(dec_f.astype(jnp.float32))
    lg_b = jax.nn.log_sigmoid(dec_b.astype(jnp.float32))
    k_scale = RET_HEAD_DIM ** -0.5
    flip = lambda a: jnp.flip(a, axis=2)
    ql, kl, vl = to_heads(rq, RET_HEADS), to_heads(rk, RET_HEADS) * k_scale, to_heads(rv, RET_HEADS)
    kc_r, vc_r = to_heads(rkc, RET_HEADS) * k_scale, to_heads(rvc, RET_HEADS)
    if ctx_out:
        qc_r = to_heads(rqc, RET_HEADS)
        zeros = jnp.zeros((hc.shape[0], RET_HEADS, RET_HEAD_DIM, RET_HEAD_DIM), jnp.float32)
        oc_f, sc_f = retention_chunkwise(qc_r, kc_r, vc_r, lg_f, zeros)
        oc_b, sc_b = retention_chunkwise(flip(qc_r), flip(kc_r), flip(vc_r), lg_b, zeros)
        ret_c = retention_out(oc_f + flip(oc_b), rgc, gn_g)
    else:
        sc_f = retention_final_state(kc_r, vc_r, lg_f)
        sc_b = retention_final_state(flip(kc_r), flip(vc_r), lg_b)
    o_f, _ = retention_chunkwise(ql, kl, vl, lg_f, sc_f)
    o_b, _ = retention_chunkwise(flip(ql), flip(kl), flip(vl), lg_b, sc_b)
    ret = retention_out(o_f + flip(o_b), rg, gn_g)

    f32 = jnp.float32
    lam = (jnp.exp(jnp.sum(lq1.astype(f32) * lk1.astype(f32)))
           - jnp.exp(jnp.sum(lq2.astype(f32) * lk2.astype(f32))) + lam_init)
    q_scale = DIFF_QK_HEAD ** -0.5
    qd = apply_rope(diff_qk(dq, qn_g), cos, sin) * q_scale
    kd = apply_rope(diff_qk(dk, kn_g), cos, sin)
    vd = to_heads(dv, DIFF_HEADS)
    kdc = diff_qk(dkc, kn_g)
    vdc = to_heads(dvc, DIFF_HEADS)
    k_all = jnp.concatenate([kdc, kd], axis=3)
    v_all = jnp.concatenate([vdc, vd], axis=2)
    diff = diff_post(diff_attend(qd, k_all, v_all, lam), subln_g, lam_init)
    out = jnp.concatenate([ret, diff], axis=-1) @ w_out
    if ctx_out:
        qdc = diff_qk(dqc, qn_g) * q_scale
        diff_c = diff_post(diff_attend(qdc, kdc, vdc, lam), subln_g, lam_init)
        out_c = jnp.concatenate([ret_c, diff_c], axis=-1) @ w_out
        return out, out_c
    return out, None

def swiglu(h, wg, wu, wd):
    return (jax.nn.silu(h @ wg) * (h @ wu)) @ wd

def moe_swiglu(h, rw, rb, wg, wu, wd):
    shp = h.shape
    t = h.reshape(-1, shp[-1])
    logits = (t @ rw).astype(jnp.float32) + rb.astype(jnp.float32)
    top_v, top_i = lax.top_k(logits, TOP_K)
    top_w = jax.nn.softmax(top_v, axis=-1)
    gates = jnp.sum(jax.nn.one_hot(top_i, N_EXPERTS, dtype=jnp.float32) * top_w[..., None], axis=1)
    y = jnp.zeros_like(t)
    for e in range(N_EXPERTS):
        y = y + gates[:, e:e + 1].astype(t.dtype) * swiglu(t, wg[e], wu[e], wd[e])
    return y.reshape(shp)

def setup_inputs(seed: int = 0) -> dict:
    key = jax.random.key(seed)
    ks = jax.random.split(key, 28)
    nrm = jax.random.normal
    f32 = jnp.float32
    base_decay = jnp.log(2.0 ** (5.0 + jnp.arange(RET_HEADS, dtype=f32)) - 1.0)
    return {
        "x": nrm(ks[0], (BATCH, SEQ, D_MODEL), f32),
        "c": nrm(ks[1], (BATCH, D_MODEL), f32),
        "ctx": nrm(ks[2], (BATCH, CTX_LEN, D_MODEL), f32),
        "c_ctx": nrm(ks[3], (D_MODEL,), f32),
        "ada_w": nrm(ks[4], (DEPTH, D_MODEL, 6 * D_MODEL), f32) * D_MODEL ** -0.5,
        "ada_b": nrm(ks[5], (DEPTH, 6 * D_MODEL), f32) * 0.02,
        "norm1_g": 1.0 + 0.02 * nrm(ks[6], (DEPTH, D_MODEL), f32),
        "norm2_g": 1.0 + 0.02 * nrm(ks[7], (DEPTH, D_MODEL), f32),
        "w_in": nrm(ks[8], (DEPTH, D_MODEL, D_PROJ), f32) * D_MODEL ** -0.5,
        "ret_decay_fwd": base_decay + 0.05 * nrm(ks[9], (DEPTH, RET_HEADS), f32),
        "ret_decay_bwd": base_decay + 0.05 * nrm(ks[10], (DEPTH, RET_HEADS), f32),
        "ret_gn_g": 1.0 + 0.02 * nrm(ks[11], (DEPTH, RET_DIM), f32),
        "diff_qn_g": 1.0 + 0.02 * nrm(ks[12], (DEPTH, DIFF_QK_HEAD), f32),
        "diff_kn_g": 1.0 + 0.02 * nrm(ks[13], (DEPTH, DIFF_QK_HEAD), f32),
        "lam_q1": 0.1 * nrm(ks[14], (DEPTH, DIFF_QK_HEAD), f32),
        "lam_k1": 0.1 * nrm(ks[15], (DEPTH, DIFF_QK_HEAD), f32),
        "lam_q2": 0.1 * nrm(ks[16], (DEPTH, DIFF_QK_HEAD), f32),
        "lam_k2": 0.1 * nrm(ks[17], (DEPTH, DIFF_QK_HEAD), f32),
        "diff_subln_g": 1.0 + 0.02 * nrm(ks[18], (DEPTH, DIFF_V_HEAD), f32),
        "w_out": nrm(ks[19], (DEPTH, D_MIX, D_MODEL), f32) * D_MIX ** -0.5,
        "ffn_w_gate": nrm(ks[20], (N_DENSE, D_MODEL, D_FF), f32) * D_MODEL ** -0.5,
        "ffn_w_up": nrm(ks[21], (N_DENSE, D_MODEL, D_FF), f32) * D_MODEL ** -0.5,
        "ffn_w_down": nrm(ks[22], (N_DENSE, D_FF, D_MODEL), f32) * D_FF ** -0.5,
        "router_w": nrm(ks[23], (N_MOE, D_MODEL, N_EXPERTS), f32) * D_MODEL ** -0.5,
        "router_b": nrm(ks[24], (N_MOE, N_EXPERTS), f32) * 0.01,
        "moe_w_gate": nrm(ks[25], (N_MOE, N_EXPERTS, D_MODEL, D_FF), f32) * D_MODEL ** -0.5,
        "moe_w_up": nrm(ks[26], (N_MOE, N_EXPERTS, D_MODEL, D_FF), f32) * D_MODEL ** -0.5,
        "moe_w_down": nrm(ks[27], (N_MOE, N_EXPERTS, D_FF, D_MODEL), f32) * D_FF ** -0.5,
    }

def reference(x, c, ctx, c_ctx, ada_w, ada_b, norm1_g, norm2_g, w_in, ret_decay_fwd, ret_decay_bwd,
              ret_gn_g, diff_qn_g, diff_kn_g, lam_q1, lam_k1, lam_q2, lam_k2, diff_subln_g, w_out,
              ffn_w_gate, ffn_w_up, ffn_w_down, router_w, router_b, moe_w_gate, moe_w_up, moe_w_down):
    b, t, _ = x.shape
    rows = t // GRID_W
    row_pos = jnp.repeat(jnp.arange(rows, dtype=jnp.float32), GRID_W)
    col_pos = jnp.tile(jnp.arange(GRID_W, dtype=jnp.float32), rows)
    cos, sin = axial_rope(row_pos, col_pos, DIFF_QK_HEAD)

    def channel_mixer(h, l):
        if l % 2 == 0:
            i = l // 2
            return swiglu(h, ffn_w_gate[i], ffn_w_up[i], ffn_w_down[i])
        i = l // 2
        return moe_swiglu(h, router_w[i], router_b[i], moe_w_gate[i], moe_w_up[i], moe_w_down[i])

    xc = ctx
    for l in range(DEPTH):
        ctx_out = l < DEPTH - 1
        lam_init = 0.8 - 0.6 * float(np.exp(-0.3 * l))
        mod = jnp.split(jax.nn.silu(c) @ ada_w[l] + ada_b[l], 6, axis=-1)
        mod = [m[:, None, :] for m in mod]
        modc = jnp.split(jax.nn.silu(c_ctx) @ ada_w[l] + ada_b[l], 6, axis=-1)

        h = modulate(rms_norm(x, norm1_g[l]), mod[0], mod[1])
        hc = modulate(rms_norm(xc, norm1_g[l]), modc[0], modc[1])
        mix, mix_c = hybrid_mixer(h, hc, w_in[l], ret_decay_fwd[l], ret_decay_bwd[l], ret_gn_g[l],
                                  diff_qn_g[l], diff_kn_g[l], lam_q1[l], lam_k1[l], lam_q2[l], lam_k2[l],
                                  diff_subln_g[l], w_out[l], lam_init, cos, sin, ctx_out)
        x = x + mod[2] * mix
        h2 = modulate(rms_norm(x, norm2_g[l]), mod[3], mod[4])
        x = x + mod[5] * channel_mixer(h2, l)
        if ctx_out:
            xc = xc + modc[2] * mix_c
            h2c = modulate(rms_norm(xc, norm2_g[l]), modc[3], modc[4])
            xc = xc + modc[5] * channel_mixer(h2c, l)
    return x


_drawn_inputs = setup_inputs


def setup_inputs(seed=0):
    import zlib

    import numpy as np

    out = dict(_drawn_inputs(seed))
    spreads = {}
    factors = {'ret_gn_g': 3.899,
     'diff_qn_g': 8.0,
     'diff_kn_g': 8.0,
     'diff_subln_g': 3.929,
     'router_b': 11.733}
    for name, (base, spread) in spreads.items():
        noise = np.random.default_rng([zlib.crc32(name.encode()), seed]).standard_normal(out[name].shape)
        drawn = base * np.exp(spread * noise) if base else spread * noise
        out[name] = __import__('jax').numpy.asarray(drawn.astype(out[name].dtype))
    for name, factor in factors.items():
        out[name] = (out[name] * factor).astype(out[name].dtype)
    return out
```

```python
from contextlib import ExitStack

import concourse.bass as bass
from concourse import mybir

F32 = mybir.dt.float32
F32R = mybir.dt.float32r
I32 = mybir.dt.int32
U32 = mybir.dt.uint32
ALU = mybir.AluOpType
ACT = mybir.ActivationFunctionType
AX = mybir.AxisListType

P = 128
D = 1024
KD = D // P
SEQ = 256
CTX = 256
TOK = SEQ + CTX
NT = TOK // P
LT = SEQ // P
HEADS = 4
HW = HEADS * P
DQK = 64
NPROJ = 7
D_FF = 2816
FC = D_FF // P
N_EXP = 8
EPS = 1e-6
LAM_INIT = [0.8 - 0.6 * 2.718281828459045 ** (-0.3 * layer) for layer in range(2)]
K_SCALE = float(P) ** -0.5
BIG_DIST = 1e28

RAW = 5
SPL = 3
SLOT = 2048

RQ, RK, RV, RG, DQ, DK, DV = range(NPROJ)
PROJ_ORDER = [RQ, RK, RV, RG, DK, DQ, DV]

ADA_CHUNKS = 6 * D // 512
ADA_SLOTS = 2 * ADA_CHUNKS
PROJ_SLOTS = 2 * NPROJ
OUT_SLOTS = 4
MIX_SLOTS = ADA_SLOTS + PROJ_SLOTS + OUT_SLOTS
FFN_PHASES = [(0, 6), (6, 5)]
FFN_PHASE_SLOTS = [2 * n + 2 * -(-2 * n // 4) for _, n in FFN_PHASES]
FFN_SLOTS = sum(FFN_PHASE_SLOTS)
MOE_GROUPS = -(-FC // 4)
GU_SLOTS = 4 * (MOE_GROUPS - 1) + 2
MOE_SLOTS = GU_SLOTS + 2 * (MOE_GROUPS - 1) + 1
LAYER_BASE = [0, MIX_SLOTS + FFN_SLOTS]
MOE_BASE = LAYER_BASE[1] + MIX_SLOTS
RING = [(i - MOE_BASE) % RAW for i in range(MOE_BASE)]
SHORT_ROUNDS = -MOE_SLOTS % RAW
MOE_RING = list(range(RAW)) * (MOE_SLOTS // RAW + 1 - SHORT_ROUNDS) + list(range(RAW - 1)) * SHORT_ROUNDS
TURN_AFTER = GU_SLOTS + 1
GATHER_AFTER = GU_SLOTS + 3
VEC_ROWS = 6 * KD
ADAB_ROWS = 6 * KD * 2


def build(nc, io, out):
    with ExitStack() as ctx:
        base = nc.sbuf_base
        cursor = [(base + 63) // 64 * 64]

        def at(name, shape, dt, offset):
            return nc.alloc_sbuf_tensor_at(name, shape, dt, offset=offset)

        def words(shape):
            n = 1
            for s in shape[1:]:
                n *= s
            return n

        def place(name, shape, dt=F32):
            t = at(name, shape, dt, cursor[0])
            cursor[0] += (4 * words(shape) + 31) // 32 * 32
            return t

        def sem(name):
            return ctx.enter_context(nc.semaphore(name))

        raw = place("raw", [P, RAW, SLOT])
        whi = [place(f"whi{i}", [P, SLOT], F32R) for i in range(SPL)]
        wlo = [place(f"wlo{i}", [P, SLOT], F32R) for i in range(SPL)]
        x = place("x_res", [P, NT, D])
        hT_hi = place("hT_hi", [P, KD, TOK], F32R)
        hT_lo = place("hT_lo", [P, KD, TOK], F32R)
        ident = place("ident", [P, P])
        cos = place("cos", [P, LT, DQK])
        sin = place("sin", [P, LT, DQK])
        gn = place("gn", [P, HW])
        subln = place("subln", [P, 2, P])
        qn = place("qn", [P, 2, DQK])
        kn = place("kn", [P, 2, DQK])
        dec = place("dec", [P, 2, 2, HEADS])
        vcol = place("vcol", [P, VEC_ROWS])
        abcol = place("abcol", [P, ADAB_ROWS])
        modcol = [place(f"modcol{i}", [P, 6 * KD, 2]) for i in range(2)]
        modtmp = place("modtmp", [P, 4, 2])
        acol = place("acol", [P, KD, 2])
        cs32 = place("cs32", [P, KD, 2])
        cs = place("cs", [P, KD, 4], F32R)
        ss = place("ss", [P, 32])
        msq = place("msq", [P, 32])
        rstd = place("rstd", [P, 32])
        neghalf = place("neghalf", [P, 32])
        lgt = place("lgt", [P, 4, 8])
        lg = place("lg", [P, 2, 8])
        lg256 = place("lg256", [P, 2, 8])
        nlg = place("nlg", [P, 2, 8])
        lamp = place("lamp", [P, 2, 2])
        neglam = place("neglam", [P, 2])
        bst = place("bst", [P, NT, 6])
        bag = place("bag", [P, NT, 2])
        gve = place("gve", [P, NT])
        grs = place("grs", [P, NT])
        negmax = place("negmax", [P, 2, 2])
        psum_p = place("psum_p", [P, 2, 2])
        rcp = place("rcp", [P, 2, 2])
        cosg = place("cosg", [P, LT, DQK])
        sing = place("sing", [P, LT, DQK])

        A0 = (cursor[0] + 63) // 64 * 64
        KB = 1024

        def arena(name, shape, off, dt=F32):
            assert off * KB + 4 * words(shape) <= 74 * KB, name
            return at(name, shape, dt, A0 + int(off * KB))

        assert A0 + 74 * KB <= nc.sbuf_usable_end, (A0, nc.sbuf_usable_end)
        vrows = arena("vrows", [VEC_ROWS, P], 0)
        abrows = arena("abrows", [ADAB_ROWS, P], 0.5)
        lamv = arena("lamv", [P, 2, 4, DQK], 1)
        lamt = arena("lamt", [P, 2, 2, DQK], 3)
        modrow = arena("modrow", [4, 2, 512], 4)
        xn = arena("xn", [P, NT, D], 32)
        junk = arena("junk", [P, D], 48)
        htmp = arena("htmp", [P, 2, TOK], 68)
        rv = arena("rv", [P, NT, HW], 0)
        rg = arena("rg", [P, NT, HW], 8)
        dtok = arena("dtok", [P, NT, HW], 16)
        dv = arena("dv", [P, NT, HW], 24)
        qkT = arena("qkT", [P, 2, HEADS, TOK], 32)
        decL = arena("decL", [P, 384], 48)
        decC = arena("decC", [P, 384], 49.5)
        pT = arena("pT", [P, 2, 1536], 51)
        dist = arena("dist", [P, 3, 384], 63)
        scr = arena("scr", [P, 2, 512], 68)
        gscr = arena("gscr", [P, 2, 384], 68)
        gnb = arena("gnb", [P, NT, P], 72)
        dqT = arena("dqT", [P, HEADS, TOK], 32)
        dkT = arena("dkT", [P, HEADS, TOK], 40)
        prob = arena("prob", [P, 2, 2, 512], 48)
        aT = arena("aT", [P, 2, 512], 56)
        gbc = arena("gbc", [P, 2, D], 60)
        xn2 = arena("xn2", [P, NT, D], 0)
        hid_hi = arena("hid_hi", [P, 12, TOK], 0, F32R)
        hid_lo = arena("hid_lo", [P, 12, TOK], 24, F32R)
        sg = arena("sg", [P, 2, 512], 48)
        hf = arena("hf", [P, 2, 512], 52)
        y = arena("y", [P, LT, D], 8)
        g_hi = arena("g_hi", [P, KD, P], 16, F32R)
        g_lo = arena("g_lo", [P, KD, P], 20, F32R)
        h2T = arena("h2T", [P, KD, SEQ], 24)
        e_hi = arena("e_hi", [P, FC, P], 24, F32R)
        e_lo = arena("e_lo", [P, FC, P], 35, F32R)
        eh = arena("eh", [P, 2, 512], 46)
        esg = arena("esg", [P, 2, 512], 50)
        oute = arena("oute", [P, D], 54)
        pick = arena("pick", [P, LT, P], 58)
        gpick = arena("gpick", [P, LT, P], 59)
        gpickT = arena("gpickT", [P, SEQ], 60)
        triu = arena("triu", [P, P], 61)
        iota = arena("iota", [P, P], 61.5)
        ones = arena("ones", [P, P], 62)
        rw = arena("rw", [P, KD, N_EXP], 62.5)
        rt = arena("rt", [P, 16, LT, N_EXP], 62.75)
        rank17 = arena("rank17", [P, LT, 17], 72.5)
        gate16 = arena("gate16", [P, LT, 16], 63.875)
        gbc1 = arena("gbc1", [P, D], 64)
        top8 = arena("top8", [P, LT, 8], 68)
        topi = arena("topi", [P, LT, 8], 68.0625, U32)
        topf = arena("topf", [P, LT, 8], 68.125)
        steps_i = arena("steps_i", [P, 1], 68.1875, I32)
        rbias = arena("rbias", [P, N_EXP], 68.25)
        gtmp = arena("gtmp", [P, 2, 512], 68.5)

        ps = ctx.enter_context(nc.psum_tensor("ps", [P, 8, 512], F32))

        start_loaded = sem("start_loaded")
        x_loaded = sem("x_loaded")
        gn_loaded = sem("gn_loaded")
        gn_used = sem("gn_used")
        dist_loaded = sem("dist_loaded")
        moe_consts = sem("moe_consts")
        raw_full = [sem(f"raw_full{i}") for i in range(RAW)]
        hi_ready = sem("hi_ready")
        lo_ready = sem("lo_ready")
        w_used = sem("w_used")
        vT_done = sem("vT_done")
        vcol_ready = sem("vcol_ready")
        cs_silu = sem("cs_silu")
        cs_ready = sem("cs_ready")
        ada_row = sem("ada_row")
        ada_T = sem("ada_T")
        ada_col = sem("ada_col")
        ss_ready = sem("ss_ready")
        ms_ready = sem("ms_ready")
        rs_ready = sem("rs_ready")
        xn_ready = sem("xn_ready")
        xT_done = sem("xT_done")
        h_hi = sem("h_hi")
        h_lo = sem("h_lo")
        acol_ready = sem("acol_ready")
        proj_out = sem("proj_out")
        lsig = sem("lsig")
        lsig_v = sem("lsig_v")
        dec_exp = sem("dec_exp")
        dec_ready = sem("dec_ready")
        ret_s = sem("ret_s")
        ret_p = sem("ret_p")
        ret_o = sem("ret_o")
        ret_ve = sem("ret_ve")
        ret_rs = sem("ret_rs")
        ret_done = sem("ret_done")
        qk_ms = sem("qk_ms")
        qk_rs = sem("qk_rs")
        qk_tok = sem("qk_tok")
        qk_T = sem("qk_T")
        qk_out = sem("qk_out")
        att_s = sem("att_s")
        att_max = sem("att_max")
        att_exp = sem("att_exp")
        att_a = sem("att_a")
        att_T = sem("att_T")
        att_aT = sem("att_aT")
        att_o = sem("att_o")
        att_sq = sem("att_sq")
        att_ms = sem("att_ms")
        att_rs = sem("att_rs")
        att_done = sem("att_done")
        gate_T = sem("gate_T")
        gate_ready = sem("gate_ready")
        out_added = sem("out_added")
        silu_done = sem("silu_done")
        hid_ready = sem("hid_ready")
        down_added = sem("down_added")
        h2T_ready = sem("h2T_ready")
        logits_done = sem("logits_done")
        top_diff = sem("top_diff")
        top_exp = sem("top_exp")
        sel_ready = sem("sel_ready")
        rank_done = sem("rank_done")
        steps_ready = sem("steps_ready")
        pick_ready = sem("pick_ready")
        gath_done = sem("gath_done")
        gath_hi = sem("gath_hi")
        gath_lo = sem("gath_lo")
        pickT_ready = sem("pickT_ready")
        e_silu = sem("e_silu")
        e_h = sem("e_h")
        e_T = sem("e_T")
        e_hid_hi = sem("e_hid_hi")
        e_hid = sem("e_hid")
        e_out = sem("e_out")
        e_scat = sem("e_scat")
        e_y = sem("e_y")
        y_ready = sem("y_ready")
        stored = sem("stored")

        NQT = [NT, LT]
        NQ = [TOK, SEQ]
        UNITS = [NQT[0] * HEADS, NQT[1] * HEADS]
        UBASE = [0, UNITS[0]]
        NORM_TILES = [NT, NT, NT, LT]
        NBASE = [0, 4, 8, 12]
        QK_TILES = [[NT, NT], [NT, LT]]
        QK_BASE = [[0, NT], [2 * NT, 3 * NT]]
        QTB = [0, NQT[0]]
        NORM_ADDS = [2 * NT, 2 * NT + 2 * LT]
        HB = [0, 2 * KD, 3 * KD, 5 * KD, KD, 4 * KD]

        def stream():
            ada_w, w_in, w_out = io["ada_w"], io["w_in"], io["w_out"]
            wg, wu, wd = io["ffn_w_gate"], io["ffn_w_up"], io["ffn_w_down"]
            for layer in range(2):
                for n in range(ADA_CHUNKS):
                    for kh in range(2):
                        yield ada_w[layer, kh * 512:(kh + 1) * 512, n * 512:(n + 1) * 512], 4, 512
                for g in PROJ_ORDER:
                    for kh in range(2):
                        yield w_in[layer, kh * 512:(kh + 1) * 512, g * HW:(g + 1) * HW], 4, 512
                for nh in range(2):
                    for kh in range(2):
                        yield w_out[layer, kh * 512:(kh + 1) * 512, nh * 512:(nh + 1) * 512], 4, 512
                if layer == 0:
                    for first, count in FFN_PHASES:
                        for j in range(first, first + count):
                            for w in (wg, wu):
                                yield w[0, :, j * 256:(j + 1) * 256], KD, 256
                        for nh in range(2):
                            for f in range(2 * first, 2 * (first + count), 4):
                                n = min(4, 2 * (first + count) - f)
                                yield wd[0, f * P:(f + n) * P, nh * 512:(nh + 1) * 512], n, 512

        SLOTS = list(stream())
        assert len(SLOTS) == MOE_BASE
        assert MOE_SLOTS % SPL == 0 and len(MOE_RING) == MOE_SLOTS

        def moe_slot(j, e):
            if j < GU_SLOTS:
                g, rest = divmod(j, 4)
                full = g < MOE_GROUPS - 1
                w = io["moe_w_gate"] if rest < (2 if full else 1) else io["moe_w_up"]
                if not full:
                    return w[0, e, :, g * 512:D_FF], KD, D_FF - g * 512
                kh = rest % 2
                return w[0, e, kh * 512:(kh + 1) * 512, g * 512:(g + 1) * 512], 4, 512
            g, nh = divmod(j - GU_SLOTS, 2)
            if g == MOE_GROUPS - 1:
                return io["moe_w_down"][0, e, 4 * g * P:D_FF, :], FC - 4 * g, D
            return io["moe_w_down"][0, e, 4 * g * P:(4 * g + 4) * P, nh * 512:(nh + 1) * 512], 4, 512

        def gate_end(g):
            return 4 * g + 1 if g < MOE_GROUPS - 1 else GU_SLOTS - 2

        def up_end(g):
            return 4 * g + 3 if g < MOE_GROUPS - 1 else GU_SLOTS - 1

        def landed(i):
            return 16 * RING[:i + 1].count(RING[i])

        def moe_landed(it, j):
            r = MOE_RING[j]
            return it * (16 * MOE_RING.count(r)) + 16 * (RING.count(r) + MOE_RING[:j + 1].count(r))

        def split_before(order, i):
            return max(n for n in range(i) if order[n] == order[i]) + 1

        def bcast(ap, n):
            return ap.unsqueeze(0).to_broadcast([P, n])

        block = ctx.enter_context(nc.Block())

        @block.sync
        def _(sp):
            count = [0]

            def small(dst, src, s=start_loaded):
                sp.dma_start(dst, src).then_inc(s, 16)
                if s is start_loaded:
                    count[0] += 16

            def load(src, n, width, dst_slot):
                sp.dma_start(raw[:, dst_slot, 0:n * width].rearrange("p (c w) -> p c w", c=n),
                             src.rearrange("(c p) w -> p c w", p=P)).then_inc(raw_full[dst_slot], 16)

            small(ident[:], io["k_ident"])
            for n, name in enumerate(("c", "c_ctx")):
                v = io[name] if name == "c_ctx" else io[name].rearrange("a d -> (a d)")
                small(vrows[n * KD:(n + 1) * KD, :], v.rearrange("(k p) -> k p", p=P))
            for n, name in enumerate(("norm1_g", "norm2_g")):
                small(vrows[(2 + 2 * n) * KD:(4 + 2 * n) * KD, :],
                      io[name].rearrange("l (k p) -> (l k) p", p=P))
            small(abrows[:], io["ada_b"].rearrange("l (k p) -> (l k) p", p=P))
            for n, name in enumerate(("lam_q1", "lam_k1", "lam_q2", "lam_k2")):
                small(lamv[:, :, n, :], io[name].unsqueeze(0).to_broadcast([P, 2, DQK]))
            small(dec[:, :, 0, :], io["ret_decay_fwd"].unsqueeze(0).to_broadcast([P, 2, HEADS]))
            small(dec[:, :, 1, :], io["ret_decay_bwd"].unsqueeze(0).to_broadcast([P, 2, HEADS]))
            assert count[0] == START_LOADS
            for i in range(RAW):
                load(*SLOTS[i], RING[i])
            small(x[:, 0:LT, :], io["x"].rearrange("b (t p) d -> p (b t) d", p=P), x_loaded)
            small(x[:, LT:NT, :], io["ctx"].rearrange("b (t p) d -> p (b t) d", p=P), x_loaded)
            small(cos[:], io["k_cos"].rearrange("(t p) d -> p t d", p=P), x_loaded)
            small(sin[:], io["k_sin"].rearrange("(t p) d -> p t d", p=P), x_loaded)
            small(subln[:], io["diff_subln_g"].unsqueeze(0).to_broadcast([P, 2, P]), x_loaded)
            small(qn[:], io["diff_qn_g"].unsqueeze(0).to_broadcast([P, 2, DQK]), x_loaded)
            small(kn[:], io["diff_kn_g"].unsqueeze(0).to_broadcast([P, 2, DQK]), x_loaded)
            for i in range(RAW, MOE_BASE):
                for layer in range(2):
                    if i == LAYER_BASE[layer] + ADA_SLOTS + RAW:
                        if layer:
                            sp.wait_ge(gn_used, layer)
                            sp.wait_ge(down_added, 4 * NT)
                        small(gn[:], io["ret_gn_g"][layer:layer + 1, :].to_broadcast([P, HW]), gn_loaded)
                        small(dist[:], io["k_dist"].rearrange("n p c -> p n c"), dist_loaded)
                sp.wait_ge(lo_ready, split_before(RING, i))
                load(*SLOTS[i], RING[i])
            for j in range(MOE_SLOTS):
                if j == RAW:
                    sp.wait_ge(out_added, NORM_ADDS[1])
                    small(triu[:], io["k_triu"], moe_consts)
                    small(iota[:], io["k_iota"], moe_consts)
                    small(rw[:], io["router_w"].rearrange("a (k p) e -> p (a k) e", p=P), moe_consts)
                    small(rbias[:], io["router_b"].to_broadcast([P, N_EXP]), moe_consts)
                sp.wait_ge(lo_ready, split_before(RING + MOE_RING, MOE_BASE + j))
                load(*moe_slot(j, 0), MOE_RING[j])
            sp.wait_ge(steps_ready, 1)
            steps = sp.value_load(steps_i[0:1, 0:1], min_val=N_EXP, max_val=2 * N_EXP)
            with sp.Fori(1, steps) as it:
                expert = sp.snap(sp.to_reg(it & (N_EXP - 1)), min_val=0, max_val=N_EXP - 1)
                for j in range(MOE_SLOTS):
                    before = split_before(MOE_RING * 2, MOE_SLOTS + j) - MOE_SLOTS
                    sp.wait_ge(lo_ready, it * MOE_SLOTS + (MOE_BASE + before))
                    src, n, width = moe_slot(j, expert)
                    load(src, n, width, MOE_RING[j])
            sp.wait_ge(y_ready, 1)
            sp.dma_start(out.rearrange("b (t p) d -> p (b t) d", p=P), x[:, 0:LT, :]).then_inc(stored, 16)
            sp.wait_ge(stored, 16)

        def hi_split(act, i_slot, place, landed_value, used_value, n=SLOT):
            act.wait_ge(raw_full[place], landed_value)
            if used_value is not None:
                act.wait_ge(w_used, used_value)
            nc.scalar.activation(whi[i_slot % SPL][:, 0:n], raw[:, place, 0:n], ACT.Copy).then_inc(hi_ready, 1)

        def lo_split(dve, i_slot, place, hi_value, n=SLOT):
            dve.wait_ge(hi_ready, hi_value)
            nc.vector.tensor_tensor(wlo[i_slot % SPL][:, 0:n], raw[:, place, 0:n],
                                    whi[i_slot % SPL][:, 0:n].bitcast(F32),
                                    ALU.subtract).then_inc(lo_ready, 1)

        @block.scalar
        def _(act):
            nxt = [0]

            def split_to(i):
                while nxt[0] <= min(i, MOE_BASE - 1):
                    k = nxt[0]
                    n = SLOTS[k][1] * SLOTS[k][2]
                    hi_split(act, k, RING[k], landed(k), k - SPL + 1 if k >= SPL else None, n)
                    nxt[0] += 1

            def ada(layer):
                for n in range(ADA_CHUNKS):
                    s = LAYER_BASE[layer] + 2 * n + 1
                    split_to(s + 2)
                    c = layer * ADA_CHUNKS + n
                    act.wait_ge(w_used, s + 1)
                    if c >= 2:
                        act.wait_ge(ada_T, c - 1)
                    nc.scalar.copy(modrow[:, c % 2, :], ps[0:4, c % 2, :]).then_inc(ada_row, 1)

            def norm(which, layer, src_s):
                tiles = NORM_TILES[which]
                for tt in range(tiles):
                    if tt:
                        act.drain()
                    last = nc.scalar.activation(junk[:], x[:, tt, :], ACT.Square,
                                                accum_out=ss[:, tt:tt + 1])
                last.then_inc(ss_ready, 1)
                split_to(src_s)
                if which == 3:
                    return
                act.wait_ge(acol_ready, which + 1)
                shift = (0 if which % 2 == 0 else 3) * KD
                for k in range(KD):
                    act.wait_ge(xT_done, HB[which] + k + 1)
                    for s in range(2 if tiles == NT else 1):
                        last = nc.scalar.activation(
                            hT_hi[:, k, s * SEQ:(s + 1) * SEQ], ps[:, k, s * SEQ:(s + 1) * SEQ],
                            ACT.Identity, bias=modcol[layer][:, shift + k, s:s + 1],
                            scale=acol[:, k, s:s + 1])
                    last.then_inc(h_hi, 1)

            def gate_rows(n, dst, streams):
                act.wait_ge(gate_T, n + 1)
                for s in range(streams):
                    last = nc.scalar.copy(dst(s), ps[:, 2 * s:2 * s + 2, :])
                last.then_inc(gate_ready, 1)

            def decays(layer, h):
                f, b = h, HEADS + h
                n = layer * HEADS + h
                act.wait_ge(dist_loaded, 16 * (layer + 1))
                if n:
                    act.wait_ge(dec_ready, n)
                if h:
                    act.wait_ge(ret_p, n)
                nc.scalar.activation(decL[:], dist[:, 0, :], ACT.Exp, scale=lg[:, layer, f:f + 1])
                nc.scalar.activation(gscr[:, 0, :], dist[:, 1, :], ACT.Exp, scale=lg[:, layer, b:b + 1])
                nc.scalar.activation(decC[:], dist[:, 2, :], ACT.Exp, scale=lg[:, layer, f:f + 1],
                                     bias=lg256[:, layer, f:f + 1])
                nc.scalar.activation(gscr[:, 1, :], dist[:, 2, :], ACT.Exp, scale=nlg[:, layer, b:b + 1],
                                     bias=lg256[:, layer, b:b + 1]).then_inc(dec_exp, 1)

            def proj(layer, c, s):
                g = PROJ_ORDER[c]
                split_to(s + 2)
                act.wait_ge(w_used, s + 1)
                b = (c % 2) * 4
                if g in (RQ, RK):
                    w = NQ[layer] if g == RQ else TOK
                    for h in range(HEADS):
                        last = nc.scalar.copy(qkT[:, 0 if g == RQ else 1, h, 0:w], ps[:, b + h, 0:w])
                else:
                    dst = {RV: rv, RG: rg, DK: dtok, DQ: dtok, DV: dv}[g]
                    tiles = NQT[layer] if g in (RG, DQ) else NT
                    if g == DQ:
                        act.wait_ge(qk_T, 2 * layer + 1)
                    for tt in range(tiles):
                        last = nc.scalar.activation(dst[:, tt, :], ps[:, b + tt, :],
                                                    ACT.Silu if g == RG else ACT.Copy)
                last.then_inc(proj_out, 1)

            def qk_turned(layer, q):
                n = 2 * layer + q
                w = QK_TILES[layer][q] * P
                b = 4 * q
                act.wait_ge(qk_T, n + 1)
                for h in range(HEADS):
                    last = nc.scalar.copy((dqT if q else dkT)[:, h, 0:w], ps[:, b + h, 0:w])
                last.then_inc(qk_out, 1)

            def exps(layer, u):
                n = UBASE[layer] + u
                keys = TOK if u // HEADS < LT else CTX
                act.wait_ge(att_max, n + 1)
                if n >= 2:
                    act.wait_ge(att_T, n - 1)
                for m in range(2):
                    last = nc.scalar.activation(prob[:, u % 2, m, 0:keys], ps[:, 2 * (u % 2) + m, 0:keys],
                                                ACT.Exp, bias=negmax[:, u % 2, m:m + 1],
                                                accum_out=psum_p[:, u % 2, m:m + 1])
                last.then_inc(att_exp, 1)

            def turned(layer, u):
                n = UBASE[layer] + u
                keys = TOK if u // HEADS < LT else CTX
                act.wait_ge(att_T, n + 1)
                if n >= 2:
                    act.wait_ge(att_o, n - 1)
                nc.scalar.copy(aT[:, u % 2, 0:keys], ps[:, 4 + u % 2, 0:keys]).then_inc(att_aT, 1)

            def squares(layer, qt):
                n = QTB[layer] + qt
                act.wait_ge(att_o, UBASE[layer] + HEADS * (qt + 1))
                if n:
                    act.wait_ge(att_ms, n)
                nc.scalar.activation(scr[:, 0, :], ps[:, 6 + qt % 2, :], ACT.Square).then_inc(att_sq, 1)

            act.wait_ge(vcol_ready, 1)
            nc.scalar.activation(cs32[:, :, 0], vcol[:, 0:KD], ACT.Silu)
            nc.scalar.activation(cs32[:, :, 1], vcol[:, KD:2 * KD], ACT.Silu).then_inc(cs_silu, 1)
            act.wait_ge(lsig_v, 1)
            nc.scalar.activation(lgt[:, 1:3, :], lgt[:, 1:3, :], ACT.Exp)
            nc.scalar.activation(lamp[:], lamp[:], ACT.Exp).then_inc(lsig, 1)
            act.wait_ge(lsig_v, 2)
            nc.scalar.activation(lgt[:, 1:3, :], lgt[:, 1:3, :], ACT.Ln).then_inc(lsig, 1)

            for layer in range(2):
                base_s = LAYER_BASE[layer]
                ada(layer)
                proj_s = base_s + ADA_SLOTS
                if layer == 0:
                    act.wait_ge(x_loaded, 16 * 7)
                else:
                    act.wait_ge(down_added, 4 * NT)
                norm(2 * layer, layer, proj_s + 2)
                for c in range(NPROJ):
                    s = proj_s + 2 * c + 1
                    if c == 5:
                        for h in range(HEADS):
                            decays(layer, h)
                        qk_turned(layer, 0)
                    proj(layer, c, s)
                qk_turned(layer, 1)
                out_s = proj_s + PROJ_SLOTS
                split_to(out_s + 2)
                U = UNITS[layer]
                for u in range(U + 2):
                    if u < U:
                        exps(layer, u)
                    if 1 <= u <= U:
                        turned(layer, u - 1)
                    if u >= 2 and (u - 2) % HEADS == HEADS - 1:
                        squares(layer, (u - 2) // HEADS)
                for k in range(KD):
                    act.wait_ge(xT_done, HB[4 + layer] + k + 1)
                    nc.scalar.copy(hT_hi[:, k, 0:NQ[layer]], ps[:, k, 0:NQ[layer]]).then_inc(h_hi, 1)
                gate_rows(2 * layer, lambda s: gbc[:, s, :].rearrange("p (a c) -> p a c", a=2), 2 - layer)
                split_to(out_s + 3)
                split_to(out_s + 5)
                act.wait_ge(out_added, NORM_ADDS[layer])
                norm(2 * layer + 1, layer, out_s + 6)
                if layer == 0:
                    gate_rows(1, lambda s: gbc[:, s, :].rearrange("p (a c) -> p a c", a=2), 2)
                    s = base_s + MIX_SLOTS
                    fchunk = 0
                    for ph, (first, count) in enumerate(FFN_PHASES):
                        for j in range(count):
                            for fi in range(2):
                                split_to(s + 1 + 2)
                                act.wait_ge(w_used, s + 2)
                                if fchunk >= 2:
                                    act.wait_ge(hid_ready, fchunk - 1)
                                nc.scalar.activation(sg[:, fi, :], ps[:, 4 * (j % 2) + fi, :],
                                                     ACT.Silu).then_inc(silu_done, 1)
                                fchunk += 1
                            s += 2
                        s += FFN_PHASE_SLOTS[ph] - 2 * count
                        split_to(s - 1)
            gate_rows(3, lambda s: gbc1[:].rearrange("p (a c) -> p a c", a=2), 1)
            act.wait_ge(top_diff, 1)
            nc.scalar.activation(topf[:, :, 2], topf[:, :, 3], ACT.Exp).then_inc(top_exp, 1)

            act.wait_ge(steps_ready, 1)
            steps = act.value_load(steps_i[0:1, 0:1], min_val=N_EXP, max_val=2 * N_EXP)

            def gathered(n):
                act.wait_ge(gath_done, n)
                for k in range(KD):
                    last = nc.scalar.activation(
                        g_hi[:, k, :], ps[:, k // 4, (k % 4) * P:(k % 4 + 1) * P], ACT.Identity,
                        bias=modcol[1][:, 3 * KD + k, 0:1], scale=acol[:, k, 0:1])
                last.then_inc(gath_hi, 1)

            def down_out(w_value):
                act.wait_ge(w_used, w_value)
                nc.scalar.copy(oute[:].rearrange("p (a c) -> p a c", a=2), ps[:, 5:7, :]).then_inc(e_out, 1)

            gathered(1)
            with act.Fori(0, steps) as it:
                nxt_e = [0]

                def split_e(last):
                    while nxt_e[0] <= last:
                        j = nxt_e[0]
                        hi_split(act, MOE_BASE + j, MOE_RING[j], moe_landed(it, j),
                                 it * MOE_SLOTS + (MOE_BASE + j - SPL + 1))
                        nxt_e[0] += 1

                def hidden(g):
                    n = min(4, FC - 4 * g)
                    act.wait_ge(e_T, it * MOE_GROUPS + (g + 1))
                    nc.scalar.copy(e_hi[:, 4 * g:4 * g + n, :],
                                   ps[:, (4, 7)[g % 2], 0:n * P].rearrange("p (f s) -> p f s", s=P)).then_inc(e_hid_hi, 1)

                split_e(1)
                down_out(it * MOE_SLOTS + MOE_BASE)
                split_e(2)
                for g in range(MOE_GROUPS):
                    w = min(512, D_FF - 512 * g)
                    split_e(gate_end(g) + SPL)
                    act.wait_ge(w_used, it * MOE_SLOTS + (MOE_BASE + gate_end(g) + 1))
                    if g >= 2:
                        act.wait_ge(e_h, it * MOE_GROUPS + (g - 1))
                    nc.scalar.activation(esg[:, g % 2, 0:w], ps[:, g % 2, 0:w], ACT.Silu).then_inc(e_silu, 1)
                    if g:
                        hidden(g - 1)
                split_e(TURN_AFTER + SPL)
                hidden(MOE_GROUPS - 1)
                split_e(GATHER_AFTER + SPL)
                gathered(it + 2)
                nc.scalar.copy(gpickT[:], ps[:, 3, 0:SEQ]).then_inc(pickT_ready, 1)
                split_e(MOE_SLOTS - 1)
            down_out(act.snap(steps * MOE_SLOTS + MOE_BASE, min_val=N_EXP * MOE_SLOTS + MOE_BASE,
                              max_val=2 * N_EXP * MOE_SLOTS + MOE_BASE))

        @block.gpsimd
        def _(pool):
            def inv_sqrt(dst, src, n, wait, value, done):
                pool.wait_ge(wait, value)
                nc.gpsimd.tensor_tensor(dst, src, neghalf[:, 0:n], ALU.pow).then_inc(done, 1)

            nc.gpsimd.memset(neghalf[:], -0.5).then_inc(rs_ready, 1)
            pool.wait_ge(rs_ready, 1)
            for layer in range(2):
                inv_sqrt(rstd[:, 0:NT], msq[:, 0:NT], NT, ms_ready, 2 * layer + 1, rs_ready)
                for h in range(HEADS):
                    n = NQT[layer]
                    inv_sqrt(grs[:, 0:n], gve[:, 0:n], n, ret_ve, layer * HEADS + h + 1, ret_rs)
                for q in range(2):
                    n = 8 * QK_TILES[layer][q]
                    inv_sqrt(rstd[:, 0:n], msq[:, 0:n], n, qk_ms, 2 * layer + q + 1, qk_rs)
                for qt in range(NQT[layer]):
                    inv_sqrt(rstd[:, 0:HEADS], msq[:, 0:HEADS], HEADS, att_ms, QTB[layer] + qt + 1, att_rs)
                n = NORM_TILES[2 * layer + 1]
                inv_sqrt(rstd[:, 0:n], msq[:, 0:n], n, ms_ready, 2 * layer + 2, rs_ready)

        @block.vector
        def _(dve):
            nxt = [0]
            v = nc.vector

            def split_to(i):
                while nxt[0] <= min(i, MOE_BASE - 1):
                    k = nxt[0]
                    lo_split(dve, k, RING[k], k + 1, SLOTS[k][1] * SLOTS[k][2])
                    nxt[0] += 1

            def ada(layer):
                for n in range(ADA_CHUNKS):
                    split_to(LAYER_BASE[layer] + 2 * n + 3)
                    c = layer * ADA_CHUNKS + n
                    dve.wait_ge(ada_T, c + 1)
                    t = ps[:, 2 + c % 2, 0:16].rearrange("p (j r) -> p j r", r=4)
                    b = abcol[:, layer * 6 * KD + 4 * n:layer * 6 * KD + 4 * n + 4]
                    v.tensor_tensor(modtmp[:], t[:, :, 0:2], b.unsqueeze(2).to_broadcast([P, 4, 2]), ALU.add)
                    dve.drain()
                    v.tensor_tensor(modcol[layer][:, 4 * n:4 * n + 4, :], t[:, :, 2:4], modtmp[:],
                                    ALU.add).then_inc(ada_col, 1)
                    dve.drain()

            def norm(which, layer, src_s):
                tiles = NORM_TILES[which]
                buf = xn if which % 2 == 0 else xn2
                scale = (1 if which % 2 == 0 else 4) * KD
                shift = (0 if which % 2 == 0 else 3) * KD
                gains = vcol[:, (2 + which % 2 * 2 + layer) * KD:(3 + which % 2 * 2 + layer) * KD]
                dve.wait_ge(ss_ready, which + 1)
                v.tensor_scalar(msq[:, 0:tiles], ss[:, 0:tiles], 1.0 / D, EPS, ALU.mult,
                                ALU.add).then_inc(ms_ready, 1)
                for s in range(2):
                    last = v.scalar_tensor_tensor(acol[:, :, s], modcol[layer][:, scale:scale + KD, s], 1.0,
                                                  gains, ALU.add, ALU.mult)
                last.then_inc(acol_ready, 1)
                split_to(src_s)
                dve.wait_ge(rs_ready, which + 2)
                for tt in range(tiles):
                    v.tensor_scalar(buf[:, tt, :], x[:, tt, :], rstd[:, tt:tt + 1], None,
                                    ALU.mult).then_inc(xn_ready, 1)
                for k in range(KD):
                    dve.wait_ge(*((xT_done if which == 3 else h_hi), HB[which] + k + 1))
                    for s in range(2 if tiles == NT else 1):
                        cols = slice(s * SEQ, (s + 1) * SEQ)
                        dst = h2T[:, k, :] if which == 3 else htmp[:, k % 2, cols]
                        last = v.tensor_scalar(dst, ps[:, k, cols], acol[:, k, s:s + 1],
                                               modcol[layer][:, shift + k, s:s + 1], ALU.mult, ALU.add)
                    if which == 3:
                        last.then_inc(h2T_ready, 1)
                        continue
                    dve.drain()
                    v.tensor_tensor(hT_lo[:, k, :], htmp[:, k % 2, :], hT_hi[:, k, :].bitcast(F32),
                                    ALU.subtract).then_inc(h_lo, 1)

            def decays(layer, h):
                dve.wait_ge(dec_exp, layer * HEADS + h + 1)
                v.tensor_tensor(decL[:], decL[:], gscr[:, 0, :], ALU.add)
                v.tensor_tensor(decC[:], decC[:], gscr[:, 1, :], ALU.add).then_inc(dec_ready, 1)

            def weigh(layer, h):
                n = layer * HEADS + h
                dve.wait_ge(ret_s, n + 1)
                dve.drain()
                b = 4 * ((h + 1) % 2)
                buf = pT[:, h % 2, :]
                for kt in range(NT):
                    i = kt % LT
                    near = decL[:, P * (1 - i):P * (1 - i) + SEQ]
                    far = decC[:, P * (1 - i):P * (1 - i) + SEQ]
                    bank, off, dst = (b, kt * SEQ, kt * SEQ) if kt < LT else (b + kt - 1, 0, 512 * (kt - 1))
                    last = v.scalar_tensor_tensor(buf[:, dst:dst + SEQ], ps[:, bank, off:off + SEQ], K_SCALE,
                                                  near if kt < LT else far, ALU.mult, ALU.mult)
                    if kt >= LT and layer == 0:
                        last = v.scalar_tensor_tensor(buf[:, dst + SEQ:dst + TOK], ps[:, bank, SEQ:TOK],
                                                      K_SCALE, near, ALU.mult, ALU.mult)
                last.then_inc(ret_p, 1)

            def group_norm(layer, h):
                n = layer * HEADS + h
                b = 4 * ((h + 1) % 2) + 3
                dve.wait_ge(ret_o, n + 1)
                for qt in range(NQT[layer]):
                    v.bn_stats(bst[:, qt, :], ps[:, b, qt * P:(qt + 1) * P])
                dve.drain()
                for qt in range(NQT[layer]):
                    v.bn_aggr(bag[:, qt, :], bst[:, qt, :])
                dve.drain()
                v.tensor_scalar(gve[:, 0:NQT[layer]], bag[:, 0:NQT[layer], 1], EPS, None,
                                ALU.add).then_inc(ret_ve, 1)
                dve.wait_ge(ret_rs, n + 1)
                for qt in range(NQT[layer]):
                    last = v.tensor_scalar(gnb[:, qt, :], ps[:, b, qt * P:(qt + 1) * P],
                                           bag[:, qt, 0:1], grs[:, qt:qt + 1], ALU.subtract, ALU.mult)
                dve.drain()
                cols = slice(h * P, (h + 1) * P)
                v.tensor_tensor(rg[:, 0:NQT[layer], cols], rg[:, 0:NQT[layer], cols],
                                gnb[:, 0:NQT[layer], :], ALU.mult).then_inc(ret_done, 1)

            def qk_norm(layer, q):
                tiles = QK_TILES[layer][q]
                c = PROJ_ORDER.index(DQ if q else DK)
                gain = (qn if q else kn)[:, layer, :]
                half = DQK // 2
                for tt in range(LT):
                    v.tensor_tensor(cosg[:, tt, :], cos[:, tt, :], gain, ALU.mult)
                    v.scalar_tensor_tensor(sing[:, tt, 0:half], sin[:, tt, 0:half], -1.0, gain[:, half:DQK],
                                           ALU.mult, ALU.mult)
                    v.tensor_tensor(sing[:, tt, half:DQK], sin[:, tt, half:DQK], gain[:, 0:half], ALU.mult)
                dve.wait_ge(proj_out, layer * NPROJ + c + 1)
                for tt in range(tiles):
                    v.tensor_tensor(scr[:, tt % 2, :], dtok[:, tt, :], dtok[:, tt, :], ALU.mult)
                    dve.drain()
                    v.tensor_reduce(ss[:, 8 * tt:8 * tt + 8], scr[:, tt % 2, :].rearrange("p (g e) -> p g e", e=DQK),
                                    AX.X, ALU.add)
                dve.drain()
                v.tensor_scalar(msq[:, 0:8 * tiles], ss[:, 0:8 * tiles], 1.0 / DQK, EPS, ALU.mult,
                                ALU.add).then_inc(qk_ms, 1)
                dve.wait_ge(qk_rs, 2 * layer + q + 1)
                if q:
                    v.tensor_scalar(rstd[:, 0:8 * tiles], rstd[:, 0:8 * tiles], float(DQK) ** -0.5, None, ALU.mult)
                    dve.drain()
                for tt in range(tiles):
                    a = dtok[:, tt, :].rearrange("p (g e) -> p g e", e=DQK)
                    r = rstd[:, 8 * tt:8 * tt + 8].unsqueeze(2).to_broadcast([P, 8, DQK])
                    v.tensor_tensor(a, a, r, ALU.mult)
                    dve.drain()
                    if tt < LT:
                        t1 = scr[:, 0, :].rearrange("p (g e) -> p g e", e=DQK)
                        t2 = scr[:, 1, :].rearrange("p (g e) -> p g e", e=DQK)
                        cg = cosg[:, tt, :].unsqueeze(1).to_broadcast([P, 8, DQK])
                        sa = sing[:, tt, 0:half].unsqueeze(1).to_broadcast([P, 8, half])
                        sb = sing[:, tt, half:DQK].unsqueeze(1).to_broadcast([P, 8, half])
                        v.tensor_tensor(t1, a, cg, ALU.mult)
                        v.tensor_tensor(t2[:, :, 0:half], a[:, :, half:DQK], sa, ALU.mult)
                        v.tensor_tensor(t2[:, :, half:DQK], a[:, :, 0:half], sb, ALU.mult)
                        dve.drain()
                        v.tensor_tensor(a, t1, t2, ALU.add).then_inc(qk_tok, 1)
                        dve.drain()
                    else:
                        v.tensor_tensor(a, a, gain.unsqueeze(1).to_broadcast([P, 8, DQK]),
                                        ALU.mult).then_inc(qk_tok, 1)

            def row_max(layer, u):
                n = UBASE[layer] + u
                keys = TOK if u // HEADS < LT else CTX
                dve.wait_ge(att_s, n + 1)
                v.tensor_reduce(negmax[:, u % 2, :], ps[:, 2 * (u % 2):2 * (u % 2) + 2, 0:keys], AX.X, ALU.max,
                                negate=True).then_inc(att_max, 1)

            def combine(layer, u):
                n = UBASE[layer] + u
                keys = TOK if u // HEADS < LT else CTX
                dve.wait_ge(att_exp, n + 1)
                v.reciprocal(rcp[:, u % 2, :], psum_p[:, u % 2, :])
                dve.drain()
                v.tensor_scalar(prob[:, u % 2, 1, 0:keys], prob[:, u % 2, 1, 0:keys], rcp[:, u % 2, 1:2],
                                neglam[:, layer:layer + 1], ALU.mult, ALU.mult)
                dve.drain()
                v.scalar_tensor_tensor(prob[:, u % 2, 0, 0:keys], prob[:, u % 2, 0, 0:keys], rcp[:, u % 2, 0:1],
                                       prob[:, u % 2, 1, 0:keys], ALU.mult, ALU.add).then_inc(att_a, 1)

            def sub_norm(layer, qt):
                n = QTB[layer] + qt
                dve.wait_ge(att_sq, n + 1)
                v.tensor_reduce(ss[:, 0:HEADS], scr[:, 0, :].rearrange("p (h e) -> p h e", e=P), AX.X, ALU.add)
                dve.drain()
                v.tensor_scalar(msq[:, 0:HEADS], ss[:, 0:HEADS], 1.0 / P, EPS, ALU.mult,
                                ALU.add).then_inc(att_ms, 1)
                dve.wait_ge(att_rs, n + 1)
                v.tensor_scalar(rstd[:, 0:HEADS], rstd[:, 0:HEADS], 1.0 - LAM_INIT[layer], None, ALU.mult)
                dve.drain()
                o = dtok[:, qt, :].rearrange("p (h e) -> p h e", e=P)
                v.tensor_tensor(o, ps[:, 6 + qt % 2, :].rearrange("p (h e) -> p h e", e=P),
                                rstd[:, 0:HEADS].unsqueeze(2).to_broadcast([P, HEADS, P]), ALU.mult)
                dve.drain()
                v.tensor_tensor(o, o, subln[:, layer, :].unsqueeze(1).to_broadcast([P, HEADS, P]),
                                ALU.mult).then_inc(att_done, 1)

            def add_gated(bank, tt, nh, gate, done, k):
                cols = slice(nh * 512, (nh + 1) * 512)
                v.tensor_tensor(scr[:, k % 2, :], ps[:, bank, :], gate, ALU.mult)
                dve.drain()
                v.tensor_tensor(x[:, tt, cols], x[:, tt, cols], scr[:, k % 2, :], ALU.add).then_inc(done, 1)

            dve.wait_ge(vT_done, 1)
            v.tensor_copy(vcol[:], ps[:, 0, 0:VEC_ROWS])
            v.tensor_copy(abcol[:], ps[:, 1, 0:ADAB_ROWS]).then_inc(vcol_ready, 1)
            dve.wait_ge(start_loaded, START_LOADS)
            d8 = dec[:].rearrange("p l d h -> p l (d h)")
            v.tensor_scalar(lgt[:, 1:3, :], d8, -1.0, None, ALU.mult)
            v.tensor_scalar(lg[:], d8, 0.0, None, ALU.min)
            v.tensor_tensor(lamt[:, :, 0, :], lamv[:, :, 0, :], lamv[:, :, 1, :], ALU.mult)
            v.tensor_tensor(lamt[:, :, 1, :], lamv[:, :, 2, :], lamv[:, :, 3, :], ALU.mult)
            dve.drain()
            v.tensor_tensor(lgt[:, 1:3, :], lgt[:, 1:3, :], d8, ALU.min)
            v.tensor_reduce(lamp[:], lamt[:], AX.X, ALU.add).then_inc(lsig_v, 1)
            dve.wait_ge(cs_silu, 1)
            v.tensor_copy(cs[:, :, 0:2], cs32[:])
            dve.drain()
            v.tensor_tensor(cs[:, :, 2:4], cs32[:], cs[:, :, 0:2].bitcast(F32), ALU.subtract).then_inc(cs_ready, 1)
            dve.wait_ge(lsig, 1)
            v.tensor_scalar(lgt[:, 1:3, :], lgt[:, 1:3, :], 1.0, None, ALU.add).then_inc(lsig_v, 1)
            v.tensor_tensor(neglam[:], lamp[:, :, 1], lamp[:, :, 0], ALU.subtract)
            dve.drain()
            for layer in range(2):
                v.tensor_scalar(neglam[:, layer:layer + 1], neglam[:, layer:layer + 1], -LAM_INIT[layer], None,
                                ALU.add)
            dve.wait_ge(lsig, 2)
            v.tensor_tensor(lg[:], lg[:], lgt[:, 1:3, :], ALU.subtract)
            dve.drain()
            v.tensor_scalar(lg[:], lg[:], -1e-20, None, ALU.min)
            dve.drain()
            v.tensor_scalar(lg256[:], lg[:], float(CTX), None, ALU.mult)
            v.tensor_scalar(nlg[:], lg[:], -1.0, None, ALU.mult)
            dve.drain()

            for layer in range(2):
                base_s = LAYER_BASE[layer]
                ada(layer)
                proj_s = base_s + ADA_SLOTS
                norm(2 * layer, layer, proj_s + 2)
                for c in range(4):
                    split_to(proj_s + 2 * c + 1 + 2)
                split_to(proj_s + 2 * 3 + 1 + 3)
                dve.wait_ge(gn_loaded, 16 * (layer + 1))
                dve.wait_ge(proj_out, layer * NPROJ + PROJ_ORDER.index(RG) + 1)
                t = NQT[layer]
                v.tensor_tensor(rg[:, 0:t, :], rg[:, 0:t, :], gn[:].unsqueeze(1).to_broadcast([P, t, HW]),
                                ALU.mult).then_inc(gn_used, 1)
                split_to(proj_s + 2 * 4 + 1 + 2)
                for h in range(HEADS):
                    decays(layer, h)
                    weigh(layer, h)
                    if h:
                        group_norm(layer, h - 1)
                group_norm(layer, HEADS - 1)
                qk_norm(layer, 0)
                split_to(proj_s + 2 * 5 + 1 + 2)
                qk_norm(layer, 1)
                out_s = proj_s + PROJ_SLOTS
                split_to(out_s + 2)
                U = UNITS[layer]
                for u in range(U + 3):
                    if u < U:
                        row_max(layer, u)
                    if 1 <= u <= U:
                        combine(layer, u - 1)
                    if u >= 3 and (u - 3) % HEADS == HEADS - 1:
                        sub_norm(layer, (u - 3) // HEADS)
                for k in range(KD):
                    dve.wait_ge(h_hi, HB[4 + layer] + k + 1)
                    v.tensor_tensor(hT_lo[:, k, 0:NQ[layer]], ps[:, k, 0:NQ[layer]],
                                    hT_hi[:, k, 0:NQ[layer]].bitcast(F32), ALU.subtract).then_inc(h_lo, 1)
                dve.wait_ge(gate_ready, 2 * layer + 1)
                for nh in range(2):
                    split_to(out_s + 2 * nh + 1 + 2)
                    dve.wait_ge(w_used, out_s + 2 * nh + 2)
                    for tt in range(NQT[layer]):
                        add_gated(4 * (1 - nh) + tt, tt, nh, gbc[:, 0 if tt < LT else 1, nh * 512:(nh + 1) * 512],
                                  out_added, tt)
                norm(2 * layer + 1, layer, out_s + 6)
                if layer == 0:
                    s = base_s + MIX_SLOTS
                    fchunk = 0
                    for ph, (first, count) in enumerate(FFN_PHASES):
                        for j in range(count):
                            for fi in range(2):
                                split_to(s + 1 + 2)
                                dve.wait_ge(silu_done, fchunk + 1)
                                v.tensor_tensor(hf[:, fi, :], ps[:, 4 * (j % 2) + 2 + fi, :], sg[:, fi, :], ALU.mult)
                                dve.drain()
                                v.tensor_copy(hid_hi[:, 2 * j + fi, :], hf[:, fi, :])
                                dve.drain()
                                v.tensor_tensor(hid_lo[:, 2 * j + fi, :], hf[:, fi, :],
                                                hid_hi[:, 2 * j + fi, :].bitcast(F32),
                                                ALU.subtract).then_inc(hid_ready, 1)
                                fchunk += 1
                            s += 2
                        if ph == 0:
                            dve.wait_ge(gate_ready, 2)
                        half = (FFN_PHASE_SLOTS[ph] - 2 * count) // 2
                        for nh in range(2):
                            s += half
                            split_to(s - 1 + 3)
                            dve.wait_ge(w_used, s)
                            for tt in range(NT):
                                add_gated(4 * nh + tt, tt, nh,
                                          gbc[:, 0 if tt < LT else 1, nh * 512:(nh + 1) * 512], down_added, tt)

            dve.wait_ge(moe_consts, 16 * 4)
            v.memset(ones[:], 1.0)
            dve.wait_ge(logits_done, 1)
            lgts = rt[:, 0, :, :]
            v.tensor_tensor(lgts, ps[:, 4, 0:16].rearrange("p (t e) -> p t e", e=N_EXP),
                            rbias[:].unsqueeze(1).to_broadcast([P, LT, N_EXP]), ALU.add)
            dve.drain()
            for tt in range(LT):
                v.max(top8[:, tt, :], rt[:, 0, tt, :])
            dve.drain()
            for tt in range(LT):
                v.max_index(topi[:, tt, :], top8[:, tt, :], rt[:, 0, tt, :])
            dve.drain()
            v.tensor_copy(topf[:, :, 0:2], topi[:, :, 0:2])
            v.tensor_tensor(topf[:, :, 3], top8[:, :, 1], top8[:, :, 0], ALU.subtract).then_inc(top_diff, 1)
            dve.drain()
            for tt in range(LT):
                for j in range(2):
                    v.tensor_scalar(rt[:, 1 + j, tt, :], iota[:, 0:N_EXP], topf[:, tt, j:j + 1], None, ALU.is_equal)
            dve.drain()
            v.tensor_tensor(rt[:, 3, :, :], rt[:, 1, :, :], rt[:, 2, :, :], ALU.add).then_inc(sel_ready, 1)
            dve.wait_ge(top_exp, 1)
            v.tensor_scalar(topf[:, :, 4], topf[:, :, 2], 1.0, None, ALU.add)
            dve.drain()
            v.reciprocal(topf[:, :, 5], topf[:, :, 4])
            dve.drain()
            v.tensor_tensor(topf[:, :, 6], topf[:, :, 5], topf[:, :, 2], ALU.mult)
            dve.drain()
            for tt in range(LT):
                v.tensor_scalar(rt[:, 4, tt, :], rt[:, 1, tt, :], topf[:, tt, 5:6], None, ALU.mult)
            dve.drain()
            for tt in range(LT):
                for rep in range(2):
                    v.scalar_tensor_tensor(gate16[:, tt, rep * N_EXP:(rep + 1) * N_EXP], rt[:, 2, tt, :],
                                           topf[:, tt, 6:7], rt[:, 4, tt, :], ALU.mult, ALU.add)
            dve.wait_ge(rank_done, 1)
            ranks = ps[:, 5, 0:16].rearrange("p (t e) -> p t e", e=N_EXP)
            v.tensor_tensor(rt[:, 5, :, :], ranks, rt[:, 3, :, :], ALU.mult)
            v.tensor_reduce(topf[:, 0, 7:8], ps[:, 5, 16:16 + N_EXP], AX.X, ALU.max)
            dve.drain()
            for tt in range(LT):
                v.tensor_scalar(rank17[:, tt, 0:N_EXP], rt[:, 5, tt, :], -1.0, None, ALU.add)
                v.tensor_scalar(rank17[:, tt, N_EXP:16], rt[:, 5, tt, :], -1.0 - P, None, ALU.add)
            v.tensor_scalar(topf[:, 1, 7:8], topf[:, 0, 7:8], float(P), float(N_EXP), ALU.is_gt, ALU.mult)
            dve.drain()
            v.tensor_scalar(steps_i[:], topf[:, 1, 7:8], float(N_EXP), None, ALU.add)
            v.memset(rank17[:, :, 16:17], -1.0)
            v.memset(y[:], 0.0)
            v.memset(gpickT[:], 0.0).then_inc(pickT_ready, 1)
            dve.drain().then_inc(steps_ready, 1)
            steps = dve.value_load(steps_i[0:1, 0:1], min_val=N_EXP, max_val=2 * N_EXP)

            def pick_tokens(col):
                for tt in range(LT):
                    last = v.tensor_scalar(pick[:, tt, :], iota[:], rank17[:, tt, col], None, ALU.is_equal)
                last.then_inc(pick_ready, 1)

            def gathered(n):
                dve.wait_ge(gath_hi, n)
                for k in range(KD):
                    v.tensor_scalar(gtmp[:, k // 4, (k % 4) * P:(k % 4 + 1) * P],
                                    ps[:, k // 4, (k % 4) * P:(k % 4 + 1) * P],
                                    acol[:, k, 0:1], modcol[1][:, 3 * KD + k, 0:1], ALU.mult, ALU.add)
                dve.drain()
                v.tensor_tensor(g_lo[:].rearrange("p k s -> p (k s)"), gtmp[:].rearrange("p a c -> p (a c)"),
                                g_hi[:].rearrange("p k s -> p (k s)").bitcast(F32),
                                ALU.subtract).then_inc(gath_lo, 1)

            def add_rows(n):
                dve.wait_ge(e_scat, n)
                for tt in range(LT):
                    rows = y[:, tt, :].rearrange("p (a c) -> p a c", a=2)
                    last = v.tensor_tensor(rows, rows, ps[:, 4 + 2 * tt:6 + 2 * tt, :], ALU.add)
                last.then_inc(e_y, 1)

            pick_tokens(slice(0, 1))
            gathered(1)
            with dve.Fori(0, steps) as it:
                nxt_e = [0]

                def split_e(last):
                    while nxt_e[0] <= last:
                        j = nxt_e[0]
                        lo_split(dve, MOE_BASE + j, MOE_RING[j], it * MOE_SLOTS + (MOE_BASE + j + 1))
                        nxt_e[0] += 1

                def hidden(g):
                    n = min(4, FC - 4 * g)
                    dve.wait_ge(e_hid_hi, it * MOE_GROUPS + (g + 1))
                    v.tensor_tensor(e_lo[:, 4 * g:4 * g + n, :],
                                    ps[:, (4, 7)[g % 2], 0:n * P].rearrange("p (f s) -> p f s", s=P),
                                    e_hi[:, 4 * g:4 * g + n, :].bitcast(F32), ALU.subtract).then_inc(e_hid, 1)

                split_e(3)
                add_rows(it + 1)
                for g in range(MOE_GROUPS):
                    w = min(512, D_FF - 512 * g)
                    split_e(gate_end(g) + SPL)
                    if g:
                        hidden(g - 1)
                    if g == 1:
                        dve.wait_ge(gath_done, it + 1)
                        for tt in range(LT):
                            v.tensor_scalar(gpick[:, tt, :], iota[:], rank17[:, tt, bass.ds(it, 1)],
                                            gate16[:, tt, bass.ds(it, 1)], ALU.is_equal, ALU.mult)
                        pick_tokens(bass.ds(it + 1, 1))
                    split_e(up_end(g) + SPL)
                    dve.wait_ge(e_silu, it * MOE_GROUPS + (g + 1))
                    dve.wait_ge(w_used, it * MOE_SLOTS + (MOE_BASE + up_end(g) + 1))
                    v.tensor_tensor(eh[:, g % 2, 0:w], ps[:, 2 + g % 2, 0:w], esg[:, g % 2, 0:w],
                                    ALU.mult).then_inc(e_h, 1)
                split_e(TURN_AFTER + SPL)
                hidden(MOE_GROUPS - 1)
                split_e(GATHER_AFTER + SPL)
                gathered(it + 2)
                split_e(MOE_SLOTS - 1)
            add_rows(dve.snap(steps + 1, min_val=N_EXP + 1, max_val=2 * N_EXP + 1))
            dve.drain()
            dve.wait_ge(gate_ready, 4)
            for tt in range(LT):
                v.tensor_tensor(y[:, tt, :], y[:, tt, :], gbc1[:], ALU.mult)
            dve.drain()
            for tt in range(LT):
                last = v.tensor_tensor(x[:, tt, :], x[:, tt, :], y[:, tt, :], ALU.add)
            last.then_inc(y_ready, 1)

        @block.tensor
        def _(pe):
            mm = nc.tensor.matmul

            def product(dst, stat, mov, first, last):
                mm(dst, stat[0], mov[0], start=first, stop=False)
                mm(dst, stat[0], mov[1], start=False, stop=False)
                return mm(dst, stat[1], mov[0], start=False, stop=last)

            def parts(i):
                return whi[i % SPL], wlo[i % SPL]

            def slot(i, n, width):
                hi, lo = parts(i)
                pe.wait_ge(lo_ready, i + 1)
                return [t[:, 0:n * width].rearrange("p (c w) -> p c w", c=n) for t in (hi, lo)]

            def ada(layer):
                for n in range(ADA_CHUNKS + 1):
                    c = layer * ADA_CHUNKS + n
                    if n < ADA_CHUNKS:
                        if c >= 2:
                            pe.wait_ge(ada_row, c - 1)
                        for kh in range(2):
                            w = slot(LAYER_BASE[layer] + 2 * n + kh, 4, 512)
                            for k in range(4):
                                for part in range(2):
                                    last = mm(ps[0:4, c % 2, :], cs[:, 4 * kh + k, :], w[part][:, k, :],
                                              start=(kh + k + part == 0), stop=(kh == 1 and k == 3 and part == 1))
                            last.then_inc(w_used, 1)
                    if n >= 1:
                        d = c - 1
                        pe.wait_ge(ada_row, d + 1)
                        if d >= 2:
                            pe.wait_ge(ada_col, d - 1)
                        for j in range(4):
                            last = nc.tensor.transpose(ps[:, 2 + d % 2, 4 * j:4 * j + 4],
                                                       modrow[:, d % 2, j * P:(j + 1) * P], ident[0:4, 0:4])
                        last.then_inc(ada_T, 1)

            def turn(which, tiles, src, ready):
                for k in range(KD):
                    for tt in range(tiles):
                        if k == 0:
                            pe.wait_ge(*ready(tt))
                        last = nc.tensor.transpose(ps[:, k, tt * P:(tt + 1) * P], src(k, tt), ident[:])
                    last.then_inc(xT_done, 1)

            def gate_rows(m, layer, streams):
                for s in range(streams):
                    for k in range(KD):
                        last = mm(ps[:, 2 * s + k // 4, (k % 4) * P:(k % 4 + 1) * P],
                                  modcol[layer][:, m * KD + k, s:s + 1].to_broadcast([P, P]), ident[:],
                                  start=True, stop=True)
                last.then_inc(gate_T, 1)

            def proj(layer, c):
                g = PROJ_ORDER[c]
                b = 4 * (c % 2)
                for kh in range(2):
                    i = LAYER_BASE[layer] + ADA_SLOTS + 2 * c + kh
                    w = slot(i, 4, 512)
                    for t in range(HEADS if g in (RQ, RK) else (NQT[layer] if g in (RG, DQ) else NT)):
                        for k in range(4):
                            kk = 4 * kh + k
                            if g in (RQ, RK):
                                n = NQ[layer] if g == RQ else TOK
                                last = product(ps[:, b + t, 0:n], [p[:, k, t * P:(t + 1) * P] for p in w],
                                               [hT_hi[:, kk, 0:n], hT_lo[:, kk, 0:n]], kk == 0, kk == KD - 1)
                            else:
                                cols = slice(t * P, (t + 1) * P)
                                last = product(ps[:, b + t, :], [hT_hi[:, kk, cols], hT_lo[:, kk, cols]],
                                               [p[:, k, :] for p in w], kk == 0, kk == KD - 1)
                    last.then_inc(w_used, 1)

            def ret_scores(layer, h):
                b = 4 * ((h + 1) % 2)
                n = NQ[layer]
                for kt in range(NT):
                    keys = qkT[:, 1, h, kt * P:(kt + 1) * P]
                    if kt < LT:
                        last = mm(ps[:, b, kt * SEQ:(kt + 1) * SEQ], keys, qkT[:, 0, h, 0:SEQ], start=True, stop=True)
                    else:
                        last = mm(ps[:, b + kt - 1, 0:n], keys, qkT[:, 0, h, 0:n], start=True, stop=True)
                last.then_inc(ret_s, 1)

            def ret_values(layer, h):
                b = 4 * ((h + 1) % 2) + 3
                pe.wait_ge(ret_p, layer * HEADS + h + 1)
                at_kt = [0, SEQ, 512, 1024]
                for qt in range(NQT[layer]):
                    kts = range(NT) if qt < LT else range(LT, NT)
                    for kt in kts:
                        o = at_kt[kt] + qt * P
                        last = mm(ps[:, b, qt * P:(qt + 1) * P], pT[:, h % 2, o:o + P],
                                  rv[:, kt, h * P:(h + 1) * P], start=(kt == kts[0]), stop=(kt == NT - 1))
                last.then_inc(ret_o, 1)

            def qk_turn(layer, q):
                b = 4 * q
                for tt in range(QK_TILES[layer][q]):
                    pe.wait_ge(qk_tok, QK_BASE[layer][q] + tt + 1)
                    for h in range(HEADS):
                        last = nc.tensor.transpose(ps[:, b + h, tt * P:(tt + 1) * P],
                                                   dtok[:, tt, h * P:(h + 1) * P], ident[:])
                last.then_inc(qk_T, 1)

            def scores(layer, u):
                qt, h = divmod(u, HEADS)
                n = UBASE[layer] + u
                first = 0 if qt < LT else SEQ
                if u >= 2:
                    pe.wait_ge(att_exp, n - 1)
                for m in range(2):
                    rows = slice(m * DQK, (m + 1) * DQK)
                    last = mm(ps[:, 2 * (u % 2) + m, 0:TOK - first], dqT[rows, h, qt * P:(qt + 1) * P],
                              dkT[rows, h, first:TOK], start=True, stop=True)
                last.then_inc(att_s, 1)

            def turn_a(layer, u):
                n = UBASE[layer] + u
                keys = TOK if u // HEADS < LT else CTX
                pe.wait_ge(att_a, n + 1)
                if u >= 2:
                    pe.wait_ge(att_aT, n - 1)
                for j in range(keys // P):
                    last = nc.tensor.transpose(ps[:, 4 + u % 2, j * P:(j + 1) * P],
                                               prob[:, u % 2, 0, j * P:(j + 1) * P], ident[:])
                last.then_inc(att_T, 1)

            def values(layer, u):
                qt, h = divmod(u, HEADS)
                n = UBASE[layer] + u
                pe.wait_ge(att_aT, n + 1)
                if h == 0 and qt >= 2:
                    pe.wait_ge(att_done, QTB[layer] + qt - 1)
                kts = range(NT) if qt < LT else range(LT, NT)
                for kt in kts:
                    j = kt - kts[0]
                    last = mm(ps[:, 6 + qt % 2, h * P:(h + 1) * P], aT[:, u % 2, j * P:(j + 1) * P],
                              dv[:, kt, h * P:(h + 1) * P], start=(j == 0), stop=(kt == NT - 1))
                last.then_inc(att_o, 1)

            pe.wait_ge(start_loaded, START_LOADS)
            nc.tensor.transpose(ps[:, 0, 0:VEC_ROWS], vrows[:], ident[0:VEC_ROWS, 0:VEC_ROWS])
            nc.tensor.transpose(ps[:, 1, 0:ADAB_ROWS], abrows[:],
                                ident[0:ADAB_ROWS, 0:ADAB_ROWS]).then_inc(vT_done, 1)
            pe.wait_ge(vcol_ready, 1)
            pe.wait_ge(cs_ready, 1)
            for layer in range(2):
                ada(layer)
                pe.wait_ge(ada_col, (layer + 1) * ADA_CHUNKS)
                turn(2 * layer, NT, lambda k, tt: xn[:, tt, k * P:(k + 1) * P],
                     lambda tt: (xn_ready, NBASE[2 * layer] + tt + 1))
                pe.wait_ge(h_lo, HB[2 * layer] + KD)
                for c in range(5):
                    if c >= 2:
                        pe.wait_ge(proj_out, layer * NPROJ + c - 1)
                    proj(layer, c)
                pe.wait_ge(proj_out, layer * NPROJ + 4)
                for h in range(HEADS + 1):
                    if h < HEADS:
                        if h == 1:
                            pe.wait_ge(proj_out, layer * NPROJ + 5)
                        if h >= 2:
                            pe.wait_ge(ret_done, layer * HEADS + h - 1)
                        ret_scores(layer, h)
                    if h:
                        ret_values(layer, h - 1)
                pe.wait_ge(ret_done, layer * HEADS + HEADS)
                proj(layer, 5)
                qk_turn(layer, 0)
                pe.wait_ge(qk_out, 2 * layer + 1)
                proj(layer, 6)
                pe.wait_ge(proj_out, layer * NPROJ + 6)
                qk_turn(layer, 1)
                pe.wait_ge(proj_out, layer * NPROJ + 7)
                pe.wait_ge(qk_out, 2 * layer + 2)
                U = UNITS[layer]
                for u in range(U + 2):
                    if u < U:
                        scores(layer, u)
                    if 1 <= u <= U:
                        turn_a(layer, u - 1)
                    if u >= 2:
                        values(layer, u - 2)
                pe.wait_ge(att_done, QTB[layer] + NQT[layer])
                turn(4 + layer, NQT[layer],
                     lambda k, tt: rg[:, tt, k * P:(k + 1) * P] if k < HEADS else dtok[:, tt, (k - HEADS) * P:(k - HEADS + 1) * P],
                     lambda tt: (ret_done, layer * HEADS + HEADS))
                pe.wait_ge(h_lo, HB[4 + layer] + KD)
                gate_rows(2, layer, 2 - layer)
                for nh in range(2):
                    if nh:
                        pe.wait_ge(gate_ready, 2 * layer + 1)
                    for kh in range(2):
                        w = slot(LAYER_BASE[layer] + ADA_SLOTS + PROJ_SLOTS + 2 * nh + kh, 4, 512)
                        for tt in range(NQT[layer]):
                            cols = slice(tt * P, (tt + 1) * P)
                            for k in range(4):
                                kk = 4 * kh + k
                                last = product(ps[:, 4 * (1 - nh) + tt, :], [hT_hi[:, kk, cols], hT_lo[:, kk, cols]],
                                               [p[:, k, :] for p in w], kk == 0, kk == KD - 1)
                        last.then_inc(w_used, 1)
                pe.wait_ge(out_added, NORM_ADDS[layer])
                which = 2 * layer + 1
                turn(which, NORM_TILES[which], lambda k, tt: xn2[:, tt, k * P:(k + 1) * P],
                     lambda tt: (xn_ready, NBASE[which] + tt + 1))
                if layer == 0:
                    pe.wait_ge(h_lo, HB[1] + KD)
                    gate_rows(5, 0, 2)
                    s = MIX_SLOTS
                    for ph, (first, count) in enumerate(FFN_PHASES):
                        if ph == 0:
                            pe.wait_ge(gate_ready, 2)
                        else:
                            pe.wait_ge(down_added, 2 * NT * ph)
                        for j in range(count):
                            if j >= 2:
                                pe.wait_ge(hid_ready, 2 * (first + j - 1))
                            for up in range(2):
                                w = slot(s + up, KD, 256)
                                for fi in range(2):
                                    for k in range(KD):
                                        last = product(ps[:, 4 * (j % 2) + 2 * up + fi, :],
                                                       [p[:, k, fi * P:(fi + 1) * P] for p in w],
                                                       [hT_hi[:, k, :], hT_lo[:, k, :]], k == 0, k == KD - 1)
                                last.then_inc(w_used, 1)
                            s += 2
                        pe.wait_ge(hid_ready, 2 * (first + count))
                        half = (FFN_PHASE_SLOTS[ph] - 2 * count) // 2
                        for nh in range(2):
                            for q in range(half):
                                n = min(4, 2 * count - 4 * q)
                                w = slot(s + q, n, 512)
                                for tt in range(NT):
                                    cols = slice(tt * P, (tt + 1) * P)
                                    for k in range(n):
                                        f = 4 * q + k
                                        last = product(ps[:, 4 * nh + tt, :], [hid_hi[:, f, cols], hid_lo[:, f, cols]],
                                                       [p[:, k, :] for p in w], f == 0, f == 2 * count - 1)
                                last.then_inc(w_used, 1)
                            s += half
                    pe.wait_ge(down_added, 4 * NT)

            pe.wait_ge(h2T_ready, KD)
            gate_rows(5, 1, 1)
            pe.wait_ge(moe_consts, 16 * 4)
            for tt in range(LT):
                for k in range(KD):
                    last = mm(ps[:, 4, tt * N_EXP:(tt + 1) * N_EXP], h2T[:, k, tt * P:(tt + 1) * P], rw[:, k, :],
                              start=(k == 0), stop=(k == KD - 1))
            last.then_inc(logits_done, 1)
            pe.wait_ge(sel_ready, 1)
            mm(ps[:, 5, 0:N_EXP], triu[:], rt[:, 3, 0, :], start=True, stop=True)
            mm(ps[:, 5, N_EXP:16], triu[:], rt[:, 3, 1, :], start=True, stop=False)
            mm(ps[:, 5, N_EXP:16], ones[:], rt[:, 3, 0, :], start=False, stop=True)
            mm(ps[:, 5, 16:24], ones[:], rt[:, 3, 0, :], start=True, stop=False)
            mm(ps[:, 5, 16:24], ones[:], rt[:, 3, 1, :], start=False, stop=True).then_inc(rank_done, 1)
            pe.wait_ge(gate_ready, 4)

            pe.wait_ge(steps_ready, 1)
            steps = pe.value_load(steps_i[0:1, 0:1], min_val=N_EXP, max_val=2 * N_EXP)

            def gather():
                for k in range(KD):
                    for tt in range(LT):
                        last = mm(ps[:, k // 4, (k % 4) * P:(k % 4 + 1) * P], xn2[:, tt, k * P:(k + 1) * P],
                                  pick[:, tt, :], start=(tt == 0), stop=(tt == LT - 1))
                last.then_inc(gath_done, 1)

            def scatter(n):
                pe.wait_ge(pickT_ready, n)
                pe.wait_ge(e_out, n)
                for tt in range(LT):
                    for nh in range(2):
                        last = mm(ps[:, 4 + 2 * tt + nh, :], gpickT[:, tt * P:(tt + 1) * P],
                                  oute[:, nh * 512:(nh + 1) * 512], start=True, stop=True)
                last.then_inc(e_scat, 1)

            pe.wait_ge(pick_ready, 1)
            gather()
            with pe.Fori(0, steps) as it:
                def eslot(j, n, width):
                    pe.wait_ge(lo_ready, it * MOE_SLOTS + (MOE_BASE + j + 1))
                    hi, lo = parts(MOE_BASE + j)
                    return [t[:, 0:n * width].rearrange("p (c w) -> p c w", c=n) for t in (hi, lo)]

                def turn_h(g):
                    n = min(4, FC - 4 * g)
                    pe.wait_ge(e_h, it * MOE_GROUPS + (g + 1))
                    if g == 0:
                        pe.wait_ge(e_y, it + 1)
                    if g >= 2:
                        pe.wait_ge(e_hid, it * MOE_GROUPS + (g - 1))
                    for f in range(n):
                        last = nc.tensor.transpose(ps[:, (4, 7)[g % 2], f * P:(f + 1) * P],
                                                   eh[:, g % 2, f * P:(f + 1) * P], ident[:])
                    last.then_inc(e_T, 1)

                pe.wait_ge(gath_lo, it + 1)
                for g in range(MOE_GROUPS):
                    width = min(512, D_FF - 512 * g)
                    kn = 4 if width == 512 else KD
                    if g >= 2:
                        pe.wait_ge(e_h, it * MOE_GROUPS + (g - 1))
                    for up in range(2):
                        for kh in range(KD // kn):
                            w = eslot(4 * g + (KD // kn) * up + kh, kn, width)
                            for k in range(kn):
                                kk = kn * kh + k
                                last = product(ps[:, 2 * up + g % 2, 0:width], [g_hi[:, kk, :], g_lo[:, kk, :]],
                                               [p[:, k, :] for p in w], kk == 0, kk == KD - 1)
                            last.then_inc(w_used, 1)
                        if not up:
                            if g:
                                turn_h(g - 1)
                            else:
                                scatter(it + 1)
                for g in range(MOE_GROUPS):
                    n = min(4, FC - 4 * g)
                    pe.wait_ge(e_hid, it * MOE_GROUPS + (g + 1))
                    for nh in range(2):
                        if g < MOE_GROUPS - 1:
                            w = eslot(GU_SLOTS + 2 * g + nh, n, 512)
                        elif nh == 0:
                            w = eslot(GU_SLOTS + 2 * g, n, D)
                        cols = slice(nh * 512, (nh + 1) * 512) if g == MOE_GROUPS - 1 else slice(0, 512)
                        for k in range(n):
                            f = 4 * g + k
                            last = product(ps[:, 5 + nh, :], [e_hi[:, f, :], e_lo[:, f, :]],
                                           [p[:, k, cols] for p in w], f == 0, f == FC - 1)
                        if g < MOE_GROUPS - 1 or nh == 1:
                            last.then_inc(w_used, 1)
                    if g == 0:
                        turn_h(MOE_GROUPS - 1)
                    if g == 1:
                        pe.wait_ge(pick_ready, it + 2)
                        for tt in range(LT):
                            nc.tensor.transpose(ps[:, 3, tt * P:(tt + 1) * P], gpick[:, tt, :], ident[:])
                        gather()
            scatter(pe.snap(steps + 1, min_val=N_EXP + 1, max_val=2 * N_EXP + 1))


_INS = ["x", "c", "ctx", "c_ctx", "ada_w", "ada_b", "norm1_g", "norm2_g", "w_in", "ret_decay_fwd", "ret_decay_bwd",
        "ret_gn_g", "diff_qn_g", "diff_kn_g", "lam_q1", "lam_k1", "lam_q2", "lam_k2", "diff_subln_g", "w_out",
        "ffn_w_gate", "ffn_w_up", "ffn_w_down", "router_w", "router_b", "moe_w_gate", "moe_w_up", "moe_w_down"]
START_LOADS = 16 * 12


def constants():
    import numpy as np

    f32 = np.float32
    grid_w = 64
    n_freq = DQK // 4
    inv = f32(10000.0) ** (-np.arange(n_freq, dtype=f32) / f32(n_freq))
    pos = np.arange(SEQ)
    ang = np.concatenate([(pos // grid_w).astype(f32)[:, None] * inv, (pos % grid_w).astype(f32)[:, None] * inv], -1)
    ang = np.concatenate([ang, ang], -1).astype(f32)
    delta = (np.arange(384)[None, :] - P - np.arange(P)[:, None]).astype(f32)
    dist = np.stack([np.where(delta >= 0, delta, BIG_DIST), np.where(delta <= 0, -delta, BIG_DIST), delta]).astype(f32)
    return {
        "k_ident": np.eye(P, dtype=f32),
        "k_triu": np.triu(np.ones((P, P), f32)),
        "k_iota": np.tile(np.arange(P, dtype=f32), (P, 1)),
        "k_cos": np.cos(ang).astype(f32),
        "k_sin": np.sin(ang).astype(f32),
        "k_dist": dist,
    }


def kernel(**inputs):
    import numpy as np
    import concourse.bacc as bacc
    from concourse.bass_utils import run_bass_kernel_spmd

    nc = bacc.Bacc("TRN2", target_bir_lowering=False, num_devices=1, dynamic_dma_scratch_size=16)
    arrays, io = {}, {}
    for name, a in [(n, inputs[n]) for n in _INS] + list(constants().items()):
        a = np.ascontiguousarray(a)
        arrays[f"in_{name}"] = a
        io[name] = nc.dram_tensor(f"in_{name}", a.shape, mybir.dt.from_np(a.dtype), kind="ExternalInput").ap()
    out = nc.dram_tensor("out_latent", (1, SEQ, D), F32, kind="ExternalOutput").ap()
    build(nc, io, out)
    r = run_bass_kernel_spmd(nc, [arrays], core_ids=[0])
    return r.results[0]["out_latent"]
```

```python
from contextlib import ExitStack

import concourse.bass as bass
from concourse import mybir

F32 = mybir.dt.float32
F32R = mybir.dt.float32r
I32 = mybir.dt.int32
U32 = mybir.dt.uint32
ALU = mybir.AluOpType
ACT = mybir.ActivationFunctionType
AX = mybir.AxisListType

P = 128
D = 1024
KD = D // P
SEQ = 256
CTX = 256
TOK = SEQ + CTX
NT = TOK // P
LT = SEQ // P
HEADS = 4
HW = HEADS * P
DQK = 64
NPROJ = 7
D_FF = 2816
FC = D_FF // P
N_EXP = 8
EPS = 1e-6
LAM_INIT = [0.8 - 0.6 * 2.718281828459045 ** (-0.3 * layer) for layer in range(2)]
K_SCALE = float(P) ** -0.5
BIG_DIST = 1e28

RAW = 5
SPL = 3
SLOT = 2048

RQ, RK, RV, RG, DQ, DK, DV = range(NPROJ)
PROJ_ORDER = [RQ, RK, RV, RG, DK, DQ, DV]

ADA_CHUNKS = 6 * D // 512
ADA_EARLY = 2 * D // 512
RET_FILL = [ADA_EARLY, ADA_EARLY + HEADS + 8]
DIFF_FILL = [f + HEADS for f in RET_FILL]
EARLY_PROJ = 5
OUT_SLOTS = 4
FFN_PHASES = [(0, 6), (6, 5)]
FFN_PHASE_SLOTS = [2 * n + 2 * -(-2 * n // 4) for _, n in FFN_PHASES]
FFN_SLOTS = sum(FFN_PHASE_SLOTS)
MOE_GROUPS = -(-FC // 4)
GU_SLOTS = 4 * (MOE_GROUPS - 1) + 2
MOE_SLOTS = GU_SLOTS + 2 * (MOE_GROUPS - 1) + 1
MOE_BASE = 2 * 2 * ADA_CHUNKS + 2 * (2 * NPROJ + OUT_SLOTS) + FFN_SLOTS
RING = [(i - MOE_BASE) % RAW for i in range(MOE_BASE)]
SHORT_ROUNDS = -MOE_SLOTS % RAW
MOE_RING = list(range(RAW)) * (MOE_SLOTS // RAW + 1 - SHORT_ROUNDS) + list(range(RAW - 1)) * SHORT_ROUNDS
TURN_AFTER = GU_SLOTS + 1
GATHER_AFTER = GU_SLOTS + 3
VEC_ROWS = 6 * KD
ADAB_ROWS = 6 * KD * 2


def build(nc, io, out):
    with ExitStack() as ctx:
        base = nc.sbuf_base
        cursor = [(base + 63) // 64 * 64]

        def at(name, shape, dt, offset):
            return nc.alloc_sbuf_tensor_at(name, shape, dt, offset=offset)

        def words(shape):
            n = 1
            for s in shape[1:]:
                n *= s
            return n

        def place(name, shape, dt=F32):
            t = at(name, shape, dt, cursor[0])
            cursor[0] += (4 * words(shape) + 31) // 32 * 32
            return t

        def sem(name):
            return ctx.enter_context(nc.semaphore(name))

        raw = place("raw", [P, RAW, SLOT])
        whi = [place(f"whi{i}", [P, SLOT], F32R) for i in range(SPL)]
        wlo = [place(f"wlo{i}", [P, SLOT], F32R) for i in range(SPL)]
        x = place("x_res", [P, NT, D])
        hT_hi = place("hT_hi", [P, KD, TOK], F32R)
        hT_lo = place("hT_lo", [P, KD, TOK], F32R)
        ident = place("ident", [P, P])
        cos = place("cos", [P, LT, DQK])
        sin = place("sin", [P, LT, DQK])
        gn = place("gn", [P, HW])
        subln = place("subln", [P, 2, P])
        qn = place("qn", [P, 2, DQK])
        kn = place("kn", [P, 2, DQK])
        dec = place("dec", [P, 2, 2, HEADS])
        vcol = place("vcol", [P, VEC_ROWS])
        abcol = place("abcol", [P, ADAB_ROWS])
        modcol = [place(f"modcol{i}", [P, 6 * KD, 2]) for i in range(2)]
        modtmp = place("modtmp", [P, 4, 2])
        acol = place("acol", [P, KD, 2])
        cs32 = place("cs32", [P, KD, 2])
        cs = place("cs", [P, KD, 4], F32R)
        ss = place("ss", [P, 32])
        msq = place("msq", [P, 32])
        rstd = place("rstd", [P, 32])
        neghalf = place("neghalf", [P, 32])
        lgt = place("lgt", [P, 4, 8])
        lg = place("lg", [P, 2, 8])
        lg256 = place("lg256", [P, 2, 8])
        nlg = place("nlg", [P, 2, 8])
        lamp = place("lamp", [P, 2, 2])
        neglam = place("neglam", [P, 2])
        bst = place("bst", [P, NT, 6])
        bag = place("bag", [P, NT, 2])
        gve = place("gve", [P, NT])
        grs = place("grs", [P, NT])
        negmax = place("negmax", [P, 2, 2])
        psum_p = place("psum_p", [P, 2, 2])
        rcp = place("rcp", [P, 2, 2])
        cosg = place("cosg", [P, LT, DQK])
        sing = place("sing", [P, LT, DQK])

        A0 = (cursor[0] + 63) // 64 * 64
        KB = 1024

        def arena(name, shape, off, dt=F32):
            assert off * KB + 4 * words(shape) <= 74 * KB, name
            return at(name, shape, dt, A0 + int(off * KB))

        assert A0 + 74 * KB <= nc.sbuf_usable_end, (A0, nc.sbuf_usable_end)
        vrows = arena("vrows", [VEC_ROWS, P], 0)
        abrows = arena("abrows", [ADAB_ROWS, P], 0.5)
        lamv = arena("lamv", [P, 2, 4, DQK], 1)
        lamt = arena("lamt", [P, 2, 2, DQK], 3)
        modrow_start = [arena(f"modrow_start{i}", [4, 512], 4 + 2 * i) for i in range(2)]
        xn = arena("xn", [P, NT, D], 32)
        junk = arena("junk", [P, D], 48)
        htmp = arena("htmp", [P, 2, 4, SEQ], 52)
        rv = arena("rv", [P, NT, HW], 0)
        rg = arena("rg", [P, NT, HW], 8)
        dtok = arena("dtok", [P, NT, HW], 16)
        dv = arena("dv", [P, NT, HW], 24)
        qkT = arena("qkT", [P, 2, HEADS, TOK], 32)
        modrow_ret = arena("modrow_ret", [4, 512], 24)
        decL = [arena(f"decL{i}", [P, 384], (48, 26)[i]) for i in range(2)]
        decC = [arena(f"decC{i}", [P, 384], (49.5, 27.5)[i]) for i in range(2)]
        pT = arena("pT", [P, 2, 1536], 51)
        dist = arena("dist", [P, 3, 384], 63)
        scr = arena("scr", [P, 2, 512], 68)
        gscr = arena("gscr", [P, 2, 384], 68)
        gnb = arena("gnb", [P, NT, P], 72)
        dqT = arena("dqT", [P, HEADS, TOK], 32)
        dkT = arena("dkT", [P, HEADS, TOK], 40)
        prob = arena("prob", [P, 2, 2, 512], 48)
        aT = arena("aT", [P, 2, 512], 56)
        modrow_diff = arena("modrow_diff", [4, 512], 72)
        gbc = arena("gbc", [P, 2, D], 60)
        xn2 = arena("xn2", [P, NT, D], 0)
        hid_hi = arena("hid_hi", [P, 12, TOK], 0, F32R)
        hid_lo = arena("hid_lo", [P, 12, TOK], 24, F32R)
        sg = arena("sg", [P, 2, 512], 48)
        hf = arena("hf", [P, 2, 512], 52)
        y = arena("y", [P, LT, D], 8)
        g_hi = arena("g_hi", [P, KD, P], 16, F32R)
        g_lo = arena("g_lo", [P, KD, P], 20, F32R)
        h2T = arena("h2T", [P, KD, SEQ], 24)
        e_hi = arena("e_hi", [P, FC, P], 24, F32R)
        e_lo = arena("e_lo", [P, FC, P], 35, F32R)
        eh = arena("eh", [P, 2, 512], 46)
        esg = arena("esg", [P, 2, 512], 50)
        oute = arena("oute", [P, D], 54)
        pick = arena("pick", [P, LT, P], 58)
        gpick = arena("gpick", [P, LT, P], 59)
        gpickT = arena("gpickT", [P, SEQ], 60)
        triu = arena("triu", [P, P], 61)
        iota = arena("iota", [P, P], 61.5)
        ones = arena("ones", [P, P], 62)
        rw = arena("rw", [P, KD, N_EXP], 62.5)
        rt = arena("rt", [P, 16, LT, N_EXP], 62.75)
        rank17 = arena("rank17", [P, LT, 17], 72.5)
        gate16 = arena("gate16", [P, LT, 16], 63.875)
        gbc1 = arena("gbc1", [P, D], 64)
        top8 = arena("top8", [P, LT, 8], 68)
        topi = arena("topi", [P, LT, 8], 68.0625, U32)
        topf = arena("topf", [P, LT, 8], 68.125)
        steps_i = arena("steps_i", [P, 1], 68.1875, I32)
        rbias = arena("rbias", [P, N_EXP], 68.25)
        gtmp = arena("gtmp", [P, 2, 512], 68.5)

        ps = ctx.enter_context(nc.psum_tensor("ps", [P, 8, 512], F32))

        start_loaded = sem("start_loaded")
        x_loaded = sem("x_loaded")
        gn_loaded = sem("gn_loaded")
        gn_used = sem("gn_used")
        dist_loaded = sem("dist_loaded")
        moe_consts = sem("moe_consts")
        raw_full = [sem(f"raw_full{i}") for i in range(RAW)]
        hi_ready = sem("hi_ready")
        lo_ready = sem("lo_ready")
        w_used = sem("w_used")
        vT_done = sem("vT_done")
        vcol_ready = sem("vcol_ready")
        cs_silu = sem("cs_silu")
        cs_ready = sem("cs_ready")
        ada_row = sem("ada_row")
        ada_T = sem("ada_T")
        ada_col = sem("ada_col")
        ss_ready = sem("ss_ready")
        ms_ready = sem("ms_ready")
        rs_ready = sem("rs_ready")
        xn_ready = sem("xn_ready")
        xT_done = sem("xT_done")
        h_whole = sem("h_whole")
        h_lo = sem("h_lo")
        acol_ready = sem("acol_ready")
        proj_out = sem("proj_out")
        lsig = sem("lsig")
        lsig_v = sem("lsig_v")
        dec_exp = sem("dec_exp")
        dec_ready = sem("dec_ready")
        ret_s = sem("ret_s")
        ret_p = sem("ret_p")
        ret_o = sem("ret_o")
        ret_ve = sem("ret_ve")
        ret_rs = sem("ret_rs")
        ret_done = sem("ret_done")
        qk_ms = sem("qk_ms")
        qk_rs = sem("qk_rs")
        qk_tok = sem("qk_tok")
        qk_T = sem("qk_T")
        qk_out = sem("qk_out")
        att_s = sem("att_s")
        att_max = sem("att_max")
        att_exp = sem("att_exp")
        att_a = sem("att_a")
        att_T = sem("att_T")
        att_aT = sem("att_aT")
        att_o = sem("att_o")
        att_sq = sem("att_sq")
        att_ms = sem("att_ms")
        att_rs = sem("att_rs")
        att_done = sem("att_done")
        cat_T = sem("cat_T")
        cat_hi = sem("cat_hi")
        cat_lo = sem("cat_lo")
        tile_out = sem("tile_out")
        gate_T = sem("gate_T")
        gate_ready = sem("gate_ready")
        out_added = sem("out_added")
        silu_done = sem("silu_done")
        hid_ready = sem("hid_ready")
        down_added = sem("down_added")
        logits_done = sem("logits_done")
        top_diff = sem("top_diff")
        top_exp = sem("top_exp")
        sel_ready = sem("sel_ready")
        rank_done = sem("rank_done")
        steps_ready = sem("steps_ready")
        pick_ready = sem("pick_ready")
        gath_done = sem("gath_done")
        gath_hi = sem("gath_hi")
        gath_lo = sem("gath_lo")
        pickT_ready = sem("pickT_ready")
        e_silu = sem("e_silu")
        e_h = sem("e_h")
        e_T = sem("e_T")
        e_hid_hi = sem("e_hid_hi")
        e_hid = sem("e_hid")
        e_out = sem("e_out")
        e_scat = sem("e_scat")
        e_y = sem("e_y")
        y_ready = sem("y_ready")
        stored = sem("stored")

        NQT = [NT, LT]
        NQ = [TOK, SEQ]
        UNITS = [NQT[0] * HEADS, NQT[1] * HEADS]
        UBASE = [0, UNITS[0]]
        NORM_TILES = [NT, NT, NT, LT]
        NBASE = [0, 4, 8, 12]
        QK_TILES = [[NT, NT], [NT, LT]]
        QK_BASE = [[0, NT], [2 * NT, 3 * NT]]
        QTB = [0, NQT[0]]
        NORM_ADDS = [2 * NT, 2 * NT + 2 * LT]
        STREAMS = [2, 2, 2, 1]
        SBASE = [0, 2, 4, 6]
        GBASE = [0, 4, 8, 12]

        def turned_at(k, s):
            return 4 * s + k // 2, k % 2 * SEQ

        OUT_HALF = [0, 2 + 2 * len(FFN_PHASES)]

        def tiles_before(half):
            n = min(half, OUT_HALF[1])
            return (NT - 1) * n + (LT - 1) * (half - n)

        def chunk_steps(layer, n_units):
            return {2 * i: DIFF_FILL[layer] + i for i in range(n_units // 2)}

        FILL = [chunk_steps(layer, UNITS[layer]) for layer in range(2)]
        assert DIFF_FILL[0] + len(FILL[0]) == RET_FILL[1] and DIFF_FILL[1] + len(FILL[1]) == 2 * ADA_CHUNKS

        def stream():
            ada_w, w_in, w_out = io["ada_w"], io["w_in"], io["w_out"]
            wg, wu, wd = io["ffn_w_gate"], io["ffn_w_up"], io["ffn_w_down"]

            def ada_chunk(c):
                layer, n = divmod(c, ADA_CHUNKS)
                for kh in range(2):
                    yield ("ada", c), ada_w[layer, kh * 512:(kh + 1) * 512, n * 512:(n + 1) * 512], 4, 512

            def proj_group(layer, c):
                g = PROJ_ORDER[c]
                for kh in range(2):
                    yield ("proj", layer, c), w_in[layer, kh * 512:(kh + 1) * 512, g * HW:(g + 1) * HW], 4, 512

            for c in range(ADA_EARLY):
                yield from ada_chunk(c)
            for layer in range(2):
                for c in range(EARLY_PROJ):
                    yield from proj_group(layer, c)
                for h in range(HEADS):
                    yield from ada_chunk(RET_FILL[layer] + h)
                for c in range(EARLY_PROJ, NPROJ):
                    yield from proj_group(layer, c)
                for c in FILL[layer].values():
                    yield from ada_chunk(c)
                for nh in range(2):
                    for kh in range(2):
                        yield ("out", layer), w_out[layer, kh * 512:(kh + 1) * 512, nh * 512:(nh + 1) * 512], 4, 512
                if layer == 0:
                    for first, count in FFN_PHASES:
                        for j in range(first, first + count):
                            for w in (wg, wu):
                                yield "ffn", w[0, :, j * 256:(j + 1) * 256], KD, 256
                        for nh in range(2):
                            for f in range(2 * first, 2 * (first + count), 4):
                                n = min(4, 2 * (first + count) - f)
                                yield "ffn", wd[0, f * P:(f + n) * P, nh * 512:(nh + 1) * 512], n, 512

        SLOTS, FIRST = [], {}
        for step, *load_of in stream():
            FIRST.setdefault(step, len(SLOTS))
            SLOTS.append(load_of)
        assert len(SLOTS) == MOE_BASE

        def ada_banks(c):
            if c < ADA_EARLY:
                return 4 + c % 2, 6 + c % 2
            b = 3 if c - RET_FILL[c >= RET_FILL[1]] < HEADS else 5
            return b, b

        def ada_rows(c):
            if c < ADA_EARLY:
                return modrow_start[c % 2]
            return modrow_ret if c - RET_FILL[c >= RET_FILL[1]] < HEADS else modrow_diff

        def ada_before(c):
            return c - 1 if c < ADA_EARLY else c

        assert MOE_SLOTS % SPL == 0 and len(MOE_RING) == MOE_SLOTS

        def moe_slot(j, e):
            if j < GU_SLOTS:
                g, rest = divmod(j, 4)
                full = g < MOE_GROUPS - 1
                w = io["moe_w_gate"] if rest < (2 if full else 1) else io["moe_w_up"]
                if not full:
                    return w[0, e, :, g * 512:D_FF], KD, D_FF - g * 512
                kh = rest % 2
                return w[0, e, kh * 512:(kh + 1) * 512, g * 512:(g + 1) * 512], 4, 512
            g, nh = divmod(j - GU_SLOTS, 2)
            if g == MOE_GROUPS - 1:
                return io["moe_w_down"][0, e, 4 * g * P:D_FF, :], FC - 4 * g, D
            return io["moe_w_down"][0, e, 4 * g * P:(4 * g + 4) * P, nh * 512:(nh + 1) * 512], 4, 512

        def gate_end(g):
            return 4 * g + 1 if g < MOE_GROUPS - 1 else GU_SLOTS - 2

        def up_end(g):
            return 4 * g + 3 if g < MOE_GROUPS - 1 else GU_SLOTS - 1

        def landed(i):
            return 16 * RING[:i + 1].count(RING[i])

        def moe_landed(it, j):
            r = MOE_RING[j]
            return it * (16 * MOE_RING.count(r)) + 16 * (RING.count(r) + MOE_RING[:j + 1].count(r))

        def split_before(order, i):
            return max(n for n in range(i) if order[n] == order[i]) + 1

        def bcast(ap, n):
            return ap.unsqueeze(0).to_broadcast([P, n])

        block = ctx.enter_context(nc.Block())

        @block.sync
        def _(sp):
            count = [0]

            def small(dst, src, s=start_loaded):
                sp.dma_start(dst, src).then_inc(s, 16)
                if s is start_loaded:
                    count[0] += 16

            def load(src, n, width, dst_slot):
                sp.dma_start(raw[:, dst_slot, 0:n * width].rearrange("p (c w) -> p c w", c=n),
                             src.rearrange("(c p) w -> p c w", p=P)).then_inc(raw_full[dst_slot], 16)

            small(ident[:], io["k_ident"])
            for n, name in enumerate(("c", "c_ctx")):
                v = io[name] if name == "c_ctx" else io[name].rearrange("a d -> (a d)")
                small(vrows[n * KD:(n + 1) * KD, :], v.rearrange("(k p) -> k p", p=P))
            for n, name in enumerate(("norm1_g", "norm2_g")):
                small(vrows[(2 + 2 * n) * KD:(4 + 2 * n) * KD, :],
                      io[name].rearrange("l (k p) -> (l k) p", p=P))
            small(abrows[:], io["ada_b"].rearrange("l (k p) -> (l k) p", p=P))
            for n, name in enumerate(("lam_q1", "lam_k1", "lam_q2", "lam_k2")):
                small(lamv[:, :, n, :], io[name].unsqueeze(0).to_broadcast([P, 2, DQK]))
            small(dec[:, :, 0, :], io["ret_decay_fwd"].unsqueeze(0).to_broadcast([P, 2, HEADS]))
            small(dec[:, :, 1, :], io["ret_decay_bwd"].unsqueeze(0).to_broadcast([P, 2, HEADS]))
            assert count[0] == START_LOADS
            for i in range(RAW):
                load(*SLOTS[i], RING[i])
            small(x[:, 0:LT, :], io["x"].rearrange("b (t p) d -> p (b t) d", p=P), x_loaded)
            small(x[:, LT:NT, :], io["ctx"].rearrange("b (t p) d -> p (b t) d", p=P), x_loaded)
            small(cos[:], io["k_cos"].rearrange("(t p) d -> p t d", p=P), x_loaded)
            small(sin[:], io["k_sin"].rearrange("(t p) d -> p t d", p=P), x_loaded)
            small(subln[:], io["diff_subln_g"].unsqueeze(0).to_broadcast([P, 2, P]), x_loaded)
            small(qn[:], io["diff_qn_g"].unsqueeze(0).to_broadcast([P, 2, DQK]), x_loaded)
            small(kn[:], io["diff_kn_g"].unsqueeze(0).to_broadcast([P, 2, DQK]), x_loaded)
            for i in range(RAW, MOE_BASE):
                for layer in range(2):
                    if i == FIRST["proj", layer, 0] + RAW:
                        if layer:
                            sp.wait_ge(gn_used, layer)
                            sp.wait_ge(down_added, 4 * NT)
                        small(gn[:], io["ret_gn_g"][layer:layer + 1, :].to_broadcast([P, HW]), gn_loaded)
                        small(dist[:], io["k_dist"].rearrange("n p c -> p n c"), dist_loaded)
                sp.wait_ge(lo_ready, split_before(RING, i))
                load(*SLOTS[i], RING[i])
            for j in range(MOE_SLOTS):
                if j == RAW:
                    sp.wait_ge(out_added, NORM_ADDS[1])
                    small(triu[:], io["k_triu"], moe_consts)
                    small(iota[:], io["k_iota"], moe_consts)
                    small(rw[:], io["router_w"].rearrange("a (k p) e -> p (a k) e", p=P), moe_consts)
                    small(rbias[:], io["router_b"].to_broadcast([P, N_EXP]), moe_consts)
                sp.wait_ge(lo_ready, split_before(RING + MOE_RING, MOE_BASE + j))
                load(*moe_slot(j, 0), MOE_RING[j])
            sp.wait_ge(steps_ready, 1)
            steps = sp.value_load(steps_i[0:1, 0:1], min_val=N_EXP, max_val=2 * N_EXP)
            with sp.Fori(1, steps) as it:
                expert = sp.snap(sp.to_reg(it & (N_EXP - 1)), min_val=0, max_val=N_EXP - 1)
                for j in range(MOE_SLOTS):
                    before = split_before(MOE_RING * 2, MOE_SLOTS + j) - MOE_SLOTS
                    sp.wait_ge(lo_ready, it * MOE_SLOTS + (MOE_BASE + before))
                    src, n, width = moe_slot(j, expert)
                    load(src, n, width, MOE_RING[j])
            sp.wait_ge(y_ready, 1)
            sp.dma_start(out.rearrange("b (t p) d -> p (b t) d", p=P), x[:, 0:LT, :]).then_inc(stored, 16)
            sp.wait_ge(stored, 16)

        def hi_split(act, i_slot, place, landed_value, used_value, n=SLOT):
            act.wait_ge(raw_full[place], landed_value)
            if used_value is not None:
                act.wait_ge(w_used, used_value)
            nc.scalar.activation(whi[i_slot % SPL][:, 0:n], raw[:, place, 0:n], ACT.Copy).then_inc(hi_ready, 1)

        def lo_split(dve, i_slot, place, hi_value, n=SLOT):
            dve.wait_ge(hi_ready, hi_value)
            nc.vector.tensor_tensor(wlo[i_slot % SPL][:, 0:n], raw[:, place, 0:n],
                                    whi[i_slot % SPL][:, 0:n].bitcast(F32),
                                    ALU.subtract).then_inc(lo_ready, 1)

        @block.scalar
        def _(act):
            nxt = [0]

            def split_to(i):
                while nxt[0] <= min(i, MOE_BASE - 1):
                    k = nxt[0]
                    n = SLOTS[k][1] * SLOTS[k][2]
                    hi_split(act, k, RING[k], landed(k), k - SPL + 1 if k >= SPL else None, n)
                    nxt[0] += 1

            def ada_row_copy(c):
                act.wait_ge(w_used, FIRST["ada", c] + 2)
                if c >= 2:
                    act.wait_ge(ada_T, ada_before(c))
                nc.scalar.copy(ada_rows(c)[:], ps[0:4, ada_banks(c)[0], :]).then_inc(ada_row, 1)

            def squares_of(which, tt):
                n = NORM_TILES[which]
                if which == 0:
                    if tt == 0:
                        act.wait_ge(x_loaded, 16 * 5)
                elif which == 2:
                    act.wait_ge(down_added, 3 * n + tt + 1)
                else:
                    act.wait_ge(out_added, NORM_ADDS[which // 2] - n + tt + 1)
                if tt:
                    act.drain()
                r = nc.scalar.activation(junk[:], x[:, tt, :], ACT.Square, accum_out=ss[:, tt:tt + 1])
                if tt % LT == LT - 1:
                    r.then_inc(ss_ready, 1)

            def modulate(which, layer):
                shift = (0 if which % 2 == 0 else 3) * KD
                act.wait_ge(acol_ready, which + 1)
                for g in range(2 * STREAMS[which]):
                    s, half = divmod(g, 2)
                    n = GBASE[which] + g
                    act.wait_ge(xT_done, n + 1)
                    if which < 3 and n >= 2:
                        act.wait_ge(h_lo, n - 1)
                    for i in range(4):
                        k = 4 * half + i
                        b, off = turned_at(k, s)
                        last = nc.scalar.activation(
                            h2T[:, k, :] if which == 3 else htmp[:, n % 2, i, :], ps[:, b, off:off + SEQ],
                            ACT.Identity, bias=modcol[layer][:, shift + k, s:s + 1], scale=acol[:, k, s:s + 1])
                    last.then_inc(h_whole, 1)

            def cat_parts(layer, ks):
                for k in ks:
                    act.wait_ge(cat_T, layer * KD + k + 1)
                    nc.scalar.copy(hT_hi[:, k, 0:NQ[layer]], ps[:, k, 0:NQ[layer]]).then_inc(cat_hi, 1)

            def gate_rows(n, dst, streams, bank=0):
                act.wait_ge(gate_T, n + 1)
                for s in range(streams):
                    last = nc.scalar.copy(dst(s), ps[:, bank + 2 * s:bank + 2 * s + 2, :])
                last.then_inc(gate_ready, 1)

            def decays(layer, h):
                f, b = h, HEADS + h
                n = layer * HEADS + h
                act.wait_ge(dist_loaded, 16 * (layer + 1))
                if n:
                    act.wait_ge(dec_ready, n)
                if n >= 2:
                    act.wait_ge(ret_p, n - 1)
                nc.scalar.activation(decL[h % 2][:], dist[:, 0, :], ACT.Exp, scale=lg[:, layer, f:f + 1])
                nc.scalar.activation(gscr[:, 0, :], dist[:, 1, :], ACT.Exp, scale=lg[:, layer, b:b + 1])
                nc.scalar.activation(decC[h % 2][:], dist[:, 2, :], ACT.Exp, scale=lg[:, layer, f:f + 1],
                                     bias=lg256[:, layer, f:f + 1])
                nc.scalar.activation(gscr[:, 1, :], dist[:, 2, :], ACT.Exp, scale=nlg[:, layer, b:b + 1],
                                     bias=lg256[:, layer, b:b + 1]).then_inc(dec_exp, 1)

            def proj(layer, c, s):
                g = PROJ_ORDER[c]
                split_to(s + 2)
                act.wait_ge(w_used, s + 1)
                b = (c % 2) * 4
                if g in (RQ, RK):
                    w = NQ[layer] if g == RQ else TOK
                    for h in range(HEADS):
                        last = nc.scalar.copy(qkT[:, 0 if g == RQ else 1, h, 0:w], ps[:, b + h, 0:w])
                else:
                    dst = {RV: rv, RG: rg, DK: dtok, DQ: dtok, DV: dv}[g]
                    tiles = NQT[layer] if g in (RG, DQ) else NT
                    if g == DQ:
                        act.wait_ge(qk_T, 2 * layer + 1)
                    for tt in range(tiles):
                        last = nc.scalar.activation(dst[:, tt, :], ps[:, b + tt, :],
                                                    ACT.Silu if g == RG else ACT.Copy)
                last.then_inc(proj_out, 1)

            def qk_turned(layer, q):
                n = 2 * layer + q
                w = QK_TILES[layer][q] * P
                b = 4 * q
                act.wait_ge(qk_T, n + 1)
                for h in range(HEADS):
                    last = nc.scalar.copy((dqT if q else dkT)[:, h, 0:w], ps[:, b + h, 0:w])
                last.then_inc(qk_out, 1)

            def exps(layer, u):
                n = UBASE[layer] + u
                keys = TOK if u // HEADS < LT else CTX
                act.wait_ge(att_max, n + 1)
                if n >= 2:
                    act.wait_ge(att_T, n - 1)
                for m in range(2):
                    last = nc.scalar.activation(prob[:, u % 2, m, 0:keys], ps[:, 2 * (u % 2) + m, 0:keys],
                                                ACT.Exp, bias=negmax[:, u % 2, m:m + 1],
                                                accum_out=psum_p[:, u % 2, m:m + 1])
                last.then_inc(att_exp, 1)

            def turned(layer, u):
                n = UBASE[layer] + u
                keys = TOK if u // HEADS < LT else CTX
                act.wait_ge(att_T, n + 1)
                if n >= 2:
                    act.wait_ge(att_o, n - 1)
                nc.scalar.copy(aT[:, u % 2, 0:keys], ps[:, 4, 0:keys]).then_inc(att_aT, 1)

            def squares(layer, qt):
                n = QTB[layer] + qt
                act.wait_ge(att_o, UBASE[layer] + HEADS * (qt + 1))
                if n:
                    act.wait_ge(att_ms, n)
                nc.scalar.activation(scr[:, 0, :], ps[:, 6 + qt % 2, :], ACT.Square).then_inc(att_sq, 1)

            act.wait_ge(vcol_ready, 1)
            nc.scalar.activation(cs32[:, :, 0], vcol[:, 0:KD], ACT.Silu)
            nc.scalar.activation(cs32[:, :, 1], vcol[:, KD:2 * KD], ACT.Silu).then_inc(cs_silu, 1)
            act.wait_ge(lsig_v, 1)
            nc.scalar.activation(lgt[:, 1:3, :], lgt[:, 1:3, :], ACT.Exp)
            nc.scalar.activation(lamp[:], lamp[:], ACT.Exp).then_inc(lsig, 1)
            act.wait_ge(lsig_v, 2)
            nc.scalar.activation(lgt[:, 1:3, :], lgt[:, 1:3, :], ACT.Ln).then_inc(lsig, 1)

            for c in range(ADA_EARLY):
                split_to(FIRST["ada", c] + 3)
                ada_row_copy(c)
                if c == 1:
                    for tt in range(NT):
                        squares_of(0, tt)
            for layer in range(2):
                proj_s = FIRST["proj", layer, 0]
                split_to(proj_s + 1)
                if layer:
                    for tt in range(NT):
                        squares_of(2, tt)
                modulate(2 * layer, layer)
                split_to(proj_s + 2)
                for c in range(EARLY_PROJ - 1):
                    proj(layer, c, proj_s + 2 * c + 1)
                decays(layer, 0)
                proj(layer, EARLY_PROJ - 1, proj_s + 2 * EARLY_PROJ - 1)
                decays(layer, 1)
                for h in range(HEADS):
                    c = RET_FILL[layer] + h
                    split_to(FIRST["ada", c] + 3)
                    ada_row_copy(c)
                    if h + 2 < HEADS:
                        decays(layer, h + 2)
                gate_rows(2 * layer, lambda s: gbc[:, s, :].rearrange("p (a c) -> p a c", a=2), 2 - layer)
                qk_turned(layer, 0)
                for c in range(EARLY_PROJ, NPROJ):
                    proj(layer, c, FIRST["proj", layer, c] + 1)
                qk_turned(layer, 1)
                out_s = FIRST["out", layer]
                U = UNITS[layer]
                for u in range(U + 2):
                    if u < U:
                        exps(layer, u)
                        c = FILL[layer].get(u - u % 2)
                        split_to(FIRST["ada", c] + 2 + u % 2)
                    if 1 <= u <= U:
                        turned(layer, u - 1)
                    if u == U:
                        cat_parts(layer, range(0, HEADS))
                    if u >= 2 and (u - 2) % HEADS == HEADS - 1:
                        squares(layer, (u - 2) // HEADS)
                    if u in FILL[layer]:
                        ada_row_copy(c)
                split_to(out_s + 2)
                cat_parts(layer, range(HEADS, KD))
                split_to(out_s + 5)
                which = 2 * layer + 1
                for tt in range(NORM_TILES[which]):
                    squares_of(which, tt)
                modulate(which, layer)
                if layer == 0:
                    gate_rows(1, lambda s: gbc[:, s, :].rearrange("p (a c) -> p a c", a=2), 2)
                    split_to(out_s + 6)
                    s = FIRST["ffn"]
                    fchunk = 0
                    for ph, (first, count) in enumerate(FFN_PHASES):
                        for j in range(count):
                            for fi in range(2):
                                split_to(s + 1 + 2)
                                act.wait_ge(w_used, s + 2)
                                if fchunk >= 2:
                                    act.wait_ge(hid_ready, fchunk - 1)
                                nc.scalar.activation(sg[:, fi, :], ps[:, 4 * (j % 2) + fi, :],
                                                     ACT.Silu).then_inc(silu_done, 1)
                                fchunk += 1
                            s += 2
                        s += FFN_PHASE_SLOTS[ph] - 2 * count
                        split_to(s - 1)
            gate_rows(3, lambda s: gbc1[:].rearrange("p (a c) -> p a c", a=2), 1, bank=6)
            act.wait_ge(top_diff, 1)
            nc.scalar.activation(topf[:, :, 2], topf[:, :, 3], ACT.Exp).then_inc(top_exp, 1)

            act.wait_ge(steps_ready, 1)
            steps = act.value_load(steps_i[0:1, 0:1], min_val=N_EXP, max_val=2 * N_EXP)

            def gathered(n):
                act.wait_ge(gath_done, n)
                for k in range(KD):
                    last = nc.scalar.activation(
                        g_hi[:, k, :], ps[:, k // 4, (k % 4) * P:(k % 4 + 1) * P], ACT.Identity,
                        bias=modcol[1][:, 3 * KD + k, 0:1], scale=acol[:, k, 0:1])
                last.then_inc(gath_hi, 1)

            def down_out(w_value):
                act.wait_ge(w_used, w_value)
                nc.scalar.copy(oute[:].rearrange("p (a c) -> p a c", a=2), ps[:, 5:7, :]).then_inc(e_out, 1)

            gathered(1)
            with act.Fori(0, steps) as it:
                nxt_e = [0]

                def split_e(last):
                    while nxt_e[0] <= last:
                        j = nxt_e[0]
                        hi_split(act, MOE_BASE + j, MOE_RING[j], moe_landed(it, j),
                                 it * MOE_SLOTS + (MOE_BASE + j - SPL + 1))
                        nxt_e[0] += 1

                def hidden(g):
                    n = min(4, FC - 4 * g)
                    act.wait_ge(e_T, it * MOE_GROUPS + (g + 1))
                    nc.scalar.copy(e_hi[:, 4 * g:4 * g + n, :],
                                   ps[:, (4, 7)[g % 2], 0:n * P].rearrange("p (f s) -> p f s", s=P)).then_inc(e_hid_hi, 1)

                split_e(1)
                down_out(it * MOE_SLOTS + MOE_BASE)
                split_e(2)
                for g in range(MOE_GROUPS):
                    w = min(512, D_FF - 512 * g)
                    split_e(gate_end(g) + SPL)
                    act.wait_ge(w_used, it * MOE_SLOTS + (MOE_BASE + gate_end(g) + 1))
                    if g >= 2:
                        act.wait_ge(e_h, it * MOE_GROUPS + (g - 1))
                    nc.scalar.activation(esg[:, g % 2, 0:w], ps[:, g % 2, 0:w], ACT.Silu).then_inc(e_silu, 1)
                    if g:
                        hidden(g - 1)
                split_e(TURN_AFTER + SPL)
                hidden(MOE_GROUPS - 1)
                split_e(GATHER_AFTER + SPL)
                gathered(it + 2)
                nc.scalar.copy(gpickT[:], ps[:, 3, 0:SEQ]).then_inc(pickT_ready, 1)
                split_e(MOE_SLOTS - 1)
            down_out(act.snap(steps * MOE_SLOTS + MOE_BASE, min_val=N_EXP * MOE_SLOTS + MOE_BASE,
                              max_val=2 * N_EXP * MOE_SLOTS + MOE_BASE))

        @block.gpsimd
        def _(pool):
            def inv_sqrt(dst, src, n, wait, value, done):
                pool.wait_ge(wait, value)
                nc.gpsimd.tensor_tensor(dst, src, neghalf[:, 0:n], ALU.pow).then_inc(done, 1)

            def norm_streams(which):
                for s in range(STREAMS[which]):
                    cols = slice(LT * s, LT * (s + 1))
                    inv_sqrt(rstd[:, cols], msq[:, cols], LT, ms_ready, SBASE[which] + s + 1, rs_ready)

            nc.gpsimd.memset(neghalf[:], -0.5).then_inc(rs_ready, 1)
            pool.wait_ge(rs_ready, 1)
            for layer in range(2):
                norm_streams(2 * layer)
                for h in range(HEADS):
                    n = NQT[layer]
                    inv_sqrt(grs[:, 0:n], gve[:, 0:n], n, ret_ve, layer * HEADS + h + 1, ret_rs)
                for q in range(2):
                    n = 8 * QK_TILES[layer][q]
                    inv_sqrt(rstd[:, 0:n], msq[:, 0:n], n, qk_ms, 2 * layer + q + 1, qk_rs)
                for qt in range(NQT[layer]):
                    inv_sqrt(rstd[:, 0:HEADS], msq[:, 0:HEADS], HEADS, att_ms, QTB[layer] + qt + 1, att_rs)
                norm_streams(2 * layer + 1)

        @block.vector
        def _(dve):
            nxt = [0]
            v = nc.vector

            def split_to(i):
                while nxt[0] <= min(i, MOE_BASE - 1):
                    k = nxt[0]
                    lo_split(dve, k, RING[k], k + 1, SLOTS[k][1] * SLOTS[k][2])
                    nxt[0] += 1

            def ada_columns(c):
                layer, n = divmod(c, ADA_CHUNKS)
                dve.wait_ge(ada_T, c + 1)
                t = ps[:, ada_banks(c)[1], 0:16].rearrange("p (j r) -> p j r", r=4)
                b = abcol[:, layer * 6 * KD + 4 * n:layer * 6 * KD + 4 * n + 4]
                v.tensor_tensor(modtmp[:], t[:, :, 0:2], b.unsqueeze(2).to_broadcast([P, 4, 2]), ALU.add)
                dve.drain()
                v.tensor_tensor(modcol[layer][:, 4 * n:4 * n + 4, :], t[:, :, 2:4], modtmp[:],
                                ALU.add).then_inc(ada_col, 1)
                dve.drain()

            def norm_mean(which, s):
                cols = slice(LT * s, LT * (s + 1))
                dve.wait_ge(ss_ready, SBASE[which] + s + 1)
                v.tensor_scalar(msq[:, cols], ss[:, cols], 1.0 / D, EPS, ALU.mult, ALU.add).then_inc(ms_ready, 1)

            def norm_columns(which, layer):
                scale = (1 if which % 2 == 0 else 4) * KD
                gains = vcol[:, (2 + which % 2 * 2 + layer) * KD:(3 + which % 2 * 2 + layer) * KD]
                for s in range(2):
                    last = v.scalar_tensor_tensor(acol[:, :, s], modcol[layer][:, scale:scale + KD, s], 1.0,
                                                  gains, ALU.add, ALU.mult)
                last.then_inc(acol_ready, 1)

            def norm_tokens(which, s):
                buf = xn if which % 2 == 0 else xn2
                dve.wait_ge(rs_ready, SBASE[which] + s + 2)
                for tt in range(LT * s, LT * (s + 1)):
                    v.tensor_scalar(buf[:, tt, :], x[:, tt, :], rstd[:, tt:tt + 1], None,
                                    ALU.mult).then_inc(xn_ready, 1)

            def norm_parts(which):
                for g in range(2 * STREAMS[which]):
                    s, half = divmod(g, 2)
                    n = GBASE[which] + g
                    hi = hT_hi[:, 4 * half:4 * half + 4, s * SEQ:(s + 1) * SEQ]
                    dve.wait_ge(h_whole, n + 1)
                    v.tensor_copy(hi, htmp[:, n % 2, :, :])
                    dve.drain()
                    v.tensor_tensor(hT_lo[:, 4 * half:4 * half + 4, s * SEQ:(s + 1) * SEQ], htmp[:, n % 2, :, :],
                                    hi.bitcast(F32), ALU.subtract).then_inc(h_lo, 1)

            def cat_parts(layer, ks):
                for k in ks:
                    dve.wait_ge(cat_hi, layer * KD + k + 1)
                    v.tensor_tensor(hT_lo[:, k, 0:NQ[layer]], ps[:, k, 0:NQ[layer]],
                                    hT_hi[:, k, 0:NQ[layer]].bitcast(F32), ALU.subtract).then_inc(cat_lo, 1)

            def add_half(half, tiles, nh, end, gates, done, norm=None):
                split_to(end + 2)
                for tt in range(tiles):
                    if tt < tiles - 1:
                        dve.wait_ge(tile_out, tiles_before(half) + tt + 1)
                    else:
                        dve.wait_ge(w_used, end + 1)
                    if norm is not None and tt == tiles - 1 and tiles == NT:
                        norm_columns(norm, norm // 2)
                        norm_tokens(norm, 0)
                    add_gated(4 * nh + tt, tt, nh, gates[:, 0 if tt < LT else 1, nh * 512:(nh + 1) * 512], done, tt)
                    if norm is not None and tt % LT == LT - 1:
                        norm_mean(norm, tt // LT)
                if norm is not None:
                    if tiles == LT:
                        norm_columns(norm, norm // 2)
                    norm_tokens(norm, STREAMS[norm] - 1)
                    if norm < 3:
                        norm_parts(norm)
                split_to(end + 3)

            def decays(layer, h):
                dve.wait_ge(dec_exp, layer * HEADS + h + 1)
                v.tensor_tensor(decL[h % 2][:], decL[h % 2][:], gscr[:, 0, :], ALU.add)
                v.tensor_tensor(decC[h % 2][:], decC[h % 2][:], gscr[:, 1, :], ALU.add).then_inc(dec_ready, 1)

            def weigh(layer, h):
                n = layer * HEADS + h
                dve.wait_ge(ret_s, n + 1)
                dve.drain()
                b = 4 * ((h + 1) % 2)
                buf = pT[:, h % 2, :]
                for kt in range(NT):
                    i = kt % LT
                    near = decL[h % 2][:, P * (1 - i):P * (1 - i) + SEQ]
                    far = decC[h % 2][:, P * (1 - i):P * (1 - i) + SEQ]
                    bank, off, dst = (b, kt * SEQ, kt * SEQ) if kt < LT else (b + kt - 1, 0, 512 * (kt - 1))
                    last = v.scalar_tensor_tensor(buf[:, dst:dst + SEQ], ps[:, bank, off:off + SEQ], K_SCALE,
                                                  near if kt < LT else far, ALU.mult, ALU.mult)
                    if kt >= LT and layer == 0:
                        last = v.scalar_tensor_tensor(buf[:, dst + SEQ:dst + TOK], ps[:, bank, SEQ:TOK],
                                                      K_SCALE, near, ALU.mult, ALU.mult)
                last.then_inc(ret_p, 1)

            def group_norm(layer, h):
                n = layer * HEADS + h
                b = 7
                dve.wait_ge(ret_o, n + 1)
                for qt in range(NQT[layer]):
                    v.bn_stats(bst[:, qt, :], ps[:, b, qt * P:(qt + 1) * P])
                dve.drain()
                for qt in range(NQT[layer]):
                    v.bn_aggr(bag[:, qt, :], bst[:, qt, :])
                dve.drain()
                v.tensor_scalar(gve[:, 0:NQT[layer]], bag[:, 0:NQT[layer], 1], EPS, None,
                                ALU.add).then_inc(ret_ve, 1)
                dve.wait_ge(ret_rs, n + 1)
                for qt in range(NQT[layer]):
                    last = v.tensor_scalar(gnb[:, qt, :], ps[:, b, qt * P:(qt + 1) * P],
                                           bag[:, qt, 0:1], grs[:, qt:qt + 1], ALU.subtract, ALU.mult)
                dve.drain()
                cols = slice(h * P, (h + 1) * P)
                v.tensor_tensor(rg[:, 0:NQT[layer], cols], rg[:, 0:NQT[layer], cols],
                                gnb[:, 0:NQT[layer], :], ALU.mult).then_inc(ret_done, 1)

            def qk_norm(layer, q):
                tiles = QK_TILES[layer][q]
                c = PROJ_ORDER.index(DQ if q else DK)
                gain = (qn if q else kn)[:, layer, :]
                half = DQK // 2
                for tt in range(LT):
                    v.tensor_tensor(cosg[:, tt, :], cos[:, tt, :], gain, ALU.mult)
                    v.scalar_tensor_tensor(sing[:, tt, 0:half], sin[:, tt, 0:half], -1.0, gain[:, half:DQK],
                                           ALU.mult, ALU.mult)
                    v.tensor_tensor(sing[:, tt, half:DQK], sin[:, tt, half:DQK], gain[:, 0:half], ALU.mult)
                dve.wait_ge(proj_out, layer * NPROJ + c + 1)
                for tt in range(tiles):
                    v.tensor_tensor(scr[:, tt % 2, :], dtok[:, tt, :], dtok[:, tt, :], ALU.mult)
                    dve.drain()
                    v.tensor_reduce(ss[:, 8 * tt:8 * tt + 8], scr[:, tt % 2, :].rearrange("p (g e) -> p g e", e=DQK),
                                    AX.X, ALU.add)
                dve.drain()
                v.tensor_scalar(msq[:, 0:8 * tiles], ss[:, 0:8 * tiles], 1.0 / DQK, EPS, ALU.mult,
                                ALU.add).then_inc(qk_ms, 1)
                dve.wait_ge(qk_rs, 2 * layer + q + 1)
                if q:
                    v.tensor_scalar(rstd[:, 0:8 * tiles], rstd[:, 0:8 * tiles], float(DQK) ** -0.5, None, ALU.mult)
                    dve.drain()
                for tt in range(tiles):
                    a = dtok[:, tt, :].rearrange("p (g e) -> p g e", e=DQK)
                    r = rstd[:, 8 * tt:8 * tt + 8].unsqueeze(2).to_broadcast([P, 8, DQK])
                    v.tensor_tensor(a, a, r, ALU.mult)
                    dve.drain()
                    if tt < LT:
                        t1 = scr[:, 0, :].rearrange("p (g e) -> p g e", e=DQK)
                        t2 = scr[:, 1, :].rearrange("p (g e) -> p g e", e=DQK)
                        cg = cosg[:, tt, :].unsqueeze(1).to_broadcast([P, 8, DQK])
                        sa = sing[:, tt, 0:half].unsqueeze(1).to_broadcast([P, 8, half])
                        sb = sing[:, tt, half:DQK].unsqueeze(1).to_broadcast([P, 8, half])
                        v.tensor_tensor(t1, a, cg, ALU.mult)
                        v.tensor_tensor(t2[:, :, 0:half], a[:, :, half:DQK], sa, ALU.mult)
                        v.tensor_tensor(t2[:, :, half:DQK], a[:, :, 0:half], sb, ALU.mult)
                        dve.drain()
                        v.tensor_tensor(a, t1, t2, ALU.add).then_inc(qk_tok, 1)
                        dve.drain()
                    else:
                        v.tensor_tensor(a, a, gain.unsqueeze(1).to_broadcast([P, 8, DQK]),
                                        ALU.mult).then_inc(qk_tok, 1)

            def row_max(layer, u):
                n = UBASE[layer] + u
                keys = TOK if u // HEADS < LT else CTX
                dve.wait_ge(att_s, n + 1)
                v.tensor_reduce(negmax[:, u % 2, :], ps[:, 2 * (u % 2):2 * (u % 2) + 2, 0:keys], AX.X, ALU.max,
                                negate=True).then_inc(att_max, 1)

            def combine(layer, u):
                n = UBASE[layer] + u
                keys = TOK if u // HEADS < LT else CTX
                dve.wait_ge(att_exp, n + 1)
                v.reciprocal(rcp[:, u % 2, :], psum_p[:, u % 2, :])
                dve.drain()
                v.tensor_scalar(prob[:, u % 2, 1, 0:keys], prob[:, u % 2, 1, 0:keys], rcp[:, u % 2, 1:2],
                                neglam[:, layer:layer + 1], ALU.mult, ALU.mult)
                dve.drain()
                v.scalar_tensor_tensor(prob[:, u % 2, 0, 0:keys], prob[:, u % 2, 0, 0:keys], rcp[:, u % 2, 0:1],
                                       prob[:, u % 2, 1, 0:keys], ALU.mult, ALU.add).then_inc(att_a, 1)

            def sub_norm(layer, qt):
                n = QTB[layer] + qt
                dve.wait_ge(att_sq, n + 1)
                v.tensor_reduce(ss[:, 0:HEADS], scr[:, 0, :].rearrange("p (h e) -> p h e", e=P), AX.X, ALU.add)
                dve.drain()
                v.tensor_scalar(msq[:, 0:HEADS], ss[:, 0:HEADS], 1.0 / P, EPS, ALU.mult,
                                ALU.add).then_inc(att_ms, 1)
                dve.wait_ge(att_rs, n + 1)
                v.tensor_scalar(rstd[:, 0:HEADS], rstd[:, 0:HEADS], 1.0 - LAM_INIT[layer], None, ALU.mult)
                dve.drain()
                o = dtok[:, qt, :].rearrange("p (h e) -> p h e", e=P)
                v.tensor_tensor(o, ps[:, 6 + qt % 2, :].rearrange("p (h e) -> p h e", e=P),
                                rstd[:, 0:HEADS].unsqueeze(2).to_broadcast([P, HEADS, P]), ALU.mult)
                dve.drain()
                v.tensor_tensor(o, o, subln[:, layer, :].unsqueeze(1).to_broadcast([P, HEADS, P]),
                                ALU.mult).then_inc(att_done, 1)

            def add_gated(bank, tt, nh, gate, done, k):
                cols = slice(nh * 512, (nh + 1) * 512)
                v.tensor_tensor(scr[:, k % 2, :], ps[:, bank, :], gate, ALU.mult)
                dve.drain()
                v.tensor_tensor(x[:, tt, cols], x[:, tt, cols], scr[:, k % 2, :], ALU.add).then_inc(done, 1)

            dve.wait_ge(vT_done, 1)
            v.tensor_copy(vcol[:], ps[:, 0, 0:VEC_ROWS])
            v.tensor_copy(abcol[:], ps[:, 1, 0:ADAB_ROWS]).then_inc(vcol_ready, 1)
            dve.wait_ge(start_loaded, START_LOADS)
            d8 = dec[:].rearrange("p l d h -> p l (d h)")
            v.tensor_scalar(lgt[:, 1:3, :], d8, -1.0, None, ALU.mult)
            v.tensor_scalar(lg[:], d8, 0.0, None, ALU.min)
            v.tensor_tensor(lamt[:, :, 0, :], lamv[:, :, 0, :], lamv[:, :, 1, :], ALU.mult)
            v.tensor_tensor(lamt[:, :, 1, :], lamv[:, :, 2, :], lamv[:, :, 3, :], ALU.mult)
            dve.drain()
            v.tensor_tensor(lgt[:, 1:3, :], lgt[:, 1:3, :], d8, ALU.min)
            v.tensor_reduce(lamp[:], lamt[:], AX.X, ALU.add).then_inc(lsig_v, 1)
            dve.wait_ge(cs_silu, 1)
            v.tensor_copy(cs[:, :, 0:2], cs32[:])
            dve.drain()
            v.tensor_tensor(cs[:, :, 2:4], cs32[:], cs[:, :, 0:2].bitcast(F32), ALU.subtract).then_inc(cs_ready, 1)
            dve.wait_ge(lsig, 1)
            v.tensor_scalar(lgt[:, 1:3, :], lgt[:, 1:3, :], 1.0, None, ALU.add).then_inc(lsig_v, 1)
            v.tensor_tensor(neglam[:], lamp[:, :, 1], lamp[:, :, 0], ALU.subtract)
            dve.drain()
            for layer in range(2):
                v.tensor_scalar(neglam[:, layer:layer + 1], neglam[:, layer:layer + 1], -LAM_INIT[layer], None,
                                ALU.add)
            dve.wait_ge(lsig, 2)
            v.tensor_tensor(lg[:], lg[:], lgt[:, 1:3, :], ALU.subtract)
            dve.drain()
            v.tensor_scalar(lg[:], lg[:], -1e-20, None, ALU.min)
            dve.drain()
            v.tensor_scalar(lg256[:], lg[:], float(CTX), None, ALU.mult)
            v.tensor_scalar(nlg[:], lg[:], -1.0, None, ALU.mult)
            dve.drain()

            for c in range(ADA_EARLY):
                split_to(FIRST["ada", c] + 3)
                ada_columns(c)
                if c == 1:
                    for s in range(2):
                        norm_mean(0, s)
                    for s in range(2):
                        norm_tokens(0, s)
            norm_columns(0, 0)
            norm_parts(0)
            for layer in range(2):
                proj_s = FIRST["proj", layer, 0]
                split_to(proj_s + 2)
                split_to(proj_s + 2 * 3 + 1 + 3)
                dve.wait_ge(gn_loaded, 16 * (layer + 1))
                dve.wait_ge(proj_out, layer * NPROJ + PROJ_ORDER.index(RG) + 1)
                t = NQT[layer]
                v.tensor_tensor(rg[:, 0:t, :], rg[:, 0:t, :], gn[:].unsqueeze(1).to_broadcast([P, t, HW]),
                                ALU.mult).then_inc(gn_used, 1)
                decays(layer, 0)
                split_to(FIRST["ada", RET_FILL[layer]] + 1)
                for h in range(HEADS):
                    weigh(layer, h)
                    if h + 1 < HEADS:
                        decays(layer, h + 1)
                    c = RET_FILL[layer] + h
                    split_to(FIRST["ada", c] + 3)
                    if h:
                        group_norm(layer, h - 1)
                    ada_columns(c)
                group_norm(layer, HEADS - 1)
                qk_norm(layer, 0)
                split_to(FIRST["proj", layer, EARLY_PROJ] + 3)
                qk_norm(layer, 1)
                out_s = FIRST["out", layer]
                split_to(FIRST["ada", DIFF_FILL[layer]] + 1)
                U = UNITS[layer]
                for u in range(U + 3):
                    if u < U:
                        row_max(layer, u)
                    if 1 <= u <= U:
                        combine(layer, u - 1)
                    if u >= 3 and (u - 3) % HEADS == HEADS - 1:
                        sub_norm(layer, (u - 3) // HEADS)
                    if u < U:
                        c = FILL[layer][u - u % 2]
                        split_to(FIRST["ada", c] + 2 + u % 2)
                        if u % 2:
                            ada_columns(c)
                    if u == U + 1:
                        cat_parts(layer, range(0, HEADS))
                split_to(out_s + 2)
                cat_parts(layer, range(HEADS, KD))
                dve.wait_ge(gate_ready, 2 * layer + 1)
                for nh in range(2):
                    add_half(OUT_HALF[layer] + nh, NQT[layer], nh, out_s + 2 * nh + 1, gbc, out_added,
                             2 * layer + 1 if nh else None)
                if layer == 0:
                    s = FIRST["ffn"]
                    fchunk = 0
                    for ph, (first, count) in enumerate(FFN_PHASES):
                        for j in range(count):
                            for fi in range(2):
                                split_to(s + 1 + 2)
                                dve.wait_ge(silu_done, fchunk + 1)
                                v.tensor_tensor(hf[:, fi, :], ps[:, 4 * (j % 2) + 2 + fi, :], sg[:, fi, :], ALU.mult)
                                dve.drain()
                                v.tensor_copy(hid_hi[:, 2 * j + fi, :], hf[:, fi, :])
                                dve.drain()
                                v.tensor_tensor(hid_lo[:, 2 * j + fi, :], hf[:, fi, :],
                                                hid_hi[:, 2 * j + fi, :].bitcast(F32),
                                                ALU.subtract).then_inc(hid_ready, 1)
                                fchunk += 1
                            s += 2
                        if ph == 0:
                            dve.wait_ge(gate_ready, 2)
                        half = (FFN_PHASE_SLOTS[ph] - 2 * count) // 2
                        for nh in range(2):
                            s += half
                            add_half(2 + 2 * ph + nh, NT, nh, s - 1, gbc, down_added,
                                     2 if ph == len(FFN_PHASES) - 1 and nh else None)

            dve.wait_ge(moe_consts, 16 * 4)
            v.memset(ones[:], 1.0)
            dve.wait_ge(logits_done, 1)
            lgts = rt[:, 0, :, :]
            v.tensor_tensor(lgts, ps[:, 4, 0:16].rearrange("p (t e) -> p t e", e=N_EXP),
                            rbias[:].unsqueeze(1).to_broadcast([P, LT, N_EXP]), ALU.add)
            dve.drain()
            for tt in range(LT):
                v.max(top8[:, tt, :], rt[:, 0, tt, :])
            dve.drain()
            for tt in range(LT):
                v.max_index(topi[:, tt, :], top8[:, tt, :], rt[:, 0, tt, :])
            dve.drain()
            v.tensor_copy(topf[:, :, 0:2], topi[:, :, 0:2])
            v.tensor_tensor(topf[:, :, 3], top8[:, :, 1], top8[:, :, 0], ALU.subtract).then_inc(top_diff, 1)
            dve.drain()
            for tt in range(LT):
                for j in range(2):
                    v.tensor_scalar(rt[:, 1 + j, tt, :], iota[:, 0:N_EXP], topf[:, tt, j:j + 1], None, ALU.is_equal)
            dve.drain()
            v.tensor_tensor(rt[:, 3, :, :], rt[:, 1, :, :], rt[:, 2, :, :], ALU.add).then_inc(sel_ready, 1)
            dve.wait_ge(top_exp, 1)
            v.tensor_scalar(topf[:, :, 4], topf[:, :, 2], 1.0, None, ALU.add)
            dve.drain()
            v.reciprocal(topf[:, :, 5], topf[:, :, 4])
            dve.drain()
            v.tensor_tensor(topf[:, :, 6], topf[:, :, 5], topf[:, :, 2], ALU.mult)
            dve.drain()
            for tt in range(LT):
                v.tensor_scalar(rt[:, 4, tt, :], rt[:, 1, tt, :], topf[:, tt, 5:6], None, ALU.mult)
            dve.drain()
            for tt in range(LT):
                for rep in range(2):
                    v.scalar_tensor_tensor(gate16[:, tt, rep * N_EXP:(rep + 1) * N_EXP], rt[:, 2, tt, :],
                                           topf[:, tt, 6:7], rt[:, 4, tt, :], ALU.mult, ALU.add)
            dve.wait_ge(rank_done, 1)
            ranks = ps[:, 5, 0:16].rearrange("p (t e) -> p t e", e=N_EXP)
            v.tensor_tensor(rt[:, 5, :, :], ranks, rt[:, 3, :, :], ALU.mult)
            v.tensor_reduce(topf[:, 0, 7:8], ps[:, 5, 16:16 + N_EXP], AX.X, ALU.max)
            dve.drain()
            for tt in range(LT):
                v.tensor_scalar(rank17[:, tt, 0:N_EXP], rt[:, 5, tt, :], -1.0, None, ALU.add)
                v.tensor_scalar(rank17[:, tt, N_EXP:16], rt[:, 5, tt, :], -1.0 - P, None, ALU.add)
            v.tensor_scalar(topf[:, 1, 7:8], topf[:, 0, 7:8], float(P), float(N_EXP), ALU.is_gt, ALU.mult)
            dve.drain()
            v.tensor_scalar(steps_i[:], topf[:, 1, 7:8], float(N_EXP), None, ALU.add)
            v.memset(rank17[:, :, 16:17], -1.0)
            v.memset(y[:], 0.0)
            v.memset(gpickT[:], 0.0).then_inc(pickT_ready, 1)
            dve.drain().then_inc(steps_ready, 1)
            steps = dve.value_load(steps_i[0:1, 0:1], min_val=N_EXP, max_val=2 * N_EXP)

            def pick_tokens(col):
                for tt in range(LT):
                    last = v.tensor_scalar(pick[:, tt, :], iota[:], rank17[:, tt, col], None, ALU.is_equal)
                last.then_inc(pick_ready, 1)

            def gathered(n):
                dve.wait_ge(gath_hi, n)
                for k in range(KD):
                    v.tensor_scalar(gtmp[:, k // 4, (k % 4) * P:(k % 4 + 1) * P],
                                    ps[:, k // 4, (k % 4) * P:(k % 4 + 1) * P],
                                    acol[:, k, 0:1], modcol[1][:, 3 * KD + k, 0:1], ALU.mult, ALU.add)
                dve.drain()
                v.tensor_tensor(g_lo[:].rearrange("p k s -> p (k s)"), gtmp[:].rearrange("p a c -> p (a c)"),
                                g_hi[:].rearrange("p k s -> p (k s)").bitcast(F32),
                                ALU.subtract).then_inc(gath_lo, 1)

            def add_rows(n):
                dve.wait_ge(e_scat, n)
                for tt in range(LT):
                    rows = y[:, tt, :].rearrange("p (a c) -> p a c", a=2)
                    last = v.tensor_tensor(rows, rows, ps[:, 4 + 2 * tt:6 + 2 * tt, :], ALU.add)
                last.then_inc(e_y, 1)

            pick_tokens(slice(0, 1))
            gathered(1)
            with dve.Fori(0, steps) as it:
                nxt_e = [0]

                def split_e(last):
                    while nxt_e[0] <= last:
                        j = nxt_e[0]
                        lo_split(dve, MOE_BASE + j, MOE_RING[j], it * MOE_SLOTS + (MOE_BASE + j + 1))
                        nxt_e[0] += 1

                def hidden(g):
                    n = min(4, FC - 4 * g)
                    dve.wait_ge(e_hid_hi, it * MOE_GROUPS + (g + 1))
                    v.tensor_tensor(e_lo[:, 4 * g:4 * g + n, :],
                                    ps[:, (4, 7)[g % 2], 0:n * P].rearrange("p (f s) -> p f s", s=P),
                                    e_hi[:, 4 * g:4 * g + n, :].bitcast(F32), ALU.subtract).then_inc(e_hid, 1)

                split_e(3)
                add_rows(it + 1)
                for g in range(MOE_GROUPS):
                    w = min(512, D_FF - 512 * g)
                    split_e(gate_end(g) + SPL)
                    if g:
                        hidden(g - 1)
                    if g == 1:
                        dve.wait_ge(gath_done, it + 1)
                        for tt in range(LT):
                            v.tensor_scalar(gpick[:, tt, :], iota[:], rank17[:, tt, bass.ds(it, 1)],
                                            gate16[:, tt, bass.ds(it, 1)], ALU.is_equal, ALU.mult)
                        pick_tokens(bass.ds(it + 1, 1))
                    split_e(up_end(g) + SPL)
                    dve.wait_ge(e_silu, it * MOE_GROUPS + (g + 1))
                    dve.wait_ge(w_used, it * MOE_SLOTS + (MOE_BASE + up_end(g) + 1))
                    v.tensor_tensor(eh[:, g % 2, 0:w], ps[:, 2 + g % 2, 0:w], esg[:, g % 2, 0:w],
                                    ALU.mult).then_inc(e_h, 1)
                split_e(TURN_AFTER + SPL)
                hidden(MOE_GROUPS - 1)
                split_e(GATHER_AFTER + SPL)
                gathered(it + 2)
                split_e(MOE_SLOTS - 1)
            add_rows(dve.snap(steps + 1, min_val=N_EXP + 1, max_val=2 * N_EXP + 1))
            dve.drain()
            dve.wait_ge(gate_ready, 4)
            for tt in range(LT):
                v.tensor_tensor(y[:, tt, :], y[:, tt, :], gbc1[:], ALU.mult)
            dve.drain()
            for tt in range(LT):
                last = v.tensor_tensor(x[:, tt, :], x[:, tt, :], y[:, tt, :], ALU.add)
            last.then_inc(y_ready, 1)

        @block.tensor
        def _(pe):
            mm = nc.tensor.matmul

            def product(dst, stat, mov, first, last):
                mm(dst, stat[0], mov[0], start=first, stop=False)
                mm(dst, stat[0], mov[1], start=False, stop=False)
                return mm(dst, stat[1], mov[0], start=False, stop=last)

            def parts(i):
                return whi[i % SPL], wlo[i % SPL]

            def slot(i, n, width):
                hi, lo = parts(i)
                pe.wait_ge(lo_ready, i + 1)
                return [t[:, 0:n * width].rearrange("p (c w) -> p c w", c=n) for t in (hi, lo)]

            def ada_product(c):
                bank = ada_banks(c)[0]
                if c >= 2:
                    pe.wait_ge(ada_col, ada_before(c))
                for kh in range(2):
                    w = slot(FIRST["ada", c] + kh, 4, 512)
                    for k in range(4):
                        for part in range(2):
                            last = mm(ps[0:4, bank, :], cs[:, 4 * kh + k, :], w[part][:, k, :],
                                      start=(kh + k + part == 0), stop=(kh == 1 and k == 3 and part == 1))
                    last.then_inc(w_used, 1)

            def ada_turn(c):
                pe.wait_ge(ada_row, c + 1)
                for j in range(4):
                    last = nc.tensor.transpose(ps[:, ada_banks(c)[1], 4 * j:4 * j + 4],
                                               ada_rows(c)[:, j * P:(j + 1) * P], ident[0:4, 0:4])
                last.then_inc(ada_T, 1)

            def turn(which, s):
                buf = xn if which % 2 == 0 else xn2
                pe.wait_ge(xn_ready, NBASE[which] + LT * (s + 1))
                for k in range(KD):
                    b, off = turned_at(k, s)
                    for t in range(LT):
                        last = nc.tensor.transpose(ps[:, b, off + t * P:off + (t + 1) * P],
                                                   buf[:, LT * s + t, k * P:(k + 1) * P], ident[:])
                    if k % 4 == 3:
                        last.then_inc(xT_done, 1)

            def cat_turn(layer, ks):
                for k in ks:
                    src, h = (rg, k) if k < HEADS else (dtok, k - HEADS)
                    for tt in range(NQT[layer]):
                        last = nc.tensor.transpose(ps[:, k, tt * P:(tt + 1) * P], src[:, tt, h * P:(h + 1) * P],
                                                   ident[:])
                    last.then_inc(cat_T, 1)

            def gate_rows(m, layer, streams, bank=0):
                for s in range(streams):
                    for k in range(KD):
                        last = mm(ps[:, bank + 2 * s + k // 4, (k % 4) * P:(k % 4 + 1) * P],
                                  modcol[layer][:, m * KD + k, s:s + 1].to_broadcast([P, P]), ident[:],
                                  start=True, stop=True)
                last.then_inc(gate_T, 1)

            def proj(layer, c):
                g = PROJ_ORDER[c]
                b = 4 * (c % 2)
                for kh in range(2):
                    i = FIRST["proj", layer, c] + kh
                    if c == 0:
                        pe.wait_ge(h_lo, GBASE[2 * layer] + 3 + kh)
                    w = slot(i, 4, 512)
                    for t in range(HEADS if g in (RQ, RK) else (NQT[layer] if g in (RG, DQ) else NT)):
                        for k in range(4):
                            kk = 4 * kh + k
                            if g in (RQ, RK):
                                n = NQ[layer] if g == RQ else TOK
                                last = product(ps[:, b + t, 0:n], [p[:, k, t * P:(t + 1) * P] for p in w],
                                               [hT_hi[:, kk, 0:n], hT_lo[:, kk, 0:n]], kk == 0, kk == KD - 1)
                            else:
                                cols = slice(t * P, (t + 1) * P)
                                last = product(ps[:, b + t, :], [hT_hi[:, kk, cols], hT_lo[:, kk, cols]],
                                               [p[:, k, :] for p in w], kk == 0, kk == KD - 1)
                    last.then_inc(w_used, 1)

            def ret_scores(layer, h):
                b = 4 * ((h + 1) % 2)
                n = NQ[layer]
                for kt in range(NT):
                    keys = qkT[:, 1, h, kt * P:(kt + 1) * P]
                    if kt < LT:
                        last = mm(ps[:, b, kt * SEQ:(kt + 1) * SEQ], keys, qkT[:, 0, h, 0:SEQ], start=True, stop=True)
                    else:
                        last = mm(ps[:, b + kt - 1, 0:n], keys, qkT[:, 0, h, 0:n], start=True, stop=True)
                last.then_inc(ret_s, 1)

            def ret_values(layer, h):
                b = 7
                pe.wait_ge(ret_p, layer * HEADS + h + 1)
                if h:
                    pe.wait_ge(ret_done, layer * HEADS + h)
                at_kt = [0, SEQ, 512, 1024]
                for qt in range(NQT[layer]):
                    kts = range(NT) if qt < LT else range(LT, NT)
                    for kt in kts:
                        o = at_kt[kt] + qt * P
                        last = mm(ps[:, b, qt * P:(qt + 1) * P], pT[:, h % 2, o:o + P],
                                  rv[:, kt, h * P:(h + 1) * P], start=(kt == kts[0]), stop=(kt == NT - 1))
                last.then_inc(ret_o, 1)

            def qk_turn(layer, q):
                b = 4 * q
                for tt in range(QK_TILES[layer][q]):
                    pe.wait_ge(qk_tok, QK_BASE[layer][q] + tt + 1)
                    for h in range(HEADS):
                        last = nc.tensor.transpose(ps[:, b + h, tt * P:(tt + 1) * P],
                                                   dtok[:, tt, h * P:(h + 1) * P], ident[:])
                last.then_inc(qk_T, 1)

            def scores(layer, u):
                qt, h = divmod(u, HEADS)
                n = UBASE[layer] + u
                first = 0 if qt < LT else SEQ
                if u >= 2:
                    pe.wait_ge(att_exp, n - 1)
                for m in range(2):
                    rows = slice(m * DQK, (m + 1) * DQK)
                    last = mm(ps[:, 2 * (u % 2) + m, 0:TOK - first], dqT[rows, h, qt * P:(qt + 1) * P],
                              dkT[rows, h, first:TOK], start=True, stop=True)
                last.then_inc(att_s, 1)

            def turn_a(layer, u):
                n = UBASE[layer] + u
                keys = TOK if u // HEADS < LT else CTX
                pe.wait_ge(att_a, n + 1)
                if u:
                    pe.wait_ge(att_aT, n)
                for j in range(keys // P):
                    last = nc.tensor.transpose(ps[:, 4, j * P:(j + 1) * P],
                                               prob[:, u % 2, 0, j * P:(j + 1) * P], ident[:])
                last.then_inc(att_T, 1)

            def values(layer, u):
                qt, h = divmod(u, HEADS)
                n = UBASE[layer] + u
                pe.wait_ge(att_aT, n + 1)
                if h == 0 and qt >= 2:
                    pe.wait_ge(att_done, QTB[layer] + qt - 1)
                kts = range(NT) if qt < LT else range(LT, NT)
                for kt in kts:
                    j = kt - kts[0]
                    last = mm(ps[:, 6 + qt % 2, h * P:(h + 1) * P], aT[:, u % 2, j * P:(j + 1) * P],
                              dv[:, kt, h * P:(h + 1) * P], start=(j == 0), stop=(kt == NT - 1))
                last.then_inc(att_o, 1)

            pe.wait_ge(start_loaded, START_LOADS)
            nc.tensor.transpose(ps[:, 0, 0:VEC_ROWS], vrows[:], ident[0:VEC_ROWS, 0:VEC_ROWS])
            nc.tensor.transpose(ps[:, 1, 0:ADAB_ROWS], abrows[:],
                                ident[0:ADAB_ROWS, 0:ADAB_ROWS]).then_inc(vT_done, 1)
            pe.wait_ge(vcol_ready, 1)
            pe.wait_ge(cs_ready, 1)
            for c in range(ADA_EARLY + 1):
                if c < ADA_EARLY:
                    ada_product(c)
                else:
                    turn(0, 0)
                if c:
                    ada_turn(c - 1)
            for layer in range(2):
                if layer == 0:
                    pe.wait_ge(ada_col, ADA_EARLY)
                else:
                    turn(2, 0)
                turn(2 * layer, 1)
                for c in range(EARLY_PROJ):
                    if c >= 2:
                        pe.wait_ge(proj_out, layer * NPROJ + c - 1)
                    proj(layer, c)
                pe.wait_ge(proj_out, layer * NPROJ + 4)
                for h in range(HEADS + 1):
                    if h < HEADS:
                        if h >= 2:
                            pe.wait_ge(ret_p, layer * HEADS + h - 1)
                        ret_scores(layer, h)
                        if h == 0:
                            pe.wait_ge(proj_out, layer * NPROJ + 5)
                        ada_product(RET_FILL[layer] + h)
                    if h:
                        ret_values(layer, h - 1)
                    if h < HEADS:
                        ada_turn(RET_FILL[layer] + h)
                pe.wait_ge(ada_col, RET_FILL[layer] + HEADS)
                gate_rows(2, layer, 2 - layer)
                pe.wait_ge(ret_done, layer * HEADS + HEADS)
                proj(layer, 5)
                pe.wait_ge(gate_ready, 2 * layer + 1)
                qk_turn(layer, 0)
                pe.wait_ge(qk_out, 2 * layer + 1)
                proj(layer, 6)
                pe.wait_ge(proj_out, layer * NPROJ + 6)
                qk_turn(layer, 1)
                pe.wait_ge(proj_out, layer * NPROJ + 7)
                pe.wait_ge(qk_out, 2 * layer + 2)
                U = UNITS[layer]
                for u in range(U + 2):
                    if u < U:
                        scores(layer, u)
                        if u in FILL[layer]:
                            ada_product(FILL[layer][u])
                        else:
                            ada_turn(FILL[layer][u - 1])
                    if 1 <= u <= U:
                        turn_a(layer, u - 1)
                    if u >= 2:
                        values(layer, u - 2)
                    if u == U:
                        cat_turn(layer, range(0, HEADS))
                pe.wait_ge(cat_lo, layer * KD + HEADS)
                n = NQT[layer]
                for nh in range(2):
                    for kh in range(2):
                        if nh == 0 and kh == 1:
                            pe.wait_ge(att_done, QTB[layer] + n)
                            pe.wait_ge(ada_col, DIFF_FILL[layer] + len(FILL[layer]))
                            cat_turn(layer, range(HEADS, KD))
                            pe.wait_ge(cat_lo, layer * KD + KD)
                        w = slot(FIRST["out", layer] + 2 * nh + kh, 4, 512)
                        for tt in range(n):
                            cols = slice(tt * P, (tt + 1) * P)
                            for k in range(4):
                                kk = 4 * kh + k
                                last = product(ps[:, 4 * nh + tt, :], [hT_hi[:, kk, cols], hT_lo[:, kk, cols]],
                                               [p[:, k, :] for p in w], kk == 0, kk == KD - 1)
                            if kh and tt < n - 1:
                                last.then_inc(tile_out, 1)
                        last.then_inc(w_used, 1)
                which = 2 * layer + 1
                for s in range(STREAMS[which]):
                    turn(which, s)
                if layer == 0:
                    pe.wait_ge(h_lo, GBASE[1] + 2)
                    gate_rows(5, 0, 2)
                    pe.wait_ge(h_lo, GBASE[1] + 4)
                    s = FIRST["ffn"]
                    for ph, (first, count) in enumerate(FFN_PHASES):
                        if ph == 0:
                            pe.wait_ge(gate_ready, 2)
                        else:
                            pe.wait_ge(down_added, 2 * NT * ph)
                        for j in range(count):
                            if j >= 2:
                                pe.wait_ge(hid_ready, 2 * (first + j - 1))
                            for up in range(2):
                                w = slot(s + up, KD, 256)
                                for fi in range(2):
                                    for k in range(KD):
                                        last = product(ps[:, 4 * (j % 2) + 2 * up + fi, :],
                                                       [p[:, k, fi * P:(fi + 1) * P] for p in w],
                                                       [hT_hi[:, k, :], hT_lo[:, k, :]], k == 0, k == KD - 1)
                                last.then_inc(w_used, 1)
                            s += 2
                        pe.wait_ge(hid_ready, 2 * (first + count))
                        half = (FFN_PHASE_SLOTS[ph] - 2 * count) // 2
                        for nh in range(2):
                            for q in range(half):
                                n = min(4, 2 * count - 4 * q)
                                w = slot(s + q, n, 512)
                                for tt in range(NT):
                                    cols = slice(tt * P, (tt + 1) * P)
                                    for k in range(n):
                                        f = 4 * q + k
                                        last = product(ps[:, 4 * nh + tt, :], [hid_hi[:, f, cols], hid_lo[:, f, cols]],
                                                       [p[:, k, :] for p in w], f == 0, f == 2 * count - 1)
                                    if q == half - 1 and tt < NT - 1:
                                        last.then_inc(tile_out, 1)
                                last.then_inc(w_used, 1)
                            s += half

            gate_rows(5, 1, 1, bank=6)
            pe.wait_ge(h_whole, GBASE[3] + 2)
            pe.wait_ge(moe_consts, 16 * 4)
            for tt in range(LT):
                for k in range(KD):
                    last = mm(ps[:, 4, tt * N_EXP:(tt + 1) * N_EXP], h2T[:, k, tt * P:(tt + 1) * P], rw[:, k, :],
                              start=(k == 0), stop=(k == KD - 1))
            last.then_inc(logits_done, 1)
            pe.wait_ge(sel_ready, 1)
            mm(ps[:, 5, 0:N_EXP], triu[:], rt[:, 3, 0, :], start=True, stop=True)
            mm(ps[:, 5, N_EXP:16], triu[:], rt[:, 3, 1, :], start=True, stop=False)
            mm(ps[:, 5, N_EXP:16], ones[:], rt[:, 3, 0, :], start=False, stop=True)
            mm(ps[:, 5, 16:24], ones[:], rt[:, 3, 0, :], start=True, stop=False)
            mm(ps[:, 5, 16:24], ones[:], rt[:, 3, 1, :], start=False, stop=True).then_inc(rank_done, 1)
            pe.wait_ge(gate_ready, 4)

            pe.wait_ge(steps_ready, 1)
            steps = pe.value_load(steps_i[0:1, 0:1], min_val=N_EXP, max_val=2 * N_EXP)

            def gather():
                for k in range(KD):
                    for tt in range(LT):
                        last = mm(ps[:, k // 4, (k % 4) * P:(k % 4 + 1) * P], xn2[:, tt, k * P:(k + 1) * P],
                                  pick[:, tt, :], start=(tt == 0), stop=(tt == LT - 1))
                last.then_inc(gath_done, 1)

            def scatter(n):
                pe.wait_ge(pickT_ready, n)
                pe.wait_ge(e_out, n)
                for tt in range(LT):
                    for nh in range(2):
                        last = mm(ps[:, 4 + 2 * tt + nh, :], gpickT[:, tt * P:(tt + 1) * P],
                                  oute[:, nh * 512:(nh + 1) * 512], start=True, stop=True)
                last.then_inc(e_scat, 1)

            pe.wait_ge(pick_ready, 1)
            gather()
            with pe.Fori(0, steps) as it:
                def eslot(j, n, width):
                    pe.wait_ge(lo_ready, it * MOE_SLOTS + (MOE_BASE + j + 1))
                    hi, lo = parts(MOE_BASE + j)
                    return [t[:, 0:n * width].rearrange("p (c w) -> p c w", c=n) for t in (hi, lo)]

                def turn_h(g):
                    n = min(4, FC - 4 * g)
                    pe.wait_ge(e_h, it * MOE_GROUPS + (g + 1))
                    if g == 0:
                        pe.wait_ge(e_y, it + 1)
                    if g >= 2:
                        pe.wait_ge(e_hid, it * MOE_GROUPS + (g - 1))
                    for f in range(n):
                        last = nc.tensor.transpose(ps[:, (4, 7)[g % 2], f * P:(f + 1) * P],
                                                   eh[:, g % 2, f * P:(f + 1) * P], ident[:])
                    last.then_inc(e_T, 1)

                pe.wait_ge(gath_lo, it + 1)
                for g in range(MOE_GROUPS):
                    width = min(512, D_FF - 512 * g)
                    kn = 4 if width == 512 else KD
                    if g >= 2:
                        pe.wait_ge(e_h, it * MOE_GROUPS + (g - 1))
                    for up in range(2):
                        for kh in range(KD // kn):
                            w = eslot(4 * g + (KD // kn) * up + kh, kn, width)
                            for k in range(kn):
                                kk = kn * kh + k
                                last = product(ps[:, 2 * up + g % 2, 0:width], [g_hi[:, kk, :], g_lo[:, kk, :]],
                                               [p[:, k, :] for p in w], kk == 0, kk == KD - 1)
                            last.then_inc(w_used, 1)
                        if not up:
                            if g:
                                turn_h(g - 1)
                            else:
                                scatter(it + 1)
                for g in range(MOE_GROUPS):
                    n = min(4, FC - 4 * g)
                    pe.wait_ge(e_hid, it * MOE_GROUPS + (g + 1))
                    for nh in range(2):
                        if g < MOE_GROUPS - 1:
                            w = eslot(GU_SLOTS + 2 * g + nh, n, 512)
                        elif nh == 0:
                            w = eslot(GU_SLOTS + 2 * g, n, D)
                        cols = slice(nh * 512, (nh + 1) * 512) if g == MOE_GROUPS - 1 else slice(0, 512)
                        for k in range(n):
                            f = 4 * g + k
                            last = product(ps[:, 5 + nh, :], [e_hi[:, f, :], e_lo[:, f, :]],
                                           [p[:, k, cols] for p in w], f == 0, f == FC - 1)
                        if g < MOE_GROUPS - 1 or nh == 1:
                            last.then_inc(w_used, 1)
                    if g == 0:
                        turn_h(MOE_GROUPS - 1)
                    if g == 1:
                        pe.wait_ge(pick_ready, it + 2)
                        for tt in range(LT):
                            nc.tensor.transpose(ps[:, 3, tt * P:(tt + 1) * P], gpick[:, tt, :], ident[:])
                        gather()
            scatter(pe.snap(steps + 1, min_val=N_EXP + 1, max_val=2 * N_EXP + 1))


_INS = ["x", "c", "ctx", "c_ctx", "ada_w", "ada_b", "norm1_g", "norm2_g", "w_in", "ret_decay_fwd", "ret_decay_bwd",
        "ret_gn_g", "diff_qn_g", "diff_kn_g", "lam_q1", "lam_k1", "lam_q2", "lam_k2", "diff_subln_g", "w_out",
        "ffn_w_gate", "ffn_w_up", "ffn_w_down", "router_w", "router_b", "moe_w_gate", "moe_w_up", "moe_w_down"]
START_LOADS = 16 * 12


def constants():
    import numpy as np

    f32 = np.float32
    grid_w = 64
    n_freq = DQK // 4
    inv = f32(10000.0) ** (-np.arange(n_freq, dtype=f32) / f32(n_freq))
    pos = np.arange(SEQ)
    ang = np.concatenate([(pos // grid_w).astype(f32)[:, None] * inv, (pos % grid_w).astype(f32)[:, None] * inv], -1)
    ang = np.concatenate([ang, ang], -1).astype(f32)
    delta = (np.arange(384)[None, :] - P - np.arange(P)[:, None]).astype(f32)
    dist = np.stack([np.where(delta >= 0, delta, BIG_DIST), np.where(delta <= 0, -delta, BIG_DIST), delta]).astype(f32)
    return {
        "k_ident": np.eye(P, dtype=f32),
        "k_triu": np.triu(np.ones((P, P), f32)),
        "k_iota": np.tile(np.arange(P, dtype=f32), (P, 1)),
        "k_cos": np.cos(ang).astype(f32),
        "k_sin": np.sin(ang).astype(f32),
        "k_dist": dist,
    }


def kernel(**inputs):
    import numpy as np
    import concourse.bacc as bacc
    from concourse.bass_utils import run_bass_kernel_spmd

    nc = bacc.Bacc("TRN2", target_bir_lowering=False, num_devices=1, dynamic_dma_scratch_size=16)
    arrays, io = {}, {}
    for name, a in [(n, inputs[n]) for n in _INS] + list(constants().items()):
        a = np.ascontiguousarray(a)
        arrays[f"in_{name}"] = a
        io[name] = nc.dram_tensor(f"in_{name}", a.shape, mybir.dt.from_np(a.dtype), kind="ExternalInput").ap()
    out = nc.dram_tensor("out_latent", (1, SEQ, D), F32, kind="ExternalOutput").ap()
    build(nc, io, out)
    r = run_bass_kernel_spmd(nc, [arrays], core_ids=[0])
    return r.results[0]["out_latent"]
```

```python
from contextlib import ExitStack

import concourse.bass as bass
from concourse import mybir

F32 = mybir.dt.float32
F32R = mybir.dt.float32r
I32 = mybir.dt.int32
U32 = mybir.dt.uint32
ALU = mybir.AluOpType
ACT = mybir.ActivationFunctionType
AX = mybir.AxisListType

P = 128
D = 1024
KD = D // P
SEQ = 256
CTX = 256
TOK = SEQ + CTX
NT = TOK // P
LT = SEQ // P
HEADS = 4
HW = HEADS * P
DQK = 64
NPROJ = 7
D_FF = 2816
FC = D_FF // P
N_EXP = 8
EPS = 1e-6
LAM_INIT = [0.8 - 0.6 * 2.718281828459045 ** (-0.3 * layer) for layer in range(2)]
K_SCALE = float(P) ** -0.5
BIG_DIST = 1e28

RAW = 6
SPL = 3
SLOT = 2048

RQ, RK, RV, RG, DQ, DK, DV = range(NPROJ)
PROJ_ORDER = [RQ, RK, RV, RG, DK, DQ, DV]

ADA_CHUNKS = 6 * D // 512
ADA_EARLY = 2 * D // 512
RET_FILL = [ADA_EARLY, ADA_EARLY + HEADS + 8]
DIFF_FILL = [f + HEADS for f in RET_FILL]
EARLY_PROJ = 5
OUT_SLOTS = 4
FFN_PHASES = [(0, 6), (6, 5)]
FFN_PHASE_SLOTS = [2 * n + 2 * -(-2 * n // 4) for _, n in FFN_PHASES]
FFN_SLOTS = sum(FFN_PHASE_SLOTS)
MOE_GROUPS = -(-FC // 4)
GU_SLOTS = 4 * (MOE_GROUPS - 1) + 2
MOE_SLOTS = GU_SLOTS + 2 * (MOE_GROUPS - 1) + 1
MOE_BASE = 2 * 2 * ADA_CHUNKS + 2 * (2 * NPROJ + OUT_SLOTS) + FFN_SLOTS
RING = [(i - MOE_BASE) % RAW for i in range(MOE_BASE)]
SHORT_ROUNDS = -MOE_SLOTS % RAW
MOE_RING = list(range(RAW)) * (MOE_SLOTS // RAW + 1 - SHORT_ROUNDS) + list(range(RAW - 1)) * SHORT_ROUNDS
TURN_AFTER = GU_SLOTS + 1
GATHER_AFTER = GU_SLOTS + 3
VEC_ROWS = 6 * KD
ADAB_ROWS = 6 * KD * 2


def build(nc, io, out):
    with ExitStack() as ctx:
        base = nc.sbuf_base
        cursor = [(base + 63) // 64 * 64]

        def at(name, shape, dt, offset):
            return nc.alloc_sbuf_tensor_at(name, shape, dt, offset=offset)

        def words(shape):
            n = 1
            for s in shape[1:]:
                n *= s
            return n

        def place(name, shape, dt=F32):
            t = at(name, shape, dt, cursor[0])
            cursor[0] += (4 * words(shape) + 31) // 32 * 32
            return t

        def sem(name):
            return ctx.enter_context(nc.semaphore(name))

        raw = place("raw", [P, RAW, SLOT])
        whi = [place(f"whi{i}", [P, SLOT], F32R) for i in range(SPL)]
        wlo = [place(f"wlo{i}", [P, SLOT], F32R) for i in range(SPL)]
        x = place("x_res", [P, NT, D])
        hT_hi = place("hT_hi", [P, KD, TOK], F32R)
        hT_lo = place("hT_lo", [P, KD, TOK], F32R)
        ident = place("ident", [P, P])
        cos = place("cos", [P, LT, DQK])
        sin = place("sin", [P, LT, DQK])
        subln = place("subln", [P, 2, P])
        qn = place("qn", [P, 2, DQK])
        kn = place("kn", [P, 2, DQK])
        dec = place("dec", [P, 2, 2, HEADS])
        vcol = place("vcol", [P, VEC_ROWS])
        abcol = place("abcol", [P, ADAB_ROWS])
        modcol = [place(f"modcol{i}", [P, 6 * KD, 2]) for i in range(2)]
        modtmp = place("modtmp", [P, 4, 2])
        acol = place("acol", [P, KD, 2])
        cs32 = place("cs32", [P, KD, 2])
        cs = place("cs", [P, KD, 4], F32R)
        ss = place("ss", [P, 32])
        msq = place("msq", [P, 32])
        rstd = place("rstd", [P, 32])
        neghalf = place("neghalf", [P, 16])
        lg = place("lg", [P, 2, 8])
        lg256 = place("lg256", [P, 2, 8])
        nlg = place("nlg", [P, 2, 8])
        neglam = place("neglam", [P, 2])
        bst = place("bst", [P, NT, 6])
        bag = place("bag", [P, NT, 2])
        gve = place("gve", [P, NT])
        grs = place("grs", [P, NT])
        negmax = place("negmax", [P, 2, 2])
        psum_p = place("psum_p", [P, 2, 2])
        rcp = place("rcp", [P, 2, HEADS, 2])
        ratio = place("ratio", [P, 2])
        cosg = place("cosg", [P, LT, DQK])
        sing = place("sing", [P, LT, DQK])

        A0 = (cursor[0] + 63) // 64 * 64
        KB = 1024
        ARENA = 72 * KB + 512

        def arena(name, shape, off, dt=F32):
            assert off * KB + 4 * words(shape) <= ARENA, name
            return at(name, shape, dt, A0 + int(off * KB))

        assert A0 + ARENA <= nc.sbuf_usable_end, (A0 + ARENA, nc.sbuf_usable_end)
        vrows = arena("vrows", [VEC_ROWS, P], 0)
        abrows = arena("abrows", [ADAB_ROWS, P], 0.5)
        lamv = arena("lamv", [P, 2, 4, DQK], 1)
        lamt = arena("lamt", [P, 2, 2, DQK], 3)
        lamp = arena("lamp", [P, 2, 2], 8)
        lgt = arena("lgt", [P, 4, 8], 8.25)
        modrow_start = [arena(f"modrow_start{i}", [4, 512], 4 + 2 * i) for i in range(2)]
        xn = arena("xn", [P, NT, D], 32)
        junk = arena("junk", [P, D], 48)
        htmp = arena("htmp", [P, 2, 4, SEQ], 52)
        rv = arena("rv", [P, NT, HW], 0)
        rg = arena("rg", [P, NT, HW], 8)
        dtok = arena("dtok", [P, NT, HW], 16)
        dv = arena("dv", [P, NT, HW], 24)
        gn = arena("gn", [P, HW], 16)
        qkT = arena("qkT", [P, 2, HEADS, TOK], 32)
        modrow_ret = arena("modrow_ret", [4, 512], 24)
        decL = [arena(f"decL{i}", [P, 384], (48, 26)[i]) for i in range(2)]
        decC = [arena(f"decC{i}", [P, 384], (49.5, 27.5)[i]) for i in range(2)]
        pT = arena("pT", [P, 2, 1536], 51)
        dist = arena("dist", [P, 3, 384], 63)
        scr = arena("scr", [P, 2, 512], 68)
        gscr = arena("gscr", [P, 2, 384], 67.5)
        gnb = arena("gnb", [P, NT, P], 70.5)
        ksq = arena("ksq", [P, 12, DQK], 29)
        qsq = arena("qsq", [P, NT, HW], 51)
        dqT = arena("dqT", [P, HEADS, TOK], 32)
        dkT = arena("dkT", [P, HEADS, TOK], 40)
        prob = arena("prob", [P, 2, 2, 512], 48)
        aT = arena("aT", [P, 2, 512], 56)
        modrow_diff = arena("modrow_diff", [4, 512], 70)
        gbc = arena("gbc", [P, 2, D], 60)
        xn2 = arena("xn2", [P, NT, D], 0)
        hid_hi = arena("hid_hi", [P, 12, TOK], 0, F32R)
        hid_lo = arena("hid_lo", [P, 12, TOK], 24, F32R)
        sg = arena("sg", [P, 2, 512], 48)
        hf = arena("hf", [P, 2, 512], 52)
        y = arena("y", [P, LT, D], 8)
        g_hi = arena("g_hi", [P, KD, P], 16, F32R)
        g_lo = arena("g_lo", [P, KD, P], 20, F32R)
        h2T = arena("h2T", [P, KD, SEQ], 24)
        e_hi = arena("e_hi", [P, FC, P], 24, F32R)
        e_lo = arena("e_lo", [P, FC, P], 35, F32R)
        eh = arena("eh", [P, 2, 512], 46)
        esg = arena("esg", [P, 2, 512], 50)
        oute = arena("oute", [P, D], 54)
        pick = arena("pick", [P, LT, P], 58)
        gpick = arena("gpick", [P, LT, P], 59)
        gpickT = arena("gpickT", [P, SEQ], 60)
        triu = arena("triu", [P, P], 61)
        iota = arena("iota", [P, P], 61.5)
        ones = arena("ones", [P, P], 62)
        rw = arena("rw", [P, KD, N_EXP], 62.5)
        rt = arena("rt", [P, 16, LT, N_EXP], 62.75)
        rank17 = arena("rank17", [P, LT, 17], 68.3125)
        gate16 = arena("gate16", [P, LT, 16], 63.875)
        gbc1 = arena("gbc1", [P, D], 64)
        top8 = arena("top8", [P, LT, 8], 68)
        topi = arena("topi", [P, LT, 8], 68.0625, U32)
        topf = arena("topf", [P, LT, 8], 68.125)
        steps_i = arena("steps_i", [P, 1], 68.1875, I32)
        rbias = arena("rbias", [P, N_EXP], 68.25)
        gtmp = arena("gtmp", [P, 2, 512], 68.5)

        ps = ctx.enter_context(nc.psum_tensor("ps", [P, 8, 512], F32))

        vec_loaded = sem("vec_loaded")
        start_loaded = sem("start_loaded")
        x_loaded = sem("x_loaded")
        tables_loaded = sem("tables_loaded")
        gn_loaded = sem("gn_loaded")
        gn_used = sem("gn_used")
        dist_loaded = sem("dist_loaded")
        moe_consts = sem("moe_consts")
        raw_full = [sem(f"raw_full{i}") for i in range(RAW)]
        hi_ready = sem("hi_ready")
        lo_ready = sem("lo_ready")
        w_used = sem("w_used")
        vT_done = sem("vT_done")
        vcol_ready = sem("vcol_ready")
        cs_silu = sem("cs_silu")
        cs_ready = sem("cs_ready")
        ada_row = sem("ada_row")
        ada_T = sem("ada_T")
        ada_col = sem("ada_col")
        ss_ready = sem("ss_ready")
        ms_ready = sem("ms_ready")
        rs_ready = sem("rs_ready")
        xn_ready = sem("xn_ready")
        xT_done = sem("xT_done")
        h_whole = sem("h_whole")
        h_lo = sem("h_lo")
        acol_ready = sem("acol_ready")
        proj_out = sem("proj_out")
        lsig = sem("lsig")
        lsig_v = sem("lsig_v")
        dec_exp = sem("dec_exp")
        dec_ready = sem("dec_ready")
        ret_s = sem("ret_s")
        ret_p = sem("ret_p")
        ret_o = sem("ret_o")
        ret_ve = sem("ret_ve")
        ret_rs = sem("ret_rs")
        ret_done = sem("ret_done")
        qk_sq = sem("qk_sq")
        qk_ms = sem("qk_ms")
        qk_rs = sem("qk_rs")
        qk_tok = sem("qk_tok")
        qk_T = sem("qk_T")
        qk_out = sem("qk_out")
        att_s = sem("att_s")
        att_max = sem("att_max")
        att_exp = sem("att_exp")
        att_a = sem("att_a")
        att_T = sem("att_T")
        att_aT = sem("att_aT")
        att_o = sem("att_o")
        att_sq = sem("att_sq")
        att_ms = sem("att_ms")
        att_rs = sem("att_rs")
        att_done = sem("att_done")
        cat_T = sem("cat_T")
        cat_hi = sem("cat_hi")
        cat_lo = sem("cat_lo")
        tile_out = sem("tile_out")
        gate_T = sem("gate_T")
        gate_ready = sem("gate_ready")
        out_added = sem("out_added")
        silu_done = sem("silu_done")
        hid_ready = sem("hid_ready")
        down_added = sem("down_added")
        logits_done = sem("logits_done")
        top_diff = sem("top_diff")
        top_exp = sem("top_exp")
        sel_ready = sem("sel_ready")
        rank_done = sem("rank_done")
        steps_ready = sem("steps_ready")
        pick_ready = sem("pick_ready")
        gath_done = sem("gath_done")
        gath_whole = sem("gath_whole")
        gath_lo = sem("gath_lo")
        pickT_ready = sem("pickT_ready")
        e_silu = sem("e_silu")
        e_h = sem("e_h")
        e_T = sem("e_T")
        e_hid_hi = sem("e_hid_hi")
        e_hid = sem("e_hid")
        e_out = sem("e_out")
        e_scat = sem("e_scat")
        e_y = sem("e_y")
        y_ready = sem("y_ready")
        stored = sem("stored")

        NQT = [NT, LT]
        NQ = [TOK, SEQ]
        UNITS = [NQT[0] * HEADS, NQT[1] * HEADS]
        UBASE = [0, UNITS[0]]
        NORM_TILES = [NT, NT, NT, LT]
        NBASE = [0, 4, 8, 12]
        QK_TILES = [[NT, NT], [NT, LT]]
        QK_BASE = [[0, NT], [2 * NT, 3 * NT]]
        QK_PARTS = [[0, 2], [4, 6]]
        QTB = [0, NQT[0]]
        NORM_ADDS = [2 * NT, 2 * NT + 2 * LT]
        STREAMS = [2, 2, 2, 1]
        SBASE = [0, 2, 4, 6]
        GBASE = [0, 4, 8, 12]

        def turned_at(k, s):
            return 4 * s + k // 2, k % 2 * SEQ

        def ffn_bank(ph, j):
            return 4 * ((FFN_PHASES[ph][1] - j) % 2)

        OUT_HALF = [0, 2 + 2 * len(FFN_PHASES)]

        def tiles_before(half):
            n = min(half, OUT_HALF[1])
            return (NT - 1) * n + (LT - 1) * (half - n)

        def down_chunks(count):
            n = 2 * count
            return ([(0, n % 4)] if n % 4 else []) + [(f, 4) for f in range(n % 4, n, 4)]

        def chunk_steps(layer, n_units):
            return {2 * i: DIFF_FILL[layer] + i for i in range(n_units // 2)}

        FILL = [chunk_steps(layer, UNITS[layer]) for layer in range(2)]
        assert DIFF_FILL[0] + len(FILL[0]) == RET_FILL[1] and DIFF_FILL[1] + len(FILL[1]) == 2 * ADA_CHUNKS

        def stream():
            ada_w, w_in, w_out = io["ada_w"], io["w_in"], io["w_out"]
            wg, wu, wd = io["ffn_w_gate"], io["ffn_w_up"], io["ffn_w_down"]

            def ada_chunk(c):
                layer, n = divmod(c, ADA_CHUNKS)
                for kh in range(2):
                    yield ("ada", c), ada_w[layer, kh * 512:(kh + 1) * 512, n * 512:(n + 1) * 512], 4, 512

            def proj_group(layer, c):
                g = PROJ_ORDER[c]
                for kh in range(2):
                    yield ("proj", layer, c), w_in[layer, kh * 512:(kh + 1) * 512, g * HW:(g + 1) * HW], 4, 512

            for c in range(ADA_EARLY):
                yield from ada_chunk(c)
            for layer in range(2):
                for c in range(EARLY_PROJ):
                    yield from proj_group(layer, c)
                for h in range(HEADS):
                    yield from ada_chunk(RET_FILL[layer] + h)
                for c in range(EARLY_PROJ, NPROJ):
                    yield from proj_group(layer, c)
                for c in FILL[layer].values():
                    yield from ada_chunk(c)
                for nh in range(2):
                    for kh in range(2):
                        yield ("out", layer), w_out[layer, kh * 512:(kh + 1) * 512, nh * 512:(nh + 1) * 512], 4, 512
                if layer == 0:
                    for first, count in FFN_PHASES:
                        for j in range(first, first + count):
                            for w in (wg, wu):
                                yield "ffn", w[0, :, j * 256:(j + 1) * 256], KD, 256
                        for nh in range(2):
                            for f, n in down_chunks(count):
                                rows = slice((2 * first + f) * P, (2 * first + f + n) * P)
                                yield "ffn", wd[0, rows, nh * 512:(nh + 1) * 512], n, 512

        SLOTS, FIRST = [], {}
        for step, *load_of in stream():
            FIRST.setdefault(step, len(SLOTS))
            SLOTS.append(load_of)
        assert len(SLOTS) == MOE_BASE

        def ada_banks(c):
            if c < ADA_EARLY:
                return 4 + c % 2, 6 + c % 2
            b = 3 if c - RET_FILL[c >= RET_FILL[1]] < HEADS else 5
            return b, b

        def ada_rows(c):
            if c < ADA_EARLY:
                return modrow_start[c % 2]
            return modrow_ret if c - RET_FILL[c >= RET_FILL[1]] < HEADS else modrow_diff

        def ada_before(c):
            return c - 1 if c < ADA_EARLY else c

        assert MOE_SLOTS % SPL == 0 and len(MOE_RING) == MOE_SLOTS

        def moe_slot(j, e):
            if j < GU_SLOTS:
                g, rest = divmod(j, 4)
                full = g < MOE_GROUPS - 1
                w = io["moe_w_gate"] if rest < (2 if full else 1) else io["moe_w_up"]
                if not full:
                    return w[0, e, :, g * 512:D_FF], KD, D_FF - g * 512
                kh = rest % 2
                return w[0, e, kh * 512:(kh + 1) * 512, g * 512:(g + 1) * 512], 4, 512
            g, nh = divmod(j - GU_SLOTS, 2)
            if g == MOE_GROUPS - 1:
                return io["moe_w_down"][0, e, 4 * g * P:D_FF, :], FC - 4 * g, D
            return io["moe_w_down"][0, e, 4 * g * P:(4 * g + 4) * P, nh * 512:(nh + 1) * 512], 4, 512

        def gate_end(g):
            return 4 * g + 1 if g < MOE_GROUPS - 1 else GU_SLOTS - 2

        def up_end(g):
            return 4 * g + 3 if g < MOE_GROUPS - 1 else GU_SLOTS - 1

        def landed(i):
            return 16 * RING[:i + 1].count(RING[i])

        def moe_landed(it, j):
            r = MOE_RING[j % MOE_SLOTS]
            return it * (16 * MOE_RING.count(r)) + 16 * (RING.count(r) + (MOE_RING * 2)[:j + 1].count(r))

        def split_before(order, i):
            return max(n for n in range(i) if order[n] == order[i]) + 1

        def bcast(ap, n):
            return ap.unsqueeze(0).to_broadcast([P, n])

        block = ctx.enter_context(nc.Block())

        @block.sync
        def _(sp):
            def small(dst, src, s=start_loaded):
                sp.dma_start(dst, src).then_inc(s, 16)

            def load(src, n, width, dst_slot):
                sp.dma_start(raw[:, dst_slot, 0:n * width].rearrange("p (c w) -> p c w", c=n),
                             src.rearrange("(c p) w -> p c w", p=P)).then_inc(raw_full[dst_slot], 16)

            small(ident[:], io["k_ident"], vec_loaded)
            for n, name in enumerate(("c", "c_ctx")):
                v = io[name] if name == "c_ctx" else io[name].rearrange("a d -> (a d)")
                small(vrows[n * KD:(n + 1) * KD, :], v.rearrange("(k p) -> k p", p=P), vec_loaded)
            for n, name in enumerate(("norm1_g", "norm2_g")):
                small(vrows[(2 + 2 * n) * KD:(4 + 2 * n) * KD, :],
                      io[name].rearrange("l (k p) -> (l k) p", p=P), vec_loaded)
            small(abrows[:], io["ada_b"].rearrange("l (k p) -> (l k) p", p=P), vec_loaded)
            load(*SLOTS[0], RING[0])
            for n, name in enumerate(("lam_q1", "lam_k1", "lam_q2", "lam_k2")):
                small(lamv[:, :, n, :], io[name].unsqueeze(0).to_broadcast([P, 2, DQK]))
            small(dec[:, :, 0, :], io["ret_decay_fwd"].unsqueeze(0).to_broadcast([P, 2, HEADS]))
            small(dec[:, :, 1, :], io["ret_decay_bwd"].unsqueeze(0).to_broadcast([P, 2, HEADS]))
            for i in range(1, 3):
                load(*SLOTS[i], RING[i])
            small(x[:, 0:LT, :], io["x"].rearrange("b (t p) d -> p (b t) d", p=P), x_loaded)
            small(x[:, LT:NT, :], io["ctx"].rearrange("b (t p) d -> p (b t) d", p=P), x_loaded)
            for i in range(3, RAW):
                load(*SLOTS[i], RING[i])
            for i in range(RAW, MOE_BASE):
                if i == FIRST["proj", 0, 1]:
                    small(cos[:], io["k_cos"].rearrange("(t p) d -> p t d", p=P), tables_loaded)
                    small(sin[:], io["k_sin"].rearrange("(t p) d -> p t d", p=P), tables_loaded)
                    small(subln[:], io["diff_subln_g"].unsqueeze(0).to_broadcast([P, 2, P]), tables_loaded)
                    small(qn[:], io["diff_qn_g"].unsqueeze(0).to_broadcast([P, 2, DQK]), tables_loaded)
                    small(kn[:], io["diff_kn_g"].unsqueeze(0).to_broadcast([P, 2, DQK]), tables_loaded)
                for layer in range(2):
                    if i == FIRST["proj", layer, 0] + RAW:
                        if layer:
                            sp.wait_ge(gn_used, layer)
                            sp.wait_ge(down_added, 4 * NT)
                        small(gn[:], io["ret_gn_g"][layer:layer + 1, :].to_broadcast([P, HW]), gn_loaded)
                        small(dist[:], io["k_dist"].rearrange("n p c -> p n c"), dist_loaded)
                sp.wait_ge(lo_ready, split_before(RING, i))
                load(*SLOTS[i], RING[i])
            for j in range(MOE_SLOTS):
                if j == RAW:
                    sp.wait_ge(out_added, NORM_ADDS[1])
                    small(triu[:], io["k_triu"], moe_consts)
                    small(iota[:], io["k_iota"], moe_consts)
                    small(rw[:], io["router_w"].rearrange("a (k p) e -> p (a k) e", p=P), moe_consts)
                    small(rbias[:], io["router_b"].to_broadcast([P, N_EXP]), moe_consts)
                sp.wait_ge(lo_ready, split_before(RING + MOE_RING, MOE_BASE + j))
                load(*moe_slot(j, 0), MOE_RING[j])
            sp.wait_ge(steps_ready, 1)
            steps = sp.value_load(steps_i[0:1, 0:1], min_val=N_EXP, max_val=2 * N_EXP)
            with sp.Fori(1, steps) as it:
                expert = sp.snap(sp.to_reg(it & (N_EXP - 1)), min_val=0, max_val=N_EXP - 1)
                for j in range(MOE_SLOTS):
                    before = split_before(MOE_RING * 2, MOE_SLOTS + j) - MOE_SLOTS
                    sp.wait_ge(lo_ready, it * MOE_SLOTS + (MOE_BASE + before))
                    src, n, width = moe_slot(j, expert)
                    load(src, n, width, MOE_RING[j])
            for j in range(SPL):
                before = split_before(MOE_RING * 2, MOE_SLOTS + j) - MOE_SLOTS
                sp.wait_ge(lo_ready, sp.snap(steps * MOE_SLOTS + (MOE_BASE + before),
                                             min_val=N_EXP * MOE_SLOTS + MOE_BASE - RAW,
                                             max_val=2 * N_EXP * MOE_SLOTS + MOE_BASE))
                load(*moe_slot(j, 0), MOE_RING[j])
            for tt in range(LT):
                sp.wait_ge(y_ready, tt + 1)
                sp.dma_start(out[0, tt * P:(tt + 1) * P, :], x[:, tt, :]).then_inc(stored, 16)
            sp.wait_ge(stored, 16 * LT)

        def hi_split(act, i_slot, place, landed_value, used_value, n=SLOT):
            act.wait_ge(raw_full[place], landed_value)
            if used_value is not None:
                act.wait_ge(w_used, used_value)
            nc.scalar.activation(whi[i_slot % SPL][:, 0:n], raw[:, place, 0:n], ACT.Copy).then_inc(hi_ready, 1)

        def lo_split(dve, i_slot, place, hi_value, n=SLOT):
            dve.wait_ge(hi_ready, hi_value)
            nc.vector.tensor_tensor(wlo[i_slot % SPL][:, 0:n], raw[:, place, 0:n],
                                    whi[i_slot % SPL][:, 0:n].bitcast(F32),
                                    ALU.subtract).then_inc(lo_ready, 1)

        @block.scalar
        def _(act):
            nxt = [0]

            def split_to(i):
                while nxt[0] <= min(i, MOE_BASE - 1):
                    k = nxt[0]
                    n = SLOTS[k][1] * SLOTS[k][2]
                    hi_split(act, k, RING[k], landed(k), k - SPL + 1 if k >= SPL else None, n)
                    nxt[0] += 1

            def ada_row_copy(c):
                act.wait_ge(w_used, FIRST["ada", c] + 2)
                if c >= 2:
                    act.wait_ge(ada_T, ada_before(c))
                nc.scalar.copy(ada_rows(c)[:], ps[0:4, ada_banks(c)[0], :]).then_inc(ada_row, 1)

            def squares_of(which, tt):
                n = NORM_TILES[which]
                if which == 0:
                    if tt == 0:
                        act.wait_ge(x_loaded, 16 * 2)
                elif which == 2:
                    act.wait_ge(down_added, 3 * n + tt + 1)
                else:
                    act.wait_ge(out_added, NORM_ADDS[which // 2] - n + tt + 1)
                if tt:
                    act.drain()
                r = nc.scalar.activation(junk[:], x[:, tt, :], ACT.Square, accum_out=ss[:, tt:tt + 1])
                if tt % LT == LT - 1:
                    r.then_inc(ss_ready, 1)

            def modulate(which, layer):
                shift = (0 if which % 2 == 0 else 3) * KD
                act.wait_ge(acol_ready, which + 1)
                for g in range(2 * STREAMS[which]):
                    s, half = divmod(g, 2)
                    n = GBASE[which] + g
                    act.wait_ge(xT_done, n + 1)
                    if which < 3 and n >= 2:
                        act.wait_ge(h_lo, n - 1)
                    for i in range(4):
                        k = 4 * half + i
                        b, off = turned_at(k, s)
                        last = nc.scalar.activation(
                            h2T[:, k, :] if which == 3 else htmp[:, n % 2, i, :], ps[:, b, off:off + SEQ],
                            ACT.Identity, bias=modcol[layer][:, shift + k, s:s + 1], scale=acol[:, k, s:s + 1])
                    last.then_inc(h_whole, 1)

            def cat_parts(layer, ks):
                for k in ks:
                    act.wait_ge(cat_T, layer * KD + k + 1)
                    nc.scalar.copy(hT_hi[:, k, 0:NQ[layer]], ps[:, k, 0:NQ[layer]]).then_inc(cat_hi, 1)

            def gate_rows(n, dst, streams, bank=0):
                act.wait_ge(gate_T, n + 1)
                for s in range(streams):
                    last = nc.scalar.copy(dst(s), ps[:, bank + 2 * s:bank + 2 * s + 2, :])
                last.then_inc(gate_ready, 1)

            def decays(layer, h):
                f, b = h, HEADS + h
                n = layer * HEADS + h
                act.wait_ge(dist_loaded, 16 * (layer + 1))
                if n:
                    act.wait_ge(dec_ready, n)
                if n >= 2:
                    act.wait_ge(ret_p, n - 1)
                nc.scalar.activation(decL[h % 2][:], dist[:, 0, :], ACT.Exp, scale=lg[:, layer, f:f + 1])
                nc.scalar.activation(gscr[:, 0, :], dist[:, 1, :], ACT.Exp, scale=lg[:, layer, b:b + 1])
                nc.scalar.activation(decC[h % 2][:], dist[:, 2, :], ACT.Exp, scale=lg[:, layer, f:f + 1],
                                     bias=lg256[:, layer, f:f + 1])
                nc.scalar.activation(gscr[:, 1, :], dist[:, 2, :], ACT.Exp, scale=nlg[:, layer, b:b + 1],
                                     bias=lg256[:, layer, b:b + 1]).then_inc(dec_exp, 1)

            def proj(layer, c, s):
                g = PROJ_ORDER[c]
                split_to(s + 2)
                act.wait_ge(w_used, s + 1)
                b = (c % 2) * 4
                if g in (RQ, RK):
                    w = NQ[layer] if g == RQ else TOK
                    for h in range(HEADS):
                        last = nc.scalar.copy(qkT[:, 0 if g == RQ else 1, h, 0:w], ps[:, b + h, 0:w])
                else:
                    dst = {RV: rv, RG: rg, DK: dtok, DQ: dtok, DV: dv}[g]
                    tiles = NQT[layer] if g in (RG, DQ) else NT
                    if g == DK:
                        act.wait_ge(gn_used, layer + 1)
                    if g == DQ:
                        act.wait_ge(qk_T, 2 * layer + 1)
                    for tt in range(tiles):
                        last = nc.scalar.activation(dst[:, tt, :], ps[:, b + tt, :],
                                                    ACT.Silu if g == RG else ACT.Copy)
                if g == DQ:
                    last.then_inc(proj_out, 1)
                    for tt in range(tiles):
                        last = nc.scalar.activation(qsq[:, tt, :], ps[:, b + tt, :], ACT.Square)
                        if tt % LT == LT - 1:
                            last.then_inc(qk_sq, 1)
                    return
                last.then_inc(proj_out, 1)

            def qk_turned(layer, q):
                n = 2 * layer + q
                w = QK_TILES[layer][q] * P
                b = 4 * q
                act.wait_ge(qk_T, n + 1)
                for h in range(HEADS):
                    last = nc.scalar.copy((dqT if q else dkT)[:, h, 0:w], ps[:, b + h, 0:w])
                last.then_inc(qk_out, 1)

            def exps(layer, u):
                n = UBASE[layer] + u
                keys = TOK if u // HEADS < LT else CTX
                act.wait_ge(att_max, n + 1)
                if n >= 2:
                    act.wait_ge(att_T, n - 1)
                for m in range(2):
                    last = nc.scalar.activation(prob[:, u % 2, m, 0:keys], ps[:, 2 * (u % 2) + m, 0:keys],
                                                ACT.Exp, bias=negmax[:, u % 2, m:m + 1],
                                                accum_out=psum_p[:, u % 2, m:m + 1])
                last.then_inc(att_exp, 1)

            def turned(layer, u):
                n = UBASE[layer] + u
                keys = TOK if u // HEADS < LT else CTX
                act.wait_ge(att_T, n + 1)
                if n >= 2:
                    act.wait_ge(att_o, n - 1)
                nc.scalar.copy(aT[:, u % 2, 0:keys], ps[:, 4, 0:keys]).then_inc(att_aT, 1)

            def squares(layer, qt):
                n = QTB[layer] + qt
                act.wait_ge(att_o, UBASE[layer] + HEADS * (qt + 1))
                if n:
                    act.wait_ge(att_ms, n)
                for h in range(HEADS):
                    cols = slice(h * P, (h + 1) * P)
                    last = nc.scalar.activation(scr[:, 0, cols], ps[:, 6 + qt % 2, cols], ACT.Square,
                                                scale=rcp[:, qt % 2, h, 0:1], accum_out=ss[:, h:h + 1])
                last.then_inc(att_sq, 1)

            act.wait_ge(vcol_ready, 1)
            nc.scalar.activation(cs32[:, :, 0], vcol[:, 0:KD], ACT.Silu)
            nc.scalar.activation(cs32[:, :, 1], vcol[:, KD:2 * KD], ACT.Silu).then_inc(cs_silu, 1)
            act.wait_ge(lsig_v, 1)
            nc.scalar.activation(lgt[:, 1:3, :], lgt[:, 1:3, :], ACT.Exp)
            nc.scalar.activation(lamp[:], lamp[:], ACT.Exp).then_inc(lsig, 1)
            act.wait_ge(lsig_v, 2)
            nc.scalar.activation(lgt[:, 1:3, :], lgt[:, 1:3, :], ACT.Ln).then_inc(lsig, 1)

            for c in range(ADA_EARLY):
                if c == 0:
                    split_to(SPL - 1)
                    for tt in range(NT):
                        squares_of(0, tt)
                split_to(min(FIRST["ada", c] + 3, 2 * ADA_EARLY))
                ada_row_copy(c)
            for layer in range(2):
                proj_s = FIRST["proj", layer, 0]
                split_to(proj_s)
                if layer:
                    for tt in range(NT):
                        squares_of(2, tt)
                modulate(2 * layer, layer)
                split_to(proj_s + 2)
                for c in range(EARLY_PROJ):
                    if c >= EARLY_PROJ - 2:
                        decays(layer, c - (EARLY_PROJ - 2))
                    proj(layer, c, proj_s + 2 * c + 1)
                for h in range(HEADS):
                    c = RET_FILL[layer] + h
                    split_to(FIRST["ada", c] + 3)
                    ada_row_copy(c)
                    if h + 2 < HEADS:
                        decays(layer, h + 2)
                    for tt in ((0, 1), (2, 3), (), ())[h]:
                        for g in range(8):
                            i = 8 * tt + g
                            if i and i % 12 == 0:
                                act.drain()
                            last = nc.scalar.activation(ksq[:, i % 12, :], dtok[:, tt, g * DQK:(g + 1) * DQK],
                                                        ACT.Square, accum_out=ss[:, i:i + 1])
                    if h < 2:
                        last.then_inc(qk_sq, 1)
                gate_rows(2 * layer, lambda s: gbc[:, s, :].rearrange("p (a c) -> p a c", a=2), 2 - layer)
                split_to(FIRST["proj", layer, EARLY_PROJ] + 2)
                qk_turned(layer, 0)
                for c in range(EARLY_PROJ, NPROJ):
                    proj(layer, c, FIRST["proj", layer, c] + 1)
                qk_turned(layer, 1)
                out_s = FIRST["out", layer]
                U = UNITS[layer]
                for u in range(U + 2):
                    if u < U:
                        c = FILL[layer][u - u % 2]
                        split_to(FIRST["ada", c] + 2 + u % 2)
                        exps(layer, u)
                    if 1 <= u <= U:
                        turned(layer, u - 1)
                    if u == U:
                        cat_parts(layer, range(0, HEADS))
                    if u >= 2 and (u - 2) % HEADS == HEADS - 1:
                        squares(layer, (u - 2) // HEADS)
                    if u in FILL[layer]:
                        ada_row_copy(c)
                split_to(out_s + 2)
                cat_parts(layer, range(HEADS, KD))
                split_to(out_s + 4)
                which = 2 * layer + 1
                for tt in range(NORM_TILES[which]):
                    squares_of(which, tt)
                modulate(which, layer)
                if layer == 0:
                    gate_rows(1, lambda s: gbc[:, s, :].rearrange("p (a c) -> p a c", a=2), 2)
                    split_to(out_s + 6)
                    s = FIRST["ffn"]
                    fchunk = 0
                    for ph, (first, count) in enumerate(FFN_PHASES):
                        for j in range(count):
                            for fi in range(2):
                                split_to(s + 1 + 2)
                                act.wait_ge(w_used, s + 2)
                                if fchunk >= 2:
                                    act.wait_ge(hid_ready, fchunk - 1)
                                nc.scalar.activation(sg[:, fi, :], ps[:, ffn_bank(ph, j) + fi, :],
                                                     ACT.Silu).then_inc(silu_done, 1)
                                fchunk += 1
                            s += 2
                        s += FFN_PHASE_SLOTS[ph] - 2 * count
                        split_to(s - 1)
            for j in range(SPL):
                hi_split(act, MOE_BASE + j, MOE_RING[j], moe_landed(0, j), MOE_BASE + j - SPL + 1)
            gate_rows(3, lambda s: gbc1[:].rearrange("p (a c) -> p a c", a=2), 1, bank=6)
            act.wait_ge(top_diff, 1)
            nc.scalar.activation(topf[:, :, 2], topf[:, :, 3], ACT.Exp).then_inc(top_exp, 1)

            act.wait_ge(steps_ready, 1)
            steps = act.value_load(steps_i[0:1, 0:1], min_val=N_EXP, max_val=2 * N_EXP)

            def gathered(n):
                for half in range(2):
                    act.wait_ge(gath_done, n + (half - 1))
                    for k in range(4 * half, 4 * half + 4):
                        last = nc.scalar.activation(
                            gtmp[:, half, (k % 4) * P:(k % 4 + 1) * P], ps[:, half, (k % 4) * P:(k % 4 + 1) * P],
                            ACT.Identity, bias=modcol[1][:, 3 * KD + k, 0:1], scale=acol[:, k, 0:1])
                    last.then_inc(gath_whole, 1)

            def down_out(w_value):
                act.wait_ge(w_used, w_value)
                nc.scalar.copy(oute[:].rearrange("p (a c) -> p a c", a=2), ps[:, 5:7, :]).then_inc(e_out, 1)

            gathered(2)
            with act.Fori(0, steps) as it:
                nxt_e = [SPL]

                def split_e(last):
                    while nxt_e[0] <= last:
                        j = nxt_e[0]
                        hi_split(act, MOE_BASE + j, MOE_RING[j % MOE_SLOTS], moe_landed(it, j),
                                 it * MOE_SLOTS + (MOE_BASE + j - SPL + 1))
                        nxt_e[0] += 1

                def hidden(g):
                    n = min(4, FC - 4 * g)
                    act.wait_ge(e_T, it * MOE_GROUPS + (g + 1))
                    nc.scalar.copy(e_hi[:, 4 * g:4 * g + n, :],
                                   ps[:, (4, 7)[g % 2], 0:n * P].rearrange("p (f s) -> p f s", s=P)).then_inc(e_hid_hi, 1)

                down_out(it * MOE_SLOTS + MOE_BASE)
                for g in range(MOE_GROUPS):
                    w = min(512, D_FF - 512 * g)
                    split_e(gate_end(g) + SPL)
                    act.wait_ge(w_used, it * MOE_SLOTS + (MOE_BASE + gate_end(g) + 1))
                    if g >= 2:
                        act.wait_ge(e_h, it * MOE_GROUPS + (g - 1))
                    nc.scalar.activation(esg[:, g % 2, 0:w], ps[:, g % 2, 0:w], ACT.Silu).then_inc(e_silu, 1)
                    if g:
                        hidden(g - 1)
                split_e(TURN_AFTER + SPL)
                hidden(MOE_GROUPS - 1)
                split_e(GATHER_AFTER + SPL)
                gathered(2 * it + 4)
                nc.scalar.copy(gpickT[:], ps[:, 3, 0:SEQ]).then_inc(pickT_ready, 1)
                split_e(MOE_SLOTS + SPL - 1)
            down_out(act.snap(steps * MOE_SLOTS + MOE_BASE, min_val=N_EXP * MOE_SLOTS + MOE_BASE,
                              max_val=2 * N_EXP * MOE_SLOTS + MOE_BASE))

        @block.gpsimd
        def _(pool):
            def inv_sqrt(dst, src, n, wait, value, done):
                pool.wait_ge(wait, value)
                nc.gpsimd.tensor_tensor(dst, src, neghalf[:, 0:n], ALU.pow).then_inc(done, 1)

            def decays(layer, h):
                pool.wait_ge(dec_exp, layer * HEADS + h + 1)
                nc.gpsimd.tensor_tensor(decL[h % 2][:], decL[h % 2][:], gscr[:, 0, :], ALU.add)
                nc.gpsimd.tensor_tensor(decC[h % 2][:], decC[h % 2][:], gscr[:, 1, :], ALU.add).then_inc(dec_ready, 1)

            def qk_roots(layer, q, pair):
                c0 = 8 * LT * pair
                inv_sqrt(rstd[:, c0:c0 + 8 * LT], msq[:, c0:c0 + 8 * LT], 8 * LT, qk_ms,
                         QK_PARTS[layer][q] + pair + 1, qk_rs)

            def norm_streams(which):
                for s in range(STREAMS[which]):
                    cols = slice(LT * s, LT * (s + 1))
                    inv_sqrt(rstd[:, cols], msq[:, cols], LT, ms_ready, SBASE[which] + s + 1, rs_ready)

            nc.gpsimd.memset(neghalf[:], -0.5).then_inc(rs_ready, 1)
            pool.wait_ge(rs_ready, 1)
            for layer in range(2):
                norm_streams(2 * layer)
                decays(layer, 0)
                decays(layer, 1)
                for h in range(HEADS):
                    if h + 2 < HEADS:
                        decays(layer, h + 2)
                    if h in (1, 2):
                        qk_roots(layer, 0, h - 1)
                    n = NQT[layer]
                    inv_sqrt(grs[:, 0:n], gve[:, 0:n], n, ret_ve, layer * HEADS + h + 1, ret_rs)
                for pair in range(QK_TILES[layer][1] // LT):
                    qk_roots(layer, 1, pair)
                for qt in range(NQT[layer]):
                    inv_sqrt(rstd[:, 0:HEADS], msq[:, 0:HEADS], HEADS, att_ms, QTB[layer] + qt + 1, att_rs)
                norm_streams(2 * layer + 1)

        @block.vector
        def _(dve):
            nxt = [0]
            v = nc.vector

            def split_to(i):
                while nxt[0] <= min(i, MOE_BASE - 1):
                    k = nxt[0]
                    lo_split(dve, k, RING[k], k + 1, SLOTS[k][1] * SLOTS[k][2])
                    nxt[0] += 1

            def ada_columns(c):
                layer, n = divmod(c, ADA_CHUNKS)
                dve.wait_ge(ada_T, c + 1)
                t = ps[:, ada_banks(c)[1], 0:16].rearrange("p (j r) -> p j r", r=4)
                b = abcol[:, layer * 6 * KD + 4 * n:layer * 6 * KD + 4 * n + 4]
                v.tensor_tensor(modtmp[:], t[:, :, 0:2], b.unsqueeze(2).to_broadcast([P, 4, 2]), ALU.add)
                dve.drain()
                v.tensor_tensor(modcol[layer][:, 4 * n:4 * n + 4, :], t[:, :, 2:4], modtmp[:],
                                ALU.add).then_inc(ada_col, 1)
                dve.drain()

            def norm_mean(which, s):
                cols = slice(LT * s, LT * (s + 1))
                dve.wait_ge(ss_ready, SBASE[which] + s + 1)
                v.tensor_scalar(msq[:, cols], ss[:, cols], 1.0 / D, EPS, ALU.mult, ALU.add).then_inc(ms_ready, 1)

            def norm_columns(which, layer):
                scale = (1 if which % 2 == 0 else 4) * KD
                gains = vcol[:, (2 + which % 2 * 2 + layer) * KD:(3 + which % 2 * 2 + layer) * KD]
                for s in range(2):
                    last = v.scalar_tensor_tensor(acol[:, :, s], modcol[layer][:, scale:scale + KD, s], 1.0,
                                                  gains, ALU.add, ALU.mult)
                last.then_inc(acol_ready, 1)

            def norm_tokens(which, s):
                buf = xn if which % 2 == 0 else xn2
                dve.wait_ge(rs_ready, SBASE[which] + s + 2)
                for tt in range(LT * s, LT * (s + 1)):
                    v.tensor_scalar(buf[:, tt, :], x[:, tt, :], rstd[:, tt:tt + 1], None,
                                    ALU.mult).then_inc(xn_ready, 1)

            def norm_parts(which):
                for g in range(2 * STREAMS[which]):
                    s, half = divmod(g, 2)
                    n = GBASE[which] + g
                    hi = hT_hi[:, 4 * half:4 * half + 4, s * SEQ:(s + 1) * SEQ]
                    dve.wait_ge(h_whole, n + 1)
                    v.tensor_copy(hi, htmp[:, n % 2, :, :])
                    dve.drain()
                    v.tensor_tensor(hT_lo[:, 4 * half:4 * half + 4, s * SEQ:(s + 1) * SEQ], htmp[:, n % 2, :, :],
                                    hi.bitcast(F32), ALU.subtract).then_inc(h_lo, 1)

            def cat_parts(layer, ks):
                for k in ks:
                    dve.wait_ge(cat_hi, layer * KD + k + 1)
                    v.tensor_tensor(hT_lo[:, k, 0:NQ[layer]], ps[:, k, 0:NQ[layer]],
                                    hT_hi[:, k, 0:NQ[layer]].bitcast(F32), ALU.subtract).then_inc(cat_lo, 1)

            def add_half(half, tiles, nh, end, gates, done, norm=None):
                split_to(end + (2 if norm is None else 1))
                for tt in range(tiles):
                    if tt < tiles - 1:
                        dve.wait_ge(tile_out, tiles_before(half) + tt + 1)
                    else:
                        dve.wait_ge(w_used, end + 1)
                    if norm is not None and tt == tiles - 1 and tiles == NT:
                        norm_columns(norm, norm // 2)
                        norm_tokens(norm, 0)
                    add_gated(4 * nh + tt, tt, nh, gates[:, 0 if tt < LT else 1, nh * 512:(nh + 1) * 512], done, tt)
                    if norm is not None and tt % LT == LT - 1:
                        norm_mean(norm, tt // LT)
                if norm is not None:
                    if tiles == LT:
                        norm_columns(norm, norm // 2)
                    norm_tokens(norm, STREAMS[norm] - 1)
                    if norm < 3:
                        norm_parts(norm)
                split_to(end + 3)

            def weigh(layer, h):
                n = layer * HEADS + h
                dve.wait_ge(dec_ready, n + 1)
                dve.wait_ge(ret_s, n + 1)
                b = 4 * ((h + 1) % 2)
                buf = pT[:, h % 2, :]
                for kt in range(NT):
                    i = kt % LT
                    near = decL[h % 2][:, P * (1 - i):P * (1 - i) + SEQ]
                    far = decC[h % 2][:, P * (1 - i):P * (1 - i) + SEQ]
                    bank, off, dst = (b, kt * SEQ, kt * SEQ) if kt < LT else (b + kt - 1, 0, 512 * (kt - 1))
                    last = v.scalar_tensor_tensor(buf[:, dst:dst + SEQ], ps[:, bank, off:off + SEQ], K_SCALE,
                                                  near if kt < LT else far, ALU.mult, ALU.mult)
                    if kt >= LT and layer == 0:
                        last = v.scalar_tensor_tensor(buf[:, dst + SEQ:dst + TOK], ps[:, bank, SEQ:TOK],
                                                      K_SCALE, near, ALU.mult, ALU.mult)
                last.then_inc(ret_p, 1)

            def group_norm(layer, h):
                n = layer * HEADS + h
                b = 7
                dve.wait_ge(ret_o, n + 1)
                for qt in range(NQT[layer]):
                    v.bn_stats(bst[:, qt, :], ps[:, b, qt * P:(qt + 1) * P])
                dve.drain()
                for qt in range(NQT[layer]):
                    v.bn_aggr(bag[:, qt, :], bst[:, qt, :])
                dve.drain()
                v.tensor_scalar(gve[:, 0:NQT[layer]], bag[:, 0:NQT[layer], 1], EPS, None,
                                ALU.add).then_inc(ret_ve, 1)
                cols = slice(h * P, (h + 1) * P)
                for qt in range(NQT[layer]):
                    v.scalar_tensor_tensor(gnb[:, qt, :], ps[:, b, qt * P:(qt + 1) * P], bag[:, qt, 0:1],
                                           rg[:, qt, cols], ALU.subtract, ALU.mult)
                dve.drain()
                dve.wait_ge(ret_rs, n + 1)
                for qt in range(NQT[layer]):
                    last = v.tensor_scalar(rg[:, qt, cols], gnb[:, qt, :], grs[:, qt:qt + 1], None, ALU.mult)
                last.then_inc(ret_done, 1)

            def qk_tables(layer, q):
                gain = (qn if q else kn)[:, layer, :]
                half = DQK // 2
                for tt in range(LT):
                    v.tensor_tensor(cosg[:, tt, :], cos[:, tt, :], gain, ALU.mult)
                    v.scalar_tensor_tensor(sing[:, tt, 0:half], sin[:, tt, 0:half], -1.0, gain[:, half:DQK],
                                           ALU.mult, ALU.mult)
                    v.tensor_tensor(sing[:, tt, half:DQK], sin[:, tt, half:DQK], gain[:, 0:half], ALU.mult)

            def qk_mean(layer, q):
                for i, t0 in enumerate(range(0, QK_TILES[layer][q], LT)):
                    dve.wait_ge(qk_sq, QK_PARTS[layer][q] + i + 1)
                    cols = slice(8 * t0, 8 * (t0 + LT))
                    if q:
                        v.tensor_reduce(ss[:, cols], qsq[:, t0:t0 + LT, :].rearrange("p t (g e) -> p (t g) e", e=DQK),
                                        AX.X, ALU.add)
                        dve.drain()
                    v.tensor_scalar(msq[:, cols], ss[:, cols], 1.0 / DQK, EPS, ALU.mult, ALU.add).then_inc(qk_ms, 1)

            def qk_norm(layer, q):
                tiles = QK_TILES[layer][q]
                c = PROJ_ORDER.index(DQ if q else DK)
                gain = (qn if q else kn)[:, layer, :]
                half = DQK // 2
                dve.wait_ge(proj_out, layer * NPROJ + c + 1)
                for tt in range(tiles):
                    if tt % LT == 0:
                        dve.wait_ge(qk_rs, QK_PARTS[layer][q] + tt // LT + 1)
                    if q and tt % LT == 0:
                        cols = slice(8 * tt, 8 * (tt + LT))
                        v.tensor_scalar(rstd[:, cols], rstd[:, cols], float(DQK) ** -0.5, None, ALU.mult)
                        dve.drain()
                    a = dtok[:, tt, :].rearrange("p (g e) -> p g e", e=DQK)
                    r = rstd[:, 8 * tt:8 * tt + 8].unsqueeze(2).to_broadcast([P, 8, DQK])
                    v.tensor_tensor(a, a, r, ALU.mult)
                    dve.drain()
                    if tt < LT:
                        t1 = scr[:, 0, :].rearrange("p (g e) -> p g e", e=DQK)
                        t2 = scr[:, 1, :].rearrange("p (g e) -> p g e", e=DQK)
                        cg = cosg[:, tt, :].unsqueeze(1).to_broadcast([P, 8, DQK])
                        sa = sing[:, tt, 0:half].unsqueeze(1).to_broadcast([P, 8, half])
                        sb = sing[:, tt, half:DQK].unsqueeze(1).to_broadcast([P, 8, half])
                        v.tensor_tensor(t1, a, cg, ALU.mult)
                        v.tensor_tensor(t2[:, :, 0:half], a[:, :, half:DQK], sa, ALU.mult)
                        v.tensor_tensor(t2[:, :, half:DQK], a[:, :, 0:half], sb, ALU.mult)
                        dve.drain()
                        v.tensor_tensor(a, t1, t2, ALU.add).then_inc(qk_tok, 1)
                        dve.drain()
                    else:
                        v.tensor_tensor(a, a, gain.unsqueeze(1).to_broadcast([P, 8, DQK]),
                                        ALU.mult).then_inc(qk_tok, 1)

            def row_max(layer, u):
                n = UBASE[layer] + u
                keys = TOK if u // HEADS < LT else CTX
                dve.wait_ge(att_s, n + 1)
                v.tensor_reduce(negmax[:, u % 2, :], ps[:, 2 * (u % 2):2 * (u % 2) + 2, 0:keys], AX.X, ALU.max,
                                negate=True).then_inc(att_max, 1)

            def combine(layer, u):
                n = UBASE[layer] + u
                keys = TOK if u // HEADS < LT else CTX
                dve.wait_ge(att_exp, n + 1)
                qt, h = divmod(u, HEADS)
                v.reciprocal(rcp[:, qt % 2, h, :], psum_p[:, u % 2, :])
                dve.drain()
                v.scalar_tensor_tensor(ratio[:, u % 2:u % 2 + 1], psum_p[:, u % 2, 0:1], neglam[:, layer:layer + 1],
                                       rcp[:, qt % 2, h, 1:2], ALU.mult, ALU.mult)
                dve.drain()
                v.scalar_tensor_tensor(prob[:, u % 2, 0, 0:keys], prob[:, u % 2, 1, 0:keys],
                                       ratio[:, u % 2:u % 2 + 1], prob[:, u % 2, 0, 0:keys],
                                       ALU.mult, ALU.add).then_inc(att_a, 1)

            def sub_mean(layer, qt):
                n = QTB[layer] + qt
                dve.wait_ge(att_sq, n + 1)
                v.tensor_scalar(msq[:, 0:HEADS], ss[:, 0:HEADS], 1.0 / P, EPS, ALU.mult,
                                ALU.add).then_inc(att_ms, 1)

            def sub_norm(layer, qt):
                n = QTB[layer] + qt
                dve.wait_ge(att_rs, n + 1)
                v.tensor_tensor(rstd[:, 0:HEADS], rstd[:, 0:HEADS], rcp[:, qt % 2, :, 0], ALU.mult)
                dve.drain()
                for h in range(HEADS):
                    cols = slice(h * P, (h + 1) * P)
                    last = v.scalar_tensor_tensor(dtok[:, qt, cols], ps[:, 6 + qt % 2, cols], rstd[:, h:h + 1],
                                                  subln[:, layer, :], ALU.mult, ALU.mult)
                last.then_inc(att_done, 1)

            def add_gated(bank, tt, nh, gate, done, k):
                cols = slice(nh * 512, (nh + 1) * 512)
                v.tensor_tensor(scr[:, k % 2, :], ps[:, bank, :], gate, ALU.mult)
                dve.drain()
                v.tensor_tensor(x[:, tt, cols], x[:, tt, cols], scr[:, k % 2, :], ALU.add).then_inc(done, 1)

            dve.wait_ge(vT_done, 1)
            v.tensor_copy(vcol[:], ps[:, 0, 0:VEC_ROWS])
            v.tensor_copy(abcol[:], ps[:, 1, 0:ADAB_ROWS]).then_inc(vcol_ready, 1)
            dve.wait_ge(start_loaded, 16 * 6)
            d8 = dec[:].rearrange("p l d h -> p l (d h)")
            v.tensor_scalar(lgt[:, 1:3, :], d8, -1.0, None, ALU.mult)
            v.tensor_scalar(lg[:], d8, 0.0, None, ALU.min)
            v.tensor_tensor(lamt[:, :, 0, :], lamv[:, :, 0, :], lamv[:, :, 1, :], ALU.mult)
            v.tensor_tensor(lamt[:, :, 1, :], lamv[:, :, 2, :], lamv[:, :, 3, :], ALU.mult)
            dve.drain()
            v.tensor_tensor(lgt[:, 1:3, :], lgt[:, 1:3, :], d8, ALU.min)
            v.tensor_reduce(lamp[:], lamt[:], AX.X, ALU.add).then_inc(lsig_v, 1)
            dve.wait_ge(cs_silu, 1)
            v.tensor_copy(cs[:, :, 0:2], cs32[:])
            dve.drain()
            v.tensor_tensor(cs[:, :, 2:4], cs32[:], cs[:, :, 0:2].bitcast(F32), ALU.subtract).then_inc(cs_ready, 1)
            dve.wait_ge(lsig, 1)
            v.tensor_scalar(lgt[:, 1:3, :], lgt[:, 1:3, :], 1.0, None, ALU.add).then_inc(lsig_v, 1)
            v.tensor_tensor(neglam[:], lamp[:, :, 1], lamp[:, :, 0], ALU.subtract)
            dve.drain()
            for layer in range(2):
                v.tensor_scalar(neglam[:, layer:layer + 1], neglam[:, layer:layer + 1], -LAM_INIT[layer], None,
                                ALU.add)
            dve.wait_ge(lsig, 2)
            v.tensor_tensor(lg[:], lg[:], lgt[:, 1:3, :], ALU.subtract)
            dve.drain()
            v.tensor_scalar(lg[:], lg[:], -1e-20, None, ALU.min)
            dve.drain()
            v.tensor_scalar(lg256[:], lg[:], float(CTX), None, ALU.mult)
            v.tensor_scalar(nlg[:], lg[:], -1.0, None, ALU.mult)
            dve.drain()

            for c in range(ADA_EARLY):
                split_to(FIRST["ada", c] + 2)
                if c:
                    ada_columns(c - 1)
                if c < ADA_EARLY - 1:
                    split_to(FIRST["ada", c] + 3)
                if c in (0, 2):
                    for s in range(2):
                        (norm_mean, norm_tokens)[c // 2](0, s)
            ada_columns(ADA_EARLY - 1)
            norm_columns(0, 0)
            norm_parts(0)
            dve.wait_ge(tables_loaded, 16 * 5)
            for layer in range(2):
                v.tensor_scalar(subln[:, layer, :], subln[:, layer, :], 1.0 - LAM_INIT[layer], None, ALU.mult)
            for layer in range(2):
                proj_s = FIRST["proj", layer, 0]
                split_to(proj_s + 2)
                split_to(proj_s + 2 * 3 + 1 + 3)
                dve.wait_ge(gn_loaded, 16 * (layer + 1))
                dve.wait_ge(proj_out, layer * NPROJ + PROJ_ORDER.index(RG) + 1)
                t = NQT[layer]
                v.tensor_tensor(rg[:, 0:t, :], rg[:, 0:t, :], gn[:].unsqueeze(1).to_broadcast([P, t, HW]),
                                ALU.mult).then_inc(gn_used, 1)
                split_to(FIRST["ada", RET_FILL[layer]] + 1)
                for h in range(HEADS):
                    weigh(layer, h)
                    if h == 2:
                        qk_mean(layer, 0)
                    c = RET_FILL[layer] + h
                    if h < HEADS - 1:
                        split_to(FIRST["ada", c] + 3)
                        ada_columns(c)
                        if h:
                            group_norm(layer, h - 1)
                    else:
                        group_norm(layer, h - 1)
                        ada_columns(c)
                        split_to(FIRST["ada", c] + 3)
                qk_tables(layer, 0)
                group_norm(layer, HEADS - 1)
                qk_norm(layer, 0)
                split_to(FIRST["proj", layer, EARLY_PROJ] + 3)
                qk_tables(layer, 1)
                qk_mean(layer, 1)
                qk_norm(layer, 1)
                out_s = FIRST["out", layer]
                split_to(FIRST["ada", DIFF_FILL[layer]] + 1)
                U = UNITS[layer]
                for u in range(U + 4):
                    if 1 <= u <= U:
                        combine(layer, u - 1)
                    if u == U:
                        split_to(out_s + 1)
                    if u < U:
                        row_max(layer, u)
                    if u >= 3 and (u - 3) % HEADS == HEADS - 1:
                        sub_mean(layer, (u - 3) // HEADS)
                    if u >= 4 and (u - 4) % HEADS == HEADS - 1:
                        sub_norm(layer, (u - 4) // HEADS)
                    if u < U:
                        c = FILL[layer][u - u % 2]
                        if u % 2:
                            ada_columns(c)
                        if u < U - 1:
                            split_to(FIRST["ada", c] + 2 + u % 2)
                    if u == U + 1:
                        cat_parts(layer, range(0, HEADS))
                split_to(out_s + 2)
                cat_parts(layer, range(HEADS, KD))
                dve.wait_ge(gate_ready, 2 * layer + 1)
                for nh in range(2):
                    add_half(OUT_HALF[layer] + nh, NQT[layer], nh, out_s + 2 * nh + 1, gbc, out_added,
                             2 * layer + 1 if nh else None)
                if layer == 0:
                    s = FIRST["ffn"]
                    fchunk = 0
                    for ph, (first, count) in enumerate(FFN_PHASES):
                        for j in range(count):
                            for fi in range(2):
                                split_to(s + 1 + 2)
                                dve.wait_ge(silu_done, fchunk + 1)
                                v.tensor_tensor(hf[:, fi, :], ps[:, ffn_bank(ph, j) + 2 + fi, :], sg[:, fi, :], ALU.mult)
                                dve.drain()
                                v.tensor_copy(hid_hi[:, 2 * j + fi, :], hf[:, fi, :])
                                dve.drain()
                                v.tensor_tensor(hid_lo[:, 2 * j + fi, :], hf[:, fi, :],
                                                hid_hi[:, 2 * j + fi, :].bitcast(F32),
                                                ALU.subtract).then_inc(hid_ready, 1)
                                fchunk += 1
                            s += 2
                        if ph == 0:
                            dve.wait_ge(gate_ready, 2)
                        half = (FFN_PHASE_SLOTS[ph] - 2 * count) // 2
                        for nh in range(2):
                            s += half
                            add_half(2 + 2 * ph + nh, NT, nh, s - 1, gbc, down_added,
                                     2 if ph == len(FFN_PHASES) - 1 and nh else None)

            dve.wait_ge(moe_consts, 16 * 4)
            v.memset(ones[:], 1.0)
            v.memset(y[:], 0.0)
            v.memset(gpickT[:], 0.0).then_inc(pickT_ready, 1)
            lo_split(dve, MOE_BASE, MOE_RING[0], MOE_BASE + 1)
            dve.wait_ge(logits_done, 1)
            lgts = rt[:, 0, :, :]
            v.tensor_tensor(lgts, ps[:, 4, 0:16].rearrange("p (t e) -> p t e", e=N_EXP),
                            rbias[:].unsqueeze(1).to_broadcast([P, LT, N_EXP]), ALU.add)
            dve.drain()
            for tt in range(LT):
                v.max(top8[:, tt, :], rt[:, 0, tt, :])
            dve.drain()
            for tt in range(LT):
                v.max_index(topi[:, tt, :], top8[:, tt, :], rt[:, 0, tt, :])
            dve.drain()
            v.tensor_copy(topf[:, :, 0:2], topi[:, :, 0:2])
            v.tensor_tensor(topf[:, :, 3], top8[:, :, 1], top8[:, :, 0], ALU.subtract).then_inc(top_diff, 1)
            dve.drain()
            for tt in range(LT):
                for j in range(2):
                    v.tensor_scalar(rt[:, 1 + j, tt, :], iota[:, 0:N_EXP], topf[:, tt, j:j + 1], None, ALU.is_equal)
            dve.drain()
            v.tensor_tensor(rt[:, 3, :, :], rt[:, 1, :, :], rt[:, 2, :, :], ALU.add).then_inc(sel_ready, 1)
            dve.wait_ge(top_exp, 1)
            v.tensor_scalar(topf[:, :, 4], topf[:, :, 2], 1.0, None, ALU.add)
            dve.drain()
            v.reciprocal(topf[:, :, 5], topf[:, :, 4])
            dve.drain()
            v.tensor_tensor(topf[:, :, 6], topf[:, :, 5], topf[:, :, 2], ALU.mult)
            dve.drain()
            for tt in range(LT):
                v.tensor_scalar(rt[:, 4, tt, :], rt[:, 1, tt, :], topf[:, tt, 5:6], None, ALU.mult)
            dve.drain()
            for tt in range(LT):
                for rep in range(2):
                    v.scalar_tensor_tensor(gate16[:, tt, rep * N_EXP:(rep + 1) * N_EXP], rt[:, 2, tt, :],
                                           topf[:, tt, 6:7], rt[:, 4, tt, :], ALU.mult, ALU.add)
            dve.wait_ge(rank_done, 1)
            ranks = ps[:, 5, 0:16].rearrange("p (t e) -> p t e", e=N_EXP)
            v.tensor_tensor(rt[:, 5, :, :], ranks, rt[:, 3, :, :], ALU.mult)
            v.tensor_reduce(topf[:, 0, 7:8], ps[:, 5, 16:16 + N_EXP], AX.X, ALU.max)
            dve.drain()
            for tt in range(LT):
                v.tensor_scalar(rank17[:, tt, 0:N_EXP], rt[:, 5, tt, :], -1.0, None, ALU.add)
                v.tensor_scalar(rank17[:, tt, N_EXP:16], rt[:, 5, tt, :], -1.0 - P, None, ALU.add)
            v.tensor_scalar(topf[:, 1, 7:8], topf[:, 0, 7:8], float(P), float(N_EXP), ALU.is_gt, ALU.mult)
            dve.drain()
            v.tensor_scalar(steps_i[:], topf[:, 1, 7:8], float(N_EXP), None, ALU.add)
            v.memset(rank17[:, :, 16:17], -1.0)
            dve.drain().then_inc(steps_ready, 1)
            steps = dve.value_load(steps_i[0:1, 0:1], min_val=N_EXP, max_val=2 * N_EXP)

            def pick_tokens(col):
                for tt in range(LT):
                    last = v.tensor_scalar(pick[:, tt, :], iota[:], rank17[:, tt, col], None, ALU.is_equal)
                last.then_inc(pick_ready, 1)

            def gathered(n):
                for half in range(2):
                    dve.wait_ge(gath_whole, n + (half - 1))
                    hi = g_hi[:, 4 * half:4 * half + 4, :].rearrange("p k s -> p (k s)")
                    lo = g_lo[:, 4 * half:4 * half + 4, :].rearrange("p k s -> p (k s)")
                    v.tensor_copy(hi, gtmp[:, half, :])
                    dve.drain()
                    v.tensor_tensor(lo, gtmp[:, half, :], hi.bitcast(F32), ALU.subtract).then_inc(gath_lo, 1)

            def add_rows(it):
                for tt in range(LT):
                    dve.wait_ge(e_scat, it * LT + (tt + 1))
                    rows = y[:, tt, :].rearrange("p (a c) -> p a c", a=2)
                    last = v.tensor_tensor(rows, rows, ps[:, 4 + 2 * tt:6 + 2 * tt, :], ALU.add)
                last.then_inc(e_y, 1)

            pick_tokens(slice(0, 1))
            for j in range(1, SPL):
                lo_split(dve, MOE_BASE + j, MOE_RING[j], MOE_BASE + j + 1)
            gathered(2)
            with dve.Fori(0, steps) as it:
                nxt_e = [SPL]

                def split_e(last):
                    while nxt_e[0] <= last:
                        j = nxt_e[0]
                        lo_split(dve, MOE_BASE + j, MOE_RING[j % MOE_SLOTS], it * MOE_SLOTS + (MOE_BASE + j + 1))
                        nxt_e[0] += 1

                def hidden(g):
                    n = min(4, FC - 4 * g)
                    dve.wait_ge(e_hid_hi, it * MOE_GROUPS + (g + 1))
                    v.tensor_tensor(e_lo[:, 4 * g:4 * g + n, :],
                                    ps[:, (4, 7)[g % 2], 0:n * P].rearrange("p (f s) -> p f s", s=P),
                                    e_hi[:, 4 * g:4 * g + n, :].bitcast(F32), ALU.subtract).then_inc(e_hid, 1)

                split_e(3)
                add_rows(it)
                for g in range(MOE_GROUPS):
                    w = min(512, D_FF - 512 * g)
                    split_e(gate_end(g) + SPL)
                    if g:
                        hidden(g - 1)
                    if g == 1:
                        dve.wait_ge(gath_done, 2 * it + 2)
                        for tt in range(LT):
                            v.tensor_scalar(gpick[:, tt, :], iota[:], rank17[:, tt, bass.ds(it, 1)],
                                            gate16[:, tt, bass.ds(it, 1)], ALU.is_equal, ALU.mult)
                        pick_tokens(bass.ds(it + 1, 1))
                    split_e(up_end(g) + SPL)
                    dve.wait_ge(e_silu, it * MOE_GROUPS + (g + 1))
                    dve.wait_ge(w_used, it * MOE_SLOTS + (MOE_BASE + up_end(g) + 1))
                    v.tensor_tensor(eh[:, g % 2, 0:w], ps[:, 2 + g % 2, 0:w], esg[:, g % 2, 0:w],
                                    ALU.mult).then_inc(e_h, 1)
                split_e(TURN_AFTER + SPL)
                hidden(MOE_GROUPS - 1)
                split_e(GATHER_AFTER + SPL)
                gathered(2 * it + 4)
                split_e(MOE_SLOTS + SPL - 1)
            dve.wait_ge(gate_ready, 4)
            for tt in range(LT):
                v.tensor_tensor(y[:, tt, :], y[:, tt, :], gbc1[:], ALU.mult)
            dve.drain()
            for tt in range(LT):
                v.tensor_tensor(x[:, tt, :], x[:, tt, :], y[:, tt, :], ALU.add)
            dve.drain()
            for tt in range(LT):
                dve.wait_ge(e_scat, dve.snap(steps * LT + (tt + 1), min_val=N_EXP * LT + 1,
                                             max_val=2 * N_EXP * LT + LT))
                v.tensor_tensor(y[:, tt, :].rearrange("p (a c) -> p a c", a=2), ps[:, 4 + 2 * tt:6 + 2 * tt, :],
                                gbc1[:].rearrange("p (a c) -> p a c", a=2), ALU.mult)
                dve.drain()
                v.tensor_tensor(x[:, tt, :], x[:, tt, :], y[:, tt, :], ALU.add).then_inc(y_ready, 1)

        @block.tensor
        def _(pe):
            mm = nc.tensor.matmul

            def product(dst, stat, mov, first, last):
                mm(dst, stat[0], mov[0], start=first, stop=False)
                mm(dst, stat[0], mov[1], start=False, stop=False)
                return mm(dst, stat[1], mov[0], start=False, stop=last)

            def parts(i):
                return whi[i % SPL], wlo[i % SPL]

            def slot(i, n, width):
                hi, lo = parts(i)
                pe.wait_ge(lo_ready, i + 1)
                return [t[:, 0:n * width].rearrange("p (c w) -> p c w", c=n) for t in (hi, lo)]

            def ada_product(c):
                bank = ada_banks(c)[0]
                if c >= 2:
                    pe.wait_ge(ada_col, ada_before(c))
                for kh in range(2):
                    w = slot(FIRST["ada", c] + kh, 4, 512)
                    for k in range(4):
                        for part in range(2):
                            last = mm(ps[0:4, bank, :], cs[:, 4 * kh + k, :], w[part][:, k, :],
                                      start=(kh + k + part == 0), stop=(kh == 1 and k == 3 and part == 1))
                    last.then_inc(w_used, 1)

            def ada_turn(c):
                pe.wait_ge(ada_row, c + 1)
                for j in range(4):
                    last = nc.tensor.transpose(ps[:, ada_banks(c)[1], 4 * j:4 * j + 4],
                                               ada_rows(c)[:, j * P:(j + 1) * P], ident[0:4, 0:4])
                last.then_inc(ada_T, 1)

            def turn(which, s):
                buf = xn if which % 2 == 0 else xn2
                pe.wait_ge(xn_ready, NBASE[which] + LT * (s + 1))
                for k in range(KD):
                    b, off = turned_at(k, s)
                    for t in range(LT):
                        last = nc.tensor.transpose(ps[:, b, off + t * P:off + (t + 1) * P],
                                                   buf[:, LT * s + t, k * P:(k + 1) * P], ident[:])
                    if k % 4 == 3:
                        last.then_inc(xT_done, 1)

            def cat_turn(layer, ks):
                for k in ks:
                    src, h = (rg, k) if k < HEADS else (dtok, k - HEADS)
                    for tt in range(NQT[layer]):
                        last = nc.tensor.transpose(ps[:, k, tt * P:(tt + 1) * P], src[:, tt, h * P:(h + 1) * P],
                                                   ident[:])
                    last.then_inc(cat_T, 1)

            def gate_rows(m, layer, streams, bank=0):
                for s in range(streams):
                    for k in range(KD):
                        last = mm(ps[:, bank + 2 * s + k // 4, (k % 4) * P:(k % 4 + 1) * P],
                                  modcol[layer][:, m * KD + k, s:s + 1].to_broadcast([P, P]), ident[:],
                                  start=True, stop=True)
                last.then_inc(gate_T, 1)

            def proj(layer, c, between=None):
                g = PROJ_ORDER[c]
                b = 4 * (c % 2)
                for kh in range(2):
                    if kh and between is not None:
                        between()
                    i = FIRST["proj", layer, c] + kh
                    if c == 0:
                        pe.wait_ge(h_lo, GBASE[2 * layer] + 3 + kh)
                    w = slot(i, 4, 512)
                    for t in range(HEADS if g in (RQ, RK) else (NQT[layer] if g in (RG, DQ) else NT)):
                        for k in range(4):
                            kk = 4 * kh + k
                            if g in (RQ, RK):
                                n = NQ[layer] if g == RQ else TOK
                                last = product(ps[:, b + t, 0:n], [p[:, k, t * P:(t + 1) * P] for p in w],
                                               [hT_hi[:, kk, 0:n], hT_lo[:, kk, 0:n]], kk == 0, kk == KD - 1)
                            else:
                                cols = slice(t * P, (t + 1) * P)
                                last = product(ps[:, b + t, :], [hT_hi[:, kk, cols], hT_lo[:, kk, cols]],
                                               [p[:, k, :] for p in w], kk == 0, kk == KD - 1)
                    last.then_inc(w_used, 1)

            def ret_scores(layer, h):
                b = 4 * ((h + 1) % 2)
                n = NQ[layer]
                for kt in range(NT):
                    keys = qkT[:, 1, h, kt * P:(kt + 1) * P]
                    if kt < LT:
                        last = mm(ps[:, b, kt * SEQ:(kt + 1) * SEQ], keys, qkT[:, 0, h, 0:SEQ], start=True, stop=True)
                    else:
                        last = mm(ps[:, b + kt - 1, 0:n], keys, qkT[:, 0, h, 0:n], start=True, stop=True)
                last.then_inc(ret_s, 1)

            def ret_values(layer, h):
                b = 7
                pe.wait_ge(ret_p, layer * HEADS + h + 1)
                if h:
                    pe.wait_ge(ret_done, layer * HEADS + h)
                at_kt = [0, SEQ, 512, 1024]
                for qt in range(NQT[layer]):
                    kts = range(NT) if qt < LT else range(LT, NT)
                    for kt in kts:
                        o = at_kt[kt] + qt * P
                        last = mm(ps[:, b, qt * P:(qt + 1) * P], pT[:, h % 2, o:o + P],
                                  rv[:, kt, h * P:(h + 1) * P], start=(kt == kts[0]), stop=(kt == NT - 1))
                last.then_inc(ret_o, 1)

            def qk_turn(layer, q):
                b = 4 * q
                for tt in range(QK_TILES[layer][q]):
                    pe.wait_ge(qk_tok, QK_BASE[layer][q] + tt + 1)
                    for h in range(HEADS):
                        last = nc.tensor.transpose(ps[:, b + h, tt * P:(tt + 1) * P],
                                                   dtok[:, tt, h * P:(h + 1) * P], ident[:])
                last.then_inc(qk_T, 1)

            def scores(layer, u):
                qt, h = divmod(u, HEADS)
                n = UBASE[layer] + u
                first = 0 if qt < LT else SEQ
                if u >= 2:
                    pe.wait_ge(att_exp, n - 1)
                for m in range(2):
                    rows = slice(m * DQK, (m + 1) * DQK)
                    last = mm(ps[:, 2 * (u % 2) + m, 0:TOK - first], dqT[rows, h, qt * P:(qt + 1) * P],
                              dkT[rows, h, first:TOK], start=True, stop=True)
                last.then_inc(att_s, 1)

            def turn_a(layer, u):
                n = UBASE[layer] + u
                keys = TOK if u // HEADS < LT else CTX
                pe.wait_ge(att_a, n + 1)
                if u:
                    pe.wait_ge(att_aT, n)
                for j in range(keys // P):
                    last = nc.tensor.transpose(ps[:, 4, j * P:(j + 1) * P],
                                               prob[:, u % 2, 0, j * P:(j + 1) * P], ident[:])
                last.then_inc(att_T, 1)

            def values(layer, u):
                qt, h = divmod(u, HEADS)
                n = UBASE[layer] + u
                pe.wait_ge(att_aT, n + 1)
                if h == 0 and qt >= 2:
                    pe.wait_ge(att_done, QTB[layer] + qt - 1)
                kts = range(NT) if qt < LT else range(LT, NT)
                for kt in kts:
                    j = kt - kts[0]
                    last = mm(ps[:, 6 + qt % 2, h * P:(h + 1) * P], aT[:, u % 2, j * P:(j + 1) * P],
                              dv[:, kt, h * P:(h + 1) * P], start=(j == 0), stop=(kt == NT - 1))
                last.then_inc(att_o, 1)

            pe.wait_ge(vec_loaded, 16 * 6)
            nc.tensor.transpose(ps[:, 0, 0:VEC_ROWS], vrows[:], ident[0:VEC_ROWS, 0:VEC_ROWS])
            nc.tensor.transpose(ps[:, 1, 0:ADAB_ROWS], abrows[:],
                                ident[0:ADAB_ROWS, 0:ADAB_ROWS]).then_inc(vT_done, 1)
            pe.wait_ge(vcol_ready, 1)
            pe.wait_ge(cs_ready, 1)
            for c in range(ADA_EARLY + 1):
                if c < ADA_EARLY:
                    ada_product(c)
                else:
                    turn(0, 0)
                if c:
                    ada_turn(c - 1)
            for layer in range(2):
                if layer == 0:
                    pe.wait_ge(ada_col, ADA_EARLY)
                else:
                    turn(2, 0)
                turn(2 * layer, 1)
                for c in range(EARLY_PROJ):
                    if c >= 2:
                        pe.wait_ge(proj_out, layer * NPROJ + c - 1)
                    proj(layer, c)
                pe.wait_ge(proj_out, layer * NPROJ + 4)
                for h in range(HEADS + 1):
                    if h < HEADS:
                        if h >= 2:
                            pe.wait_ge(ret_p, layer * HEADS + h - 1)
                        if h != 1:
                            ret_scores(layer, h)
                        if h == 0:
                            pe.wait_ge(proj_out, layer * NPROJ + 5)
                        ada_product(RET_FILL[layer] + h)
                    if h == 0:
                        ret_scores(layer, 1)
                    if h:
                        ret_values(layer, h - 1)
                    if h < HEADS:
                        ada_turn(RET_FILL[layer] + h)
                pe.wait_ge(ada_col, RET_FILL[layer] + HEADS)
                gate_rows(2, layer, 2 - layer)
                pe.wait_ge(ret_done, layer * HEADS + HEADS)

                def turn_keys():
                    pe.wait_ge(gate_ready, 2 * layer + 1)
                    qk_turn(layer, 0)

                proj(layer, 5, turn_keys)
                pe.wait_ge(qk_out, 2 * layer + 1)
                proj(layer, 6)
                pe.wait_ge(proj_out, layer * NPROJ + 6)
                qk_turn(layer, 1)
                pe.wait_ge(proj_out, layer * NPROJ + 7)
                pe.wait_ge(qk_out, 2 * layer + 2)
                U = UNITS[layer]
                for u in range(U + 2):
                    if u < U:
                        scores(layer, u)
                        if u in FILL[layer]:
                            ada_product(FILL[layer][u])
                        else:
                            ada_turn(FILL[layer][u - 1])
                    if 1 <= u <= U:
                        turn_a(layer, u - 1)
                    if u >= 2:
                        values(layer, u - 2)
                    if u == U:
                        cat_turn(layer, range(0, HEADS))
                pe.wait_ge(cat_lo, layer * KD + HEADS)
                n = NQT[layer]
                for nh in range(2):
                    for kh in range(2):
                        if nh == 0 and kh == 1:
                            pe.wait_ge(cat_lo, layer * KD + KD)
                        w = slot(FIRST["out", layer] + 2 * nh + kh, 4, 512)
                        for tt in range(n):
                            if nh == 0 and kh == 0 and tt == n - 1:
                                pe.wait_ge(att_done, QTB[layer] + n)
                                pe.wait_ge(ada_col, DIFF_FILL[layer] + len(FILL[layer]))
                                cat_turn(layer, range(HEADS, KD))
                            cols = slice(tt * P, (tt + 1) * P)
                            for k in range(4):
                                kk = 4 * kh + k
                                last = product(ps[:, 4 * nh + tt, :], [hT_hi[:, kk, cols], hT_lo[:, kk, cols]],
                                               [p[:, k, :] for p in w], kk == 0, kk == KD - 1)
                            if kh and tt < n - 1:
                                last.then_inc(tile_out, 1)
                        last.then_inc(w_used, 1)
                which = 2 * layer + 1
                for s in range(STREAMS[which]):
                    turn(which, s)
                if layer == 0:
                    pe.wait_ge(h_lo, GBASE[1] + 2)
                    gate_rows(5, 0, 2)
                    pe.wait_ge(h_lo, GBASE[1] + 4)
                    s = FIRST["ffn"]
                    for ph, (first, count) in enumerate(FFN_PHASES):
                        if ph == 0:
                            pe.wait_ge(gate_ready, 2)
                        else:
                            pe.wait_ge(down_added, 2 * NT * ph)
                        for j in range(count):
                            if j >= 2:
                                pe.wait_ge(hid_ready, 2 * (first + j - 1))
                            for up in range(2):
                                w = slot(s + up, KD, 256)
                                for fi in range(2):
                                    for k in range(KD):
                                        last = product(ps[:, ffn_bank(ph, j) + 2 * up + fi, :],
                                                       [p[:, k, fi * P:(fi + 1) * P] for p in w],
                                                       [hT_hi[:, k, :], hT_lo[:, k, :]], k == 0, k == KD - 1)
                                last.then_inc(w_used, 1)
                            s += 2
                        half = (FFN_PHASE_SLOTS[ph] - 2 * count) // 2
                        for nh in range(2):
                            for q, (f0, n) in enumerate(down_chunks(count)):
                                pe.wait_ge(hid_ready, 2 * (first + count) if nh else
                                           2 * first + max(f0 + n, 2 * count - 2))
                                w = slot(s + q, n, 512)
                                for tt in range(NT):
                                    cols = slice(tt * P, (tt + 1) * P)
                                    for k in range(n):
                                        f = f0 + k
                                        last = product(ps[:, 4 * nh + tt, :], [hid_hi[:, f, cols], hid_lo[:, f, cols]],
                                                       [p[:, k, :] for p in w], f == 0, f == 2 * count - 1)
                                    if q == half - 1 and tt < NT - 1:
                                        last.then_inc(tile_out, 1)
                                last.then_inc(w_used, 1)
                            s += half

            gate_rows(5, 1, 1, bank=6)
            pe.wait_ge(h_whole, GBASE[3] + 2)
            pe.wait_ge(moe_consts, 16 * 4)
            for tt in range(LT):
                for k in range(KD):
                    last = mm(ps[:, 4, tt * N_EXP:(tt + 1) * N_EXP], h2T[:, k, tt * P:(tt + 1) * P], rw[:, k, :],
                              start=(k == 0), stop=(k == KD - 1))
            last.then_inc(logits_done, 1)
            pe.wait_ge(sel_ready, 1)
            mm(ps[:, 5, 0:N_EXP], triu[:], rt[:, 3, 0, :], start=True, stop=True)
            mm(ps[:, 5, N_EXP:16], triu[:], rt[:, 3, 1, :], start=True, stop=False)
            mm(ps[:, 5, N_EXP:16], ones[:], rt[:, 3, 0, :], start=False, stop=True)
            mm(ps[:, 5, 16:24], ones[:], rt[:, 3, 0, :], start=True, stop=False)
            mm(ps[:, 5, 16:24], ones[:], rt[:, 3, 1, :], start=False, stop=True).then_inc(rank_done, 1)
            pe.wait_ge(gate_ready, 4)

            pe.wait_ge(steps_ready, 1)
            steps = pe.value_load(steps_i[0:1, 0:1], min_val=N_EXP, max_val=2 * N_EXP)

            def gather():
                for k in range(KD):
                    for tt in range(LT):
                        last = mm(ps[:, k // 4, (k % 4) * P:(k % 4 + 1) * P], xn2[:, tt, k * P:(k + 1) * P],
                                  pick[:, tt, :], start=(tt == 0), stop=(tt == LT - 1))
                    if k % 4 == 3:
                        last.then_inc(gath_done, 1)

            def scatter(n):
                pe.wait_ge(pickT_ready, n)
                pe.wait_ge(e_out, n)
                for tt in range(LT):
                    for nh in range(2):
                        last = mm(ps[:, 4 + 2 * tt + nh, :], gpickT[:, tt * P:(tt + 1) * P],
                                  oute[:, nh * 512:(nh + 1) * 512], start=True, stop=True)
                    last.then_inc(e_scat, 1)

            pe.wait_ge(pick_ready, 1)
            gather()
            with pe.Fori(0, steps) as it:
                def eslot(j, n, width):
                    pe.wait_ge(lo_ready, it * MOE_SLOTS + (MOE_BASE + j + 1))
                    hi, lo = parts(MOE_BASE + j)
                    return [t[:, 0:n * width].rearrange("p (c w) -> p c w", c=n) for t in (hi, lo)]

                def turn_h(g):
                    n = min(4, FC - 4 * g)
                    pe.wait_ge(e_h, it * MOE_GROUPS + (g + 1))
                    if g == 0:
                        pe.wait_ge(e_y, it + 1)
                    if g >= 2:
                        pe.wait_ge(e_hid, it * MOE_GROUPS + (g - 1))
                    for f in range(n):
                        last = nc.tensor.transpose(ps[:, (4, 7)[g % 2], f * P:(f + 1) * P],
                                                   eh[:, g % 2, f * P:(f + 1) * P], ident[:])
                    last.then_inc(e_T, 1)

                pe.wait_ge(gath_lo, 2 * it + 2)
                for g in range(MOE_GROUPS):
                    width = min(512, D_FF - 512 * g)
                    kn = 4 if width == 512 else KD
                    if g >= 2:
                        pe.wait_ge(e_h, it * MOE_GROUPS + (g - 1))
                    for up in range(2):
                        for kh in range(KD // kn):
                            w = eslot(4 * g + (KD // kn) * up + kh, kn, width)
                            for k in range(kn):
                                kk = kn * kh + k
                                last = product(ps[:, 2 * up + g % 2, 0:width], [g_hi[:, kk, :], g_lo[:, kk, :]],
                                               [p[:, k, :] for p in w], kk == 0, kk == KD - 1)
                            last.then_inc(w_used, 1)
                        if not up:
                            if g:
                                turn_h(g - 1)
                            else:
                                scatter(it + 1)
                for g in range(MOE_GROUPS):
                    n = min(4, FC - 4 * g)
                    pe.wait_ge(e_hid, it * MOE_GROUPS + (g + 1))
                    for nh in range(2):
                        if g < MOE_GROUPS - 1:
                            w = eslot(GU_SLOTS + 2 * g + nh, n, 512)
                        elif nh == 0:
                            w = eslot(GU_SLOTS + 2 * g, n, D)
                        cols = slice(nh * 512, (nh + 1) * 512) if g == MOE_GROUPS - 1 else slice(0, 512)
                        for k in range(n):
                            f = 4 * g + k
                            last = product(ps[:, 5 + nh, :], [e_hi[:, f, :], e_lo[:, f, :]],
                                           [p[:, k, cols] for p in w], f == 0, f == FC - 1)
                        if g < MOE_GROUPS - 1 or nh == 1:
                            last.then_inc(w_used, 1)
                    if GU_SLOTS + 2 * g + 1 == TURN_AFTER:
                        turn_h(MOE_GROUPS - 1)
                    if GU_SLOTS + 2 * g + 1 == GATHER_AFTER:
                        pe.wait_ge(pick_ready, it + 2)
                        for tt in range(LT):
                            nc.tensor.transpose(ps[:, 3, tt * P:(tt + 1) * P], gpick[:, tt, :], ident[:])
                        gather()
            scatter(pe.snap(steps + 1, min_val=N_EXP + 1, max_val=2 * N_EXP + 1))


_INS = ["x", "c", "ctx", "c_ctx", "ada_w", "ada_b", "norm1_g", "norm2_g", "w_in", "ret_decay_fwd", "ret_decay_bwd",
        "ret_gn_g", "diff_qn_g", "diff_kn_g", "lam_q1", "lam_k1", "lam_q2", "lam_k2", "diff_subln_g", "w_out",
        "ffn_w_gate", "ffn_w_up", "ffn_w_down", "router_w", "router_b", "moe_w_gate", "moe_w_up", "moe_w_down"]


def constants():
    import numpy as np

    f32 = np.float32
    grid_w = 64
    n_freq = DQK // 4
    inv = f32(10000.0) ** (-np.arange(n_freq, dtype=f32) / f32(n_freq))
    pos = np.arange(SEQ)
    ang = np.concatenate([(pos // grid_w).astype(f32)[:, None] * inv, (pos % grid_w).astype(f32)[:, None] * inv], -1)
    ang = np.concatenate([ang, ang], -1).astype(f32)
    delta = (np.arange(384)[None, :] - P - np.arange(P)[:, None]).astype(f32)
    dist = np.stack([np.where(delta >= 0, delta, BIG_DIST), np.where(delta <= 0, -delta, BIG_DIST), delta]).astype(f32)
    return {
        "k_ident": np.eye(P, dtype=f32),
        "k_triu": np.triu(np.ones((P, P), f32)),
        "k_iota": np.tile(np.arange(P, dtype=f32), (P, 1)),
        "k_cos": np.cos(ang).astype(f32),
        "k_sin": np.sin(ang).astype(f32),
        "k_dist": dist,
    }


def kernel(**inputs):
    import numpy as np
    import concourse.bacc as bacc
    from concourse.bass_utils import run_bass_kernel_spmd

    nc = bacc.Bacc("TRN2", target_bir_lowering=False, num_devices=1, dynamic_dma_scratch_size=16)
    arrays, io = {}, {}
    for name, a in [(n, inputs[n]) for n in _INS] + list(constants().items()):
        a = np.ascontiguousarray(a)
        arrays[f"in_{name}"] = a
        io[name] = nc.dram_tensor(f"in_{name}", a.shape, mybir.dt.from_np(a.dtype), kind="ExternalInput").ap()
    out = nc.dram_tensor("out_latent", (1, SEQ, D), F32, kind="ExternalOutput").ap()
    build(nc, io, out)
    r = run_bass_kernel_spmd(nc, [arrays], core_ids=[0])
    return r.results[0]["out_latent"]
```
